# Optimizing a Trainium2 kernel written in Bass

```python
import math
import jax, jax.numpy as jnp
from jax import lax
import numpy as np

D_MODEL = 1024
BATCH = 1
SEQ = 256
DEPTH = 1

D_MIX = D_MODEL
HEAD_DIM = 64
D_ATTN = D_MIX // 2
N_Q_HEADS = D_ATTN // HEAD_DIM
N_KV_HEADS = 2
Q_PER_KV = N_Q_HEADS // N_KV_HEADS
WINDOW = 128
BLOCK = WINDOW
D_SSM = D_MIX - D_ATTN
SSM_GROUP = 16
N_SSM_GROUPS = D_SSM // SSM_GROUP
STATE = 64
D_KV = N_KV_HEADS * HEAD_DIM
D_IN = D_ATTN + 2 * D_KV + D_SSM
D_FF = ((8 * D_MODEL // 3 + 127) // 128) * 128
N_MOD = 9
EPS = 1e-6


def rms_norm(x, g):
    xf = x.astype(jnp.float32)
    y = xf * lax.rsqrt(jnp.mean(xf * xf, axis=-1, keepdims=True) + EPS)
    return (y * g.astype(jnp.float32)).astype(x.dtype)

def modulate(h, shift, scale):
    return h * (1.0 + scale[:, None, :]) + shift[:, None, :]

def swiglu(h, w_gate, w_up, w_down):
    return (jax.nn.silu(h @ w_gate) * (h @ w_up)) @ w_down

def alibi_slopes():
    i = jnp.arange(1, N_Q_HEADS + 1, dtype=jnp.float32)
    return jnp.exp2(-8.0 * i / N_Q_HEADS)

def sliding_window_attention(q, k, v, sinks):
    b, s = q.shape[0], q.shape[1]
    nb = s // BLOCK
    qb = q.reshape(b, nb, BLOCK, N_KV_HEADS, Q_PER_KV, HEAD_DIM)
    kb = k.reshape(b, nb, BLOCK, N_KV_HEADS, HEAD_DIM)
    vb = v.reshape(b, nb, BLOCK, N_KV_HEADS, HEAD_DIM)
    pad = ((0, 0), (1, 0), (0, 0), (0, 0), (0, 0))
    kk = jnp.concatenate([jnp.pad(kb[:, :-1], pad), kb], axis=2)
    vv = jnp.concatenate([jnp.pad(vb[:, :-1], pad), vb], axis=2)

    scores = jnp.einsum('bnqkgd,bnjkd->bnkgqj', qb, kk).astype(jnp.float32) * (HEAD_DIM ** -0.5)

    qi = jnp.arange(BLOCK)[:, None]
    kj = jnp.arange(2 * BLOCK)[None, :]
    dist = qi + BLOCK - kj
    key_pos = jnp.arange(nb)[:, None, None] * BLOCK + kj[None] - BLOCK
    valid = (dist[None] >= 0) & (dist[None] < WINDOW) & (key_pos >= 0)

    slopes = alibi_slopes().reshape(N_KV_HEADS, Q_PER_KV)
    bias = -slopes[:, :, None, None] * dist.astype(jnp.float32)[None, None]
    scores = jnp.where(valid[None, :, None, None], scores + bias, -jnp.inf)

    sink = sinks.astype(jnp.float32).reshape(N_KV_HEADS, Q_PER_KV)[None, None, :, :, None, None]
    m = jnp.maximum(jnp.max(scores, axis=-1, keepdims=True), sink)
    p = jnp.exp(scores - m)
    p = p / (jnp.sum(p, axis=-1, keepdims=True) + jnp.exp(sink - m))
    out = jnp.einsum('bnkgqj,bnjkd->bnqkgd', p.astype(v.dtype), vv)
    return out.reshape(b, s, N_Q_HEADS * HEAD_DIM)

def s5_ssm(u, a_re, a_im, log_step, b_re, b_im, c_re, c_im, d_skip, w_glu, b_glu):
    f32 = jnp.float32
    bsz, s = u.shape[0], u.shape[1]
    uf = u.astype(f32).reshape(bsz, s, N_SSM_GROUPS, SSM_GROUP)
    lam = lax.complex(a_re.astype(f32), a_im.astype(f32))
    dt = jnp.exp(log_step.astype(f32))[:, None]
    lam_bar = jnp.exp(lam * dt)
    b_mat = lax.complex(b_re.astype(f32), b_im.astype(f32))
    b_bar = ((lam_bar - 1.0) / lam)[:, :, None] * b_mat
    bu = jnp.einsum('bsgh,gph->bsgp', uf.astype(jnp.complex64), b_bar)
    a = jnp.broadcast_to(lam_bar, bu.shape)

    def combine(left, right):
        a_l, b_l = left
        a_r, b_r = right
        return a_r * a_l, a_r * b_l + b_r

    _, states = lax.associative_scan(combine, (a, bu), axis=1)
    c_mat = lax.complex(c_re.astype(f32), c_im.astype(f32))
    y = jnp.real(jnp.einsum('bsgp,ghp->bsgh', states, c_mat))
    y = y + uf * d_skip.astype(f32).reshape(N_SSM_GROUPS, SSM_GROUP)
    y = jax.nn.gelu(y.reshape(bsz, s, D_SSM))
    y = y * jax.nn.sigmoid(y @ w_glu.astype(f32) + b_glu.astype(f32))
    return y.astype(u.dtype)

def first_inputs(seed: int = 0) -> dict:
    key = jax.random.key(seed)
    ks = jax.random.split(key, 40)
    f32 = jnp.float32
    L = DEPTH
    nrm = lambda k, shape, s: jax.random.normal(k, shape, f32) * s
    gain = lambda k: 1.0 + 0.05 * jax.random.normal(k, (L, D_MODEL), f32)
    n_idx = jnp.arange(STATE, dtype=f32)
    return {
        "x": jax.random.normal(ks[0], (BATCH, SEQ, D_MODEL), f32),
        "c": jax.random.normal(ks[1], (BATCH, D_MODEL), f32),
        "w_ada": nrm(ks[2], (L, D_MODEL, N_MOD * D_MODEL), 0.5 * D_MODEL ** -0.5),
        "b_ada": nrm(ks[3], (L, N_MOD * D_MODEL), 0.02),
        "g_pre_ff1": gain(ks[4]),
        "g_post_ff1": gain(ks[5]),
        "w1_gate": nrm(ks[6], (L, D_MODEL, D_FF), D_MODEL ** -0.5),
        "w1_up": nrm(ks[7], (L, D_MODEL, D_FF), D_MODEL ** -0.5),
        "w1_down": nrm(ks[8], (L, D_FF, D_MODEL), D_FF ** -0.5),
        "g_pre_mix": gain(ks[9]),
        "g_post_mix": gain(ks[10]),
        "w_in": nrm(ks[11], (L, D_MODEL, D_IN), D_MODEL ** -0.5),
        "attn_sinks": nrm(ks[12], (L, N_Q_HEADS), 1.0),
        "ssm_a_re": -0.5 + 0.01 * jax.random.normal(ks[13], (L, N_SSM_GROUPS, STATE), f32),
        "ssm_a_im": math.pi * n_idx + 0.01 * jax.random.normal(ks[14], (L, N_SSM_GROUPS, STATE), f32),
        "ssm_log_step": jax.random.uniform(ks[15], (L, N_SSM_GROUPS), f32, math.log(1e-3), math.log(1e-1)),
        "ssm_b_re": nrm(ks[16], (L, N_SSM_GROUPS, STATE, SSM_GROUP), (2 * SSM_GROUP) ** -0.5),
        "ssm_b_im": nrm(ks[17], (L, N_SSM_GROUPS, STATE, SSM_GROUP), (2 * SSM_GROUP) ** -0.5),
        "ssm_c_re": nrm(ks[18], (L, N_SSM_GROUPS, SSM_GROUP, STATE), (2 * STATE) ** -0.5),
        "ssm_c_im": nrm(ks[19], (L, N_SSM_GROUPS, SSM_GROUP, STATE), (2 * STATE) ** -0.5),
        "ssm_d": nrm(ks[20], (L, D_SSM), 1.0),
        "ssm_w_glu": nrm(ks[21], (L, D_SSM, D_SSM), D_SSM ** -0.5),
        "ssm_b_glu": nrm(ks[22], (L, D_SSM), 0.02),
        "g_attn_out": 1.0 + 0.05 * jax.random.normal(ks[23], (L, D_ATTN), f32),
        "g_ssm_out": 1.0 + 0.05 * jax.random.normal(ks[24], (L, D_SSM), f32),
        "w_out": nrm(ks[25], (L, D_MIX, D_MODEL), D_MIX ** -0.5),
        "g_pre_ff2": gain(ks[26]),
        "g_post_ff2": gain(ks[27]),
        "w2_gate": nrm(ks[28], (L, D_MODEL, D_FF), D_MODEL ** -0.5),
        "w2_up": nrm(ks[29], (L, D_MODEL, D_FF), D_MODEL ** -0.5),
        "w2_down": nrm(ks[30], (L, D_FF, D_MODEL), D_FF ** -0.5),
    }

def first_block(x, c, w_ada, b_ada, g_pre_ff1, g_post_ff1, w1_gate, w1_up, w1_down,
              g_pre_mix, g_post_mix, w_in, attn_sinks, ssm_a_re, ssm_a_im, ssm_log_step,
              ssm_b_re, ssm_b_im, ssm_c_re, ssm_c_im, ssm_d, ssm_w_glu, ssm_b_glu,
              g_attn_out, g_ssm_out, w_out, g_pre_ff2, g_post_ff2, w2_gate, w2_up, w2_down):
    bsz, s = x.shape[0], x.shape[1]
    c_act = jax.nn.silu(c)
    for l in range(DEPTH):
        mod = c_act @ w_ada[l] + b_ada[l]
        (sh1, sc1, ga1, sh2, sc2, ga2, sh3, sc3, ga3) = jnp.split(mod, N_MOD, axis=-1)

        h = modulate(rms_norm(x, g_pre_ff1[l]), sh1, sc1)
        f = swiglu(h, w1_gate[l], w1_up[l], w1_down[l])
        x = x + 0.5 * ga1[:, None, :] * rms_norm(f, g_post_ff1[l])

        h = modulate(rms_norm(x, g_pre_mix[l]), sh2, sc2)
        proj = h @ w_in[l]
        q = proj[..., :D_ATTN].reshape(bsz, s, N_Q_HEADS, HEAD_DIM)
        k = proj[..., D_ATTN:D_ATTN + D_KV].reshape(bsz, s, N_KV_HEADS, HEAD_DIM)
        v = proj[..., D_ATTN + D_KV:D_ATTN + 2 * D_KV].reshape(bsz, s, N_KV_HEADS, HEAD_DIM)
        u = proj[..., D_ATTN + 2 * D_KV:]
        attn = sliding_window_attention(q, k, v, attn_sinks[l])
        ssm = s5_ssm(u, ssm_a_re[l], ssm_a_im[l], ssm_log_step[l], ssm_b_re[l], ssm_b_im[l],
                     ssm_c_re[l], ssm_c_im[l], ssm_d[l], ssm_w_glu[l], ssm_b_glu[l])
        mixed = jnp.concatenate([rms_norm(attn, g_attn_out[l]), rms_norm(ssm, g_ssm_out[l])], axis=-1)
        mixed = mixed @ w_out[l]
        x = x + ga2[:, None, :] * rms_norm(mixed, g_post_mix[l])

        h = modulate(rms_norm(x, g_pre_ff2[l]), sh3, sc3)
        f = swiglu(h, w2_gate[l], w2_up[l], w2_down[l])
        x = x + 0.5 * ga3[:, None, :] * rms_norm(f, g_post_ff2[l])
    return x


DEPTH_2 = 2

RMS_EPS = 1e-6
D_FF_2 = 2816
MACARON_WEIGHT = 0.5
N_EVEN = (DEPTH_2 + 1) // 2
N_ODD = DEPTH_2 // 2

POOL_WIDTH = D_MODEL // 2
POOL_GROUPS = 4
POOL_GROUP_DIM = POOL_WIDTH // POOL_GROUPS
POOL_WINDOWS = (2, 4, 8, 16)

HYENA_WIDTH = D_MODEL // 2
HYENA_ORDER = 2
HYENA_SHORT_CONV = 3
HYENA_POS_DIM = 33
HYENA_FILTER_HIDDEN = 64
HYENA_FAST_DECAY_PCT = 0.3
HYENA_SLOW_DECAY_PCT = 1.5
HYENA_DECAY_TARGET = 1e-2

EVEN_IN_WIDTH = POOL_WIDTH + (HYENA_ORDER + 1) * HYENA_WIDTH
EVEN_OUT_WIDTH = POOL_WIDTH + HYENA_WIDTH

MLA_HEADS = 16
MLA_Q_LORA = 256
MLA_KV_LORA = 128
MLA_NOPE = 64
MLA_ROPE = 32
MLA_V = 64
ROPE_THETA = 10000.0
Q_BLOCK = 128


def rmsnorm(x, g):
    x32 = x.astype(jnp.float32)
    y = x32 * lax.rsqrt(jnp.mean(x32 * x32, axis=-1, keepdims=True) + RMS_EPS)
    return (y * g.astype(jnp.float32)).astype(x.dtype)

def swiglu_2(h, w_gate, w_up, w_down):
    return (jax.nn.silu(h @ w_gate) * (h @ w_up)) @ w_down

def centred_pool_minus_self(a):
    L = a.shape[1]
    a32 = a.astype(jnp.float32)
    csum = jnp.pad(jnp.cumsum(a32, axis=1), ((0, 0), (1, 0), (0, 0)))
    t = jnp.arange(L)
    outs = []
    for g, w in enumerate(POOL_WINDOWS):
        cg = csum[..., g * POOL_GROUP_DIM:(g + 1) * POOL_GROUP_DIM]
        lo = jnp.clip(t - w // 2, 0, L)
        hi = jnp.clip(t - w // 2 + w, 0, L)
        cnt = (hi - lo).astype(jnp.float32)[None, :, None]
        outs.append((jnp.take(cg, hi, axis=1) - jnp.take(cg, lo, axis=1)) / cnt)
    return (jnp.concatenate(outs, axis=-1) - a32).astype(a.dtype)

def pool_mixer(a, pool_w, pool_scale):
    B, L, _ = a.shape
    p = centred_pool_minus_self(a).reshape(B, L, POOL_GROUPS, POOL_GROUP_DIM)
    y = jnp.einsum('blgc,gcd->blgd', p, pool_w).reshape(B, L, POOL_WIDTH)
    return y * pool_scale

def short_conv_centred(u, w, b):
    L = u.shape[1]
    pad = HYENA_SHORT_CONV // 2
    up = jnp.pad(u, ((0, 0), (pad, HYENA_SHORT_CONV - 1 - pad), (0, 0)))
    y = b
    for k in range(HYENA_SHORT_CONV):
        y = y + up[:, k:k + L] * w[k]
    return y

def hyena_position_features(L):
    f32 = jnp.float32
    t = jnp.linspace(0.0, 1.0, L, dtype=f32)
    bands = (HYENA_POS_DIM - 1) // 2
    w = 2.0 * math.pi * jnp.arange(L, dtype=f32) / L
    f = jnp.linspace(1e-4, bands - 1, bands, dtype=f32)
    phase = w[:, None] * f[None, :]
    z = jnp.concatenate([t[:, None], jnp.cos(phase), -jnp.sin(phase)], axis=-1)
    return t, z

def hyena_filter_spectra(t, z, w1, b1, w2, b2, w3, b3, sin_freq, w_out, decay):
    f32 = jnp.float32
    L = t.shape[0]
    h = jnp.sin(sin_freq[0].astype(f32) * (z @ w1.astype(f32) + b1.astype(f32)))
    h = jnp.sin(sin_freq[1].astype(f32) * (h @ w2.astype(f32) + b2.astype(f32)))
    h = jnp.sin(sin_freq[2].astype(f32) * (h @ w3.astype(f32) + b3.astype(f32)))
    h = (h @ w_out.astype(f32)).reshape(L, HYENA_ORDER, 2, HYENA_WIDTH)
    h = h * jnp.exp(-t[:, None, None, None] * jnp.abs(decay.astype(f32)))
    fwd, bwd = h[:, :, 0], h[:, :, 1]
    two = jnp.concatenate(
        [fwd, jnp.zeros((1, HYENA_ORDER, HYENA_WIDTH), f32), bwd[:0:-1]], axis=0)
    two = two * lax.rsqrt(jnp.sum(two * two, axis=0, keepdims=True))
    return jnp.fft.rfft(two, axis=0)

def fft_long_conv(u, spec, bias):
    L = u.shape[1]
    u32 = u.astype(jnp.float32)
    y = jnp.fft.irfft(jnp.fft.rfft(u32, n=2 * L, axis=1) * spec[None], n=2 * L, axis=1)[:, :L]
    return (y + u32 * bias.astype(jnp.float32)).astype(u.dtype)

def hyena_mixer(u, conv_w, conv_b, spec, bias):
    u = short_conv_centred(u, conv_w, conv_b)
    parts = jnp.split(u, HYENA_ORDER + 1, axis=-1)
    z = parts[-1]
    for o in range(HYENA_ORDER):
        z = parts[o] * fft_long_conv(z, spec[:, o], bias[o])
    return z

def apply_rope(x, cos, sin):
    half = x.shape[-1] // 2
    x1, x2 = x[..., :half], x[..., half:]
    return jnp.concatenate([x1 * cos - x2 * sin, x1 * sin + x2 * cos], axis=-1)

def mla_mixer(h, w_dq, q_norm_g, w_uq, w_dkv, kv_norm_g, w_ukv, w_o, cos, sin):
    B, L, _ = h.shape
    cq = rmsnorm(h @ w_dq, q_norm_g)
    q = (cq @ w_uq).reshape(B, L, MLA_HEADS, MLA_NOPE + MLA_ROPE)
    q_nope, q_rope = q[..., :MLA_NOPE], q[..., MLA_NOPE:]
    q_rope = apply_rope(q_rope, cos[None, :, None, :], sin[None, :, None, :])
    ckv_full = h @ w_dkv
    ckv = rmsnorm(ckv_full[..., :MLA_KV_LORA], kv_norm_g)
    k_rope = apply_rope(ckv_full[..., MLA_KV_LORA:], cos[None], sin[None])
    kv = (ckv @ w_ukv).reshape(B, L, MLA_HEADS, MLA_NOPE + MLA_V)
    k_nope, v = kv[..., :MLA_NOPE], kv[..., MLA_NOPE:]
    scale = (MLA_NOPE + MLA_ROPE) ** -0.5
    nb = L // Q_BLOCK

    def to_blocks(a):
        return jnp.moveaxis(a.reshape(B, nb, Q_BLOCK, *a.shape[2:]), 1, 0)

    def attend(qs):
        qn, qr = qs
        s = (jnp.einsum('bqhd,bkhd->bhqk', qn, k_nope)
             + jnp.einsum('bqhr,bkr->bhqk', qr, k_rope))
        p = jax.nn.softmax(s.astype(jnp.float32) * scale, axis=-1).astype(v.dtype)
        return jnp.einsum('bhqk,bkhd->bqhd', p, v)

    o = lax.map(attend, (to_blocks(q_nope), to_blocks(q_rope)))
    o = jnp.moveaxis(o, 0, 1).reshape(B, L, MLA_HEADS * MLA_V)
    return o @ w_o

def second_inputs(seed: int = 0) -> dict:
    key = jax.random.key(seed)
    ks = iter(jax.random.split(key, 32))

    def nrm(shape, scale):
        return jax.random.normal(next(ks), shape, jnp.float32) * scale

    D, F, W, FH = D_MODEL, D_FF_2, HYENA_WIDTH, HYENA_FILTER_HIDDEN
    decay_base = jnp.linspace(-math.log(HYENA_DECAY_TARGET) / HYENA_SLOW_DECAY_PCT,
                              -math.log(HYENA_DECAY_TARGET) / HYENA_FAST_DECAY_PCT, W,
                              dtype=jnp.float32)
    inp = {}
    inp["x"] = nrm((BATCH, SEQ, D), 1.0)
    inp["norm_g"] = 1.0 + nrm((DEPTH_2, 3, D), 0.05)
    inp["ffn_w_gate"] = nrm((DEPTH_2, 2, D, F), D ** -0.5)
    inp["ffn_w_up"] = nrm((DEPTH_2, 2, D, F), D ** -0.5)
    inp["ffn_w_down"] = nrm((DEPTH_2, 2, F, D), F ** -0.5)
    inp["mix_w_in"] = nrm((N_EVEN, D, EVEN_IN_WIDTH), D ** -0.5)
    inp["pool_w"] = nrm((N_EVEN, POOL_GROUPS, POOL_GROUP_DIM, POOL_GROUP_DIM), POOL_GROUP_DIM ** -0.5)
    inp["pool_scale"] = 1.0 + nrm((N_EVEN, POOL_WIDTH), 0.05)
    inp["hyena_conv_w"] = nrm((N_EVEN, HYENA_SHORT_CONV, (HYENA_ORDER + 1) * W), HYENA_SHORT_CONV ** -0.5)
    inp["hyena_conv_b"] = nrm((N_EVEN, (HYENA_ORDER + 1) * W), 0.02)
    inp["hyena_ffn_w1"] = nrm((N_EVEN, HYENA_POS_DIM, FH), HYENA_POS_DIM ** -0.5)
    inp["hyena_ffn_b1"] = nrm((N_EVEN, FH), 0.02)
    inp["hyena_ffn_w2"] = nrm((N_EVEN, FH, FH), FH ** -0.5)
    inp["hyena_ffn_b2"] = nrm((N_EVEN, FH), 0.02)
    inp["hyena_ffn_w3"] = nrm((N_EVEN, FH, FH), FH ** -0.5)
    inp["hyena_ffn_b3"] = nrm((N_EVEN, FH), 0.02)
    inp["hyena_sin_freq"] = 1.0 + nrm((N_EVEN, 3, FH), 0.1)
    inp["hyena_ffn_w_out"] = nrm((N_EVEN, FH, HYENA_ORDER * 2 * W), FH ** -0.5)
    inp["hyena_decay"] = decay_base * jnp.exp(nrm((N_EVEN, HYENA_ORDER, 2, W), 0.1))
    inp["hyena_bias"] = nrm((N_EVEN, HYENA_ORDER, W), 0.5)
    inp["mix_w_out"] = nrm((N_EVEN, EVEN_OUT_WIDTH, D), EVEN_OUT_WIDTH ** -0.5)
    inp["mla_w_dq"] = nrm((N_ODD, D, MLA_Q_LORA), D ** -0.5)
    inp["mla_q_norm_g"] = 1.0 + nrm((N_ODD, MLA_Q_LORA), 0.05)
    inp["mla_w_uq"] = nrm((N_ODD, MLA_Q_LORA, MLA_HEADS * (MLA_NOPE + MLA_ROPE)), MLA_Q_LORA ** -0.5)
    inp["mla_w_dkv"] = nrm((N_ODD, D, MLA_KV_LORA + MLA_ROPE), D ** -0.5)
    inp["mla_kv_norm_g"] = 1.0 + nrm((N_ODD, MLA_KV_LORA), 0.05)
    inp["mla_w_ukv"] = nrm((N_ODD, MLA_KV_LORA, MLA_HEADS * (MLA_NOPE + MLA_V)), MLA_KV_LORA ** -0.5)
    inp["mla_w_o"] = nrm((N_ODD, MLA_HEADS * MLA_V, D), (MLA_HEADS * MLA_V) ** -0.5)
    inp["final_norm_g"] = 1.0 + nrm((D,), 0.05)
    return inp

def second_block(x, norm_g, ffn_w_gate, ffn_w_up, ffn_w_down, mix_w_in, pool_w, pool_scale,
              hyena_conv_w, hyena_conv_b, hyena_ffn_w1, hyena_ffn_b1, hyena_ffn_w2, hyena_ffn_b2,
              hyena_ffn_w3, hyena_ffn_b3, hyena_sin_freq, hyena_ffn_w_out, hyena_decay, hyena_bias,
              mix_w_out, mla_w_dq, mla_q_norm_g, mla_w_uq, mla_w_dkv, mla_kv_norm_g, mla_w_ukv,
              mla_w_o, final_norm_g):
    L = x.shape[1]
    t_pos, z_pos = hyena_position_features(L)
    inv_freq = ROPE_THETA ** (-jnp.arange(0, MLA_ROPE, 2, dtype=jnp.float32) / MLA_ROPE)
    ang = jnp.arange(L, dtype=jnp.float32)[:, None] * inv_freq[None, :]
    cos = jnp.cos(ang).astype(x.dtype)
    sin = jnp.sin(ang).astype(x.dtype)

    for i in range(DEPTH_2):
        x = x + MACARON_WEIGHT * swiglu_2(rmsnorm(x, norm_g[i, 0]),
                                        ffn_w_gate[i, 0], ffn_w_up[i, 0], ffn_w_down[i, 0])
        h = rmsnorm(x, norm_g[i, 1])
        j = i // 2
        if i % 2 == 0:
            proj = h @ mix_w_in[j]
            y_pool = pool_mixer(proj[..., :POOL_WIDTH], pool_w[j], pool_scale[j])
            spec = hyena_filter_spectra(t_pos, z_pos, hyena_ffn_w1[j], hyena_ffn_b1[j],
                                        hyena_ffn_w2[j], hyena_ffn_b2[j], hyena_ffn_w3[j],
                                        hyena_ffn_b3[j], hyena_sin_freq[j], hyena_ffn_w_out[j],
                                        hyena_decay[j])
            y_hyena = hyena_mixer(proj[..., POOL_WIDTH:], hyena_conv_w[j], hyena_conv_b[j],
                                  spec, hyena_bias[j])
            x = x + jnp.concatenate([y_pool, y_hyena], axis=-1) @ mix_w_out[j]
        else:
            x = x + mla_mixer(h, mla_w_dq[j], mla_q_norm_g[j], mla_w_uq[j], mla_w_dkv[j],
                              mla_kv_norm_g[j], mla_w_ukv[j], mla_w_o[j], cos, sin)
        x = x + MACARON_WEIGHT * swiglu_2(rmsnorm(x, norm_g[i, 2]),
                                        ffn_w_gate[i, 1], ffn_w_up[i, 1], ffn_w_down[i, 1])
    return rmsnorm(x, final_norm_g)


def setup_inputs(seed=0):
    out = dict(first_inputs(seed))
    for name, value in second_inputs(seed + 1).items():
        if name != "x":
            out[name + "_2"] = value
    return out


def reference(
    x, c, w_ada, b_ada, g_pre_ff1, g_post_ff1, w1_gate, w1_up, w1_down, g_pre_mix, g_post_mix,
    w_in, attn_sinks, ssm_a_re, ssm_a_im, ssm_log_step, ssm_b_re, ssm_b_im, ssm_c_re, ssm_c_im,
    ssm_d, ssm_w_glu, ssm_b_glu, g_attn_out, g_ssm_out, w_out, g_pre_ff2, g_post_ff2, w2_gate,
    w2_up, w2_down, norm_g_2, ffn_w_gate_2, ffn_w_up_2, ffn_w_down_2, mix_w_in_2, pool_w_2,
    pool_scale_2, hyena_conv_w_2, hyena_conv_b_2, hyena_ffn_w1_2, hyena_ffn_b1_2,
    hyena_ffn_w2_2, hyena_ffn_b2_2, hyena_ffn_w3_2, hyena_ffn_b3_2, hyena_sin_freq_2,
    hyena_ffn_w_out_2, hyena_decay_2, hyena_bias_2, mix_w_out_2, mla_w_dq_2, mla_q_norm_g_2,
    mla_w_uq_2, mla_w_dkv_2, mla_kv_norm_g_2, mla_w_ukv_2, mla_w_o_2, final_norm_g_2,
):
    x = first_block(
        x, c, w_ada, b_ada, g_pre_ff1, g_post_ff1, w1_gate, w1_up, w1_down, g_pre_mix,
        g_post_mix, w_in, attn_sinks, ssm_a_re, ssm_a_im, ssm_log_step, ssm_b_re, ssm_b_im,
        ssm_c_re, ssm_c_im, ssm_d, ssm_w_glu, ssm_b_glu, g_attn_out, g_ssm_out, w_out,
        g_pre_ff2, g_post_ff2, w2_gate, w2_up, w2_down,
    )
    return second_block(
        x, norm_g_2, ffn_w_gate_2, ffn_w_up_2, ffn_w_down_2, mix_w_in_2, pool_w_2, pool_scale_2,
        hyena_conv_w_2, hyena_conv_b_2, hyena_ffn_w1_2, hyena_ffn_b1_2, hyena_ffn_w2_2,
        hyena_ffn_b2_2, hyena_ffn_w3_2, hyena_ffn_b3_2, hyena_sin_freq_2, hyena_ffn_w_out_2,
        hyena_decay_2, hyena_bias_2, mix_w_out_2, mla_w_dq_2, mla_q_norm_g_2, mla_w_uq_2,
        mla_w_dkv_2, mla_kv_norm_g_2, mla_w_ukv_2, mla_w_o_2, final_norm_g_2,
    )


_drawn_inputs = setup_inputs


def setup_inputs(seed=0):
    import zlib

    import numpy as np

    out = dict(_drawn_inputs(seed))
    spreads = {}
    factors = {'g_pre_ff1': 3.622,
     'g_post_ff1': 4.798,
     'ssm_a_re': 8.0,
     'ssm_log_step': 2.886,
     'ssm_b_re': 3.159,
     'ssm_b_im': 3.277,
     'ssm_c_re': 3.066,
     'ssm_c_im': 3.217,
     'ssm_b_glu': 8.0,
     'g_attn_out': 2.694,
     'g_ssm_out': 3.086,
     'g_pre_ff2': 3.872,
     'g_post_ff2': 5.959,
     'pool_scale_2': 3.084,
     'mla_q_norm_g_2': 8.0,
     'mla_kv_norm_g_2': 8.0}
    for name, (base, spread) in spreads.items():
        noise = np.random.default_rng([zlib.crc32(name.encode()), seed]).standard_normal(out[name].shape)
        drawn = base * np.exp(spread * noise) if base else spread * noise
        out[name] = __import__('jax').numpy.asarray(drawn.astype(out[name].dtype))
    for name, factor in factors.items():
        out[name] = (out[name] * factor).astype(out[name].dtype)
    return out
```

```python
import math
from contextlib import ExitStack

import numpy as np
import concourse.bass as bass
from concourse import mybir

F32 = mybir.dt.float32
F32R = mybir.dt.float32r
I32 = mybir.dt.int32
ALU = mybir.AluOpType
ACT = mybir.ActivationFunctionType
AX = mybir.AxisListType

P = 128
D = 1024
KT = D // P
SEQ = 256
MT = SEQ // P
FF = 2816
FT = FF // P
PANEL = 1024
RING = 6
EPS = 1e-6
HEADS, HD = 8, 64
STATE_TILES = 16
MLA_HEADS = 16
ADA_RING = 4

FFN_PANELS = 3 * FT
MIX1_PANELS = 10 + 2 + 8
MIX2_PANELS = 4 + 12 + 8
MIX3_PANELS = 4 + 4 + 2 + 8
STAGES = [("ffn", 0), ("mix1", 0), ("ffn", 1), ("ffn", 2), ("mix2", 0), ("ffn", 3),
          ("ffn", 4), ("mix3", 0), ("ffn", 5)]
SIZE = {"ffn": FFN_PANELS, "mix1": MIX1_PANELS, "mix2": MIX2_PANELS, "mix3": MIX3_PANELS}
FIRST = {}
TOTAL = 0
for _s in STAGES:
    FIRST[_s] = TOTAL
    TOTAL += SIZE[_s[0]]

COLS = {}
_w = 0
for _name, _n in (("c", 8), ("b_ada", 72), ("g_pre", 24), ("norm_g", 48), ("pool_scale", 4),
                  ("conv_b", 12), ("conv_w", 36), ("bias", 8), ("g_attn", 4), ("g_ssm", 4),
                  ("ssm_d", 4), ("b_glu", 4), ("q_g", 2), ("kv_g", 1), ("a_re", 16), ("a_im", 16),
                  ("log_step", 16), ("sin_freq", 3), ("mlp_b", 3), ("neg_t", 2)):
    COLS[_name] = (_w, _n)
    _w += _n
N_COLS = _w

MAGIC = 12582912.0
TWO_PI = 2.0 * math.pi
TWO_PI_HI = 6.28125
TWO_PI_LO = TWO_PI - TWO_PI_HI
LN2_HI = 0.693359375
LN2_LO = math.log(2.0) - LN2_HI
PI_BELOW = 3.1415925


def build_program(nc, panels, ada, cols, rows, sinks, ssm_mats, tables, pool_mats, rope, near,
                  pool_w, decay, mlp_w, feats, x_in, out, spectrum, last_stage):
    ctx = ExitStack()
    with ctx:
        def sb(name, shape, dt=F32):
            return ctx.enter_context(nc.sbuf_tensor(name, shape, dt))

        def sem(name):
            return ctx.enter_context(nc.semaphore(name))

        X = sb("X", [P, MT, D])
        raw = sb("raw", [P, RING, PANEL])
        w_hi = sb("w_hi", [P, RING, PANEL], F32R)
        w_lo = sb("w_lo", [P, RING, PANEL], F32R)
        h_hi = sb("h_hi", [P, KT, SEQ], F32R)
        h_lo = sb("h_lo", [P, KT, SEQ], F32R)
        f_hi = sb("f_hi", [P, 2, SEQ], F32R)
        f_lo = sb("f_lo", [P, 2, SEQ], F32R)
        C = sb("C", [P, N_COLS])
        ident = sb("ident", [P, P])
        ones = sb("ones", [P, P])
        mods = sb("mods", [P, 6, KT])
        pre_scale = sb("pre_scale", [P, 3, KT])
        stat = sb("stat", [P, 64])
        par = sb("par", [P, 20, 16])
        ARENA = 26112
        arena = sb("arena", [P, ARENA])

        def region(at, *shape):
            size = int(np.prod(shape))
            assert at + size <= ARENA, (at, shape)
            v = arena[:, at:at + size]
            if len(shape) == 2:
                return v.rearrange("p (a b) -> p a b", b=shape[1])
            if len(shape) == 3:
                return v.rearrange("p (a b c) -> p a b c", b=shape[1], c=shape[2])
            return v

        xhat = region(0, MT, D)
        h32 = region(2048, KT, SEQ)
        acc = region(0, 7, D)
        acc0 = region(4096, 2, D)
        ada_ring = region(7168, ADA_RING, D)
        gate_rows = region(11264, 3, D)
        ssm_raw = region(11264, 4, 256)
        rot_tmp = region(11264, 16, 128)
        b_rows = region(13312, 2, 512)
        rot = region(14336, 2, STATE_TILES, SEQ)
        b_turned = region(22528, 2, 4, P)
        c_rows = region(23552, 3, STATE_TILES, 32)
        ffn_buf = region(25088, 4, SEQ)

        def col(name, i=0, n=1):
            at, _ = COLS[name]
            return C[:, at + i:at + i + n]

        bank = [ctx.enter_context(nc.psum_tensor(f"bank{i}", [P, 512], F32)) for i in range(8)]

        raw_loaded = [sem(f"raw_loaded{i}") for i in range(RING)]
        ada_loaded = [sem(f"ada_loaded{i}") for i in range(ADA_RING)]
        hi_ready = sem("hi_ready")
        lo_ready = sem("lo_ready")
        panel_used = sem("panel_used")
        ada_used = sem("ada_used")
        act_order = sem("act_order")
        dve_order = sem("dve_order")
        pool_order = sem("pool_order")

        class Order:
            def __init__(self, eng, s):
                self.eng, self.s, self.n = eng, s, 0

            def __call__(self, ins):
                self.n += 1
                ins.then_inc(self.s, 1)
                self.eng.wait_ge(self.s, self.n)

        def then(eng, ins, s, value):
            ins.then_inc(s, 1)
            eng.wait_ge(s, value)

        def split_hi(act, g0, i=0):
            slot = g0 % RING
            act.wait_ge(raw_loaded[slot], 16 * (g0 // RING + 1) + 16 * i)
            if g0 >= RING:
                act.wait_ge(panel_used, g0 - (RING - 1) + RING * i)
            act.activation(w_hi[:, slot, :], raw[:, slot, :], ACT.Copy).then_inc(hi_ready, 1)

        def split_lo(dve, g0, i=0):
            slot = g0 % RING
            dve.wait_ge(hi_ready, g0 + 1 + RING * i)
            dve.tensor_tensor(w_lo[:, slot, :], raw[:, slot, :], w_hi[:, slot, :].bitcast(F32),
                              ALU.subtract).then_inc(lo_ready, 1)

        def act_panels(act, first, n):
            for g in range(first, min(first + n, TOTAL)):
                split_hi(act, g)

        def dve_panels(dve, first, n):
            for g in range(first, min(first + n, TOTAL)):
                split_lo(dve, g)

        def product3(pe, out_ap, wh, wl, xh, xl, start, stop, weights_move=False):
            last = None
            for n, (w, x) in enumerate(((wh, xh), (wh, xl), (wl, xh))):
                a, b = (x, w) if weights_move else (w, x)
                last = pe.matmul(out_ap, a, b, start=start and n == 0, stop=stop and n == 2)
            return last

        def channel_product(pe, out_ap, g0, i=0, k_tiles=KT, at=0, k0=0, used=True):
            slot = g0 % RING
            pe.wait_ge(lo_ready, g0 + 1 + RING * i)
            mm = None
            for k in range(k_tiles):
                w = slice(at + k * P, at + (k + 1) * P)
                mm = product3(pe, out_ap, w_hi[:, slot, w], w_lo[:, slot, w], h_hi[:, k0 + k, :],
                              h_lo[:, k0 + k, :], k == 0, k == k_tiles - 1)
            if used:
                mm.then_inc(panel_used, 1)
            return mm

        def token_product(pe, g0, xh, xl, start, stop, i=0):
            slot = g0 % RING
            pe.wait_ge(lo_ready, g0 + 1 + RING * i)
            mm = None
            for m in range(MT):
                t = slice(m * P, (m + 1) * P)
                for n in range(2):
                    w = slice(n * 512, (n + 1) * 512)
                    mm = product3(pe, bank[2 * m + n][:, :], w_hi[:, slot, w], w_lo[:, slot, w],
                                  xh[:, t], xl[:, t], start, stop, weights_move=True)
            mm.then_inc(panel_used, 1)

        square_done = sem("square_done")
        rstd_done = sem("rstd_done")
        xhat_done = sem("xhat_done")
        turned = sem("turned")
        evac_act = sem("evac_act")
        evac_dve = sem("evac_dve")
        h_hi_done = sem("h_hi_done")
        h_lo_done = sem("h_lo_done")
        x_done = sem("x_done")
        SS, RS = 0, 2
        MINUS_HALF = 63

        def norm_scalars(n):
            if n in (0, 1, 2):
                return pre_scale[:, n, :], mods[:, 2 * n, :]
            at, _ = COLS["norm_g"]
            return C[:, at + (n - 3) * KT:at + (n - 2) * KT], None

        def norm_act_squares(act, n):
            act.wait_ge(x_done, 4 * n) if n else act.wait_ge(x_loaded, 16)
            for m in range(MT):
                act.activation(xhat[:, m, :], X[:, m, :], ACT.Square,
                               accum_out=stat[:, SS + m:SS + m + 1]).then_inc(square_done, 1)

        def norm_act_rest(act, n):
            sc, sh = norm_scalars(n)
            for b in (0, 2):
                act.wait_ge(turned, 4 * n + b + 1)
                for j in range(2):
                    k = 2 * b + j
                    ps = bank[4 + b][:, j * SEQ:(j + 1) * SEQ]
                    act.activation(h32[:, k, :], ps, ACT.Identity, scale=sc[:, k:k + 1],
                                   bias=0.0 if sh is None else sh[:, k:k + 1]).then_inc(evac_act, 1)
            for b in range(4):
                act.wait_ge(*((evac_act, 4 * n + b + 2) if b % 2 == 0 else (evac_dve, 4 * n + b + 1)))
                act.activation(h_hi[:, 2 * b:2 * b + 2, :], h32[:, 2 * b:2 * b + 2, :],
                               ACT.Copy).then_inc(h_hi_done, 1)

        def norm_pool(pool, n, order):
            for m in range(MT):
                pool.wait_ge(square_done, 2 * n + m + 1)
                ss = stat[:, SS + m:SS + m + 1]
                rs = stat[:, RS + m:RS + m + 1]
                order(pool.tensor_scalar(rs, ss, 1.0 / D, EPS, ALU.mult, ALU.add))
                pool.tensor_tensor(rs, rs, stat[:, MINUS_HALF:MINUS_HALF + 1],
                                   ALU.pow).then_inc(rstd_done, 1)

        def norm_dve(dve, n):
            for m in range(MT):
                dve.wait_ge(rstd_done, 2 * n + m + 1)
                dve.tensor_scalar(xhat[:, m, :], X[:, m, :], stat[:, RS + m:RS + m + 1], None,
                                  ALU.mult).then_inc(xhat_done, 1)
            sc, sh = norm_scalars(n)
            for b in (1, 3):
                dve.wait_ge(turned, 4 * n + b + 1)
                for j in range(2):
                    k = 2 * b + j
                    ps = bank[4 + b][:, j * SEQ:(j + 1) * SEQ]
                    if sh is None:
                        ins = dve.tensor_scalar(h32[:, k, :], ps, sc[:, k:k + 1], None, ALU.mult)
                    else:
                        ins = dve.tensor_scalar(h32[:, k, :], ps, sc[:, k:k + 1], sh[:, k:k + 1],
                                                ALU.mult, ALU.add)
                    ins.then_inc(evac_dve, 1)
            for b in range(4):
                dve.wait_ge(h_hi_done, 4 * n + b + 1)
                r = slice(2 * b, 2 * b + 2)
                dve.tensor_tensor(h_lo[:, r, :], h32[:, r, :], h_hi[:, r, :].bitcast(F32),
                                  ALU.subtract).then_inc(h_lo_done, 1)

        def norm_pe(pe, n):
            for m in range(MT):
                pe.wait_ge(xhat_done, 2 * n + m + 1)
                for b in range(4):
                    for j in range(2):
                        k = 2 * b + j
                        tr = pe.transpose(bank[4 + b][:, j * SEQ + m * P:j * SEQ + (m + 1) * P],
                                          xhat[:, m, k * P:(k + 1) * P], ident[:, :])
                    if m == MT - 1:
                        tr.then_inc(turned, 1)
            pe.wait_ge(h_lo_done, 4 * n + 4)

        silu_done = sem("silu_done")
        hidden_done = sem("hidden_done")
        f_hi_done = sem("f_hi_done")
        f_lo_done = sem("f_lo_done")

        def ffn_pe(pe, n):
            base, s0 = FIRST[("ffn", n)], FT * n

            def up(f, i=0):
                g = base + max(3 * f - 1, 0)
                if s0 + f >= 2:
                    pe.wait_ge(hidden_done, s0 + f - 1 + 2 * i)
                channel_product(pe, bank[4 + f % 2][:, 0:SEQ], g, i)
                channel_product(pe, bank[4 + f % 2][:, SEQ:2 * SEQ], g + 1, i)

            def down(f, i=0, start=False, stop=False):
                pe.wait_ge(f_lo_done, s0 + f + 1 + 2 * i)
                g = base + (3 * FT - 1 if stop else 3 * f + 4)
                token_product(pe, g, f_hi[:, f % 2, :], f_lo[:, f % 2, :], start, stop, i)

            def tiles(lo, hi):
                with pe.Fori(lo, hi) as i:
                    up(2, i)
                    down(1, i)
                    up(3, i)
                    down(2, i)

            up(0)
            up(1)
            down(0, start=True)
            if n == 0:
                tiles(0, 7)
                turn_b_pe(pe)
                tiles(7, FT // 2 - 1)
                ada_rest_pe(pe)
            else:
                tiles(0, FT // 2 - 1)
            down(FT - 1, stop=True)

        def ffn_act(act, n):
            base, s0 = FIRST[("ffn", n)], FT * n

            def hidden(f, i=0):
                act.wait_ge(panel_used, base + (3 * f + 1 if f else 2) + RING * i)
                act.activation(ffn_buf[:, f % 2, :], bank[4 + f % 2][:, 0:SEQ],
                               ACT.Silu).then_inc(silu_done, 1)
                act.wait_ge(hidden_done, s0 + f + 1 + 2 * i)
                act.activation(f_hi[:, f % 2, :], ffn_buf[:, 2 + f % 2, :],
                               ACT.Copy).then_inc(f_hi_done, 1)

            def tiles(lo, hi):
                with act.Fori(lo, hi) as i:
                    for f in (2, 3):
                        for j in range(3):
                            split_hi(act, base + 3 * f + 2 + j, i)
                        hidden(f, i)

            act_panels(act, base + 3, 2)
            hidden(0)
            act_panels(act, base + 5, 3)
            hidden(1)
            if n == 0:
                tiles(0, 7)
                turn_b_act(act)
                tiles(7, FT // 2 - 2)
            else:
                tiles(0, FT // 2 - 2)
            for f in (FT - 2, FT - 1):
                act_panels(act, base + 3 * f + 2, 3)
                hidden(f)
            act_panels(act, base + 3 * FT + 2, 1)

        def ffn_dve(dve, n):
            base, s0 = FIRST[("ffn", n)], FT * n

            def hidden(f, i=0):
                dve.wait_ge(silu_done, s0 + f + 1 + 2 * i)
                if s0 + f >= 2:
                    dve.wait_ge(f_lo_done, s0 + f - 1 + 2 * i)
                dve.tensor_tensor(ffn_buf[:, 2 + f % 2, :], ffn_buf[:, f % 2, :],
                                  bank[4 + f % 2][:, SEQ:2 * SEQ], ALU.mult).then_inc(hidden_done, 1)
                dve.wait_ge(f_hi_done, s0 + f + 1 + 2 * i)
                dve.tensor_tensor(f_lo[:, f % 2, :], ffn_buf[:, 2 + f % 2, :],
                                  f_hi[:, f % 2, :].bitcast(F32), ALU.subtract).then_inc(f_lo_done, 1)

            def tiles(lo, hi, with_ada=False):
                with dve.Fori(lo, hi) as i:
                    for f in (2, 3):
                        for j in range(3):
                            split_lo(dve, base + 3 * f + 2 + j, i)
                        if with_ada:
                            for k in range(4 * (f - 2), 4 * (f - 1)):
                                ada_add(dve, 2, k, i)
                        hidden(f, i)

            dve_panels(dve, base + 3, 2)
            hidden(0)
            dve_panels(dve, base + 5, 3)
            hidden(1)
            if n == 0:
                tiles(0, 7, with_ada=True)
                tiles(7, FT // 2 - 2)
            else:
                tiles(0, FT // 2 - 2)
            for f in (FT - 2, FT - 1):
                dve_panels(dve, base + 3 * f + 2, 3)
                hidden(f)
            dve_panels(dve, base + 3 * FT + 2, 1)

        result_squares = sem("result_squares")
        result_rstd = sem("result_rstd")
        RSS, RRS = 4, 8

        def last_panel(kind, n):
            return FIRST[(kind, n)] + SIZE[kind]

        def add_act(act, kind, n, r):
            act.wait_ge(panel_used, last_panel(kind, n))
            for q in range(4):
                act.activation(xhat[:, q // 2, (q % 2) * 512:(q % 2) * 512 + 512], bank[q][:, :],
                               ACT.Square,
                               accum_out=stat[:, RSS + q:RSS + q + 1]).then_inc(result_squares, 1)

        def add_pool(pool, r, order):
            pool.wait_ge(result_squares, 4 * r + 4)
            order(pool.tensor_tensor(stat[:, RRS:RRS + 2], stat[:, RSS:RSS + 4:2],
                                     stat[:, RSS + 1:RSS + 4:2], ALU.add))
            order(pool.tensor_scalar(stat[:, RRS:RRS + 2], stat[:, RRS:RRS + 2], 1.0 / D, EPS,
                                     ALU.mult, ALU.add))
            pool.tensor_tensor(stat[:, RRS:RRS + 2], stat[:, RRS:RRS + 2],
                               stat[:, MINUS_HALF - 1:MINUS_HALF + 1], ALU.pow).then_inc(result_rstd, 1)

        def add_dve(dve, kind, n, r, order):
            if r is not None:
                dve.wait_ge(result_rstd, r + 1)
            else:
                dve.wait_ge(panel_used, last_panel(kind, n))
            for q in range(4):
                m, c = q // 2, slice((q % 2) * 512, (q % 2) * 512 + 512)
                if r is None:
                    dve.scalar_tensor_tensor(out=X[:, m, c], in0=bank[q][:, :],
                                             scalar=0.5 if kind == "ffn" else 1.0, in1=X[:, m, c],
                                             op0=ALU.mult, op1=ALU.add).then_inc(x_done, 1)
                    continue
                order(dve.scalar_tensor_tensor(out=xhat[:, m, c], in0=bank[q][:, :],
                                               scalar=stat[:, RRS + m:RRS + m + 1],
                                               in1=gate_rows[:, r, c], op0=ALU.mult, op1=ALU.mult))
                dve.tensor_tensor(X[:, m, c], X[:, m, c], xhat[:, m, c], ALU.add).then_inc(x_done, 1)

        c_ready = sem("c_ready")
        x_loaded = sem("x_loaded")
        small_loaded = sem("small_loaded")
        const_ready = sem("const_ready")
        column_sums = sem("column_sums")
        mods_done = sem("mods_done")
        gate_sums = sem("gate_sums")
        gate_read = sem("gate_read")
        gate_bias = sem("gate_bias")
        c_act = stat[:, 16:16 + KT]

        def ada_add(dve, chunk, k, i=0):
            a = 8 * chunk + k
            slot = a % ADA_RING
            dve.wait_ge(ada_loaded[slot], 16 * (a // ADA_RING + 1) + 32 * i)
            dst = acc0[:, chunk, :] if chunk < 2 else acc[:, i, :]
            src = ada_ring[:, slot, :]
            if k:
                dve.wait_ge(ada_used, a + 8 * i)
                dve.scalar_tensor_tensor(out=dst, in0=src, scalar=c_act[:, k:k + 1], in1=dst,
                                         op0=ALU.mult, op1=ALU.add).then_inc(ada_used, 1)
            else:
                dve.tensor_scalar(dst, src, c_act[:, 0:1], None, ALU.mult).then_inc(ada_used, 1)

        def sum_columns(pe, part, at):
            mm = None
            for k in range(KT):
                mm = pe.matmul(bank[7][:, at + k:at + k + 1], part[:, k * P:(k + 1) * P],
                               ones[:, 0:1], start=True, stop=True)
            return mm

        def ada_first_pe(pe):
            for c in range(2):
                pe.wait_ge(ada_used, 8 * c + 8)
                sum_columns(pe, acc0[:, c, :], 8 * c).then_inc(column_sums, 1)

        def ada_first_dve(dve, order):
            dve.wait_ge(column_sums, 2)
            for j in range(2):
                order(dve.tensor_tensor(mods[:, j, :], bank[7][:, 8 * j:8 * j + 8],
                                        col("b_ada", 8 * j, 8), ALU.add))
            dve.scalar_tensor_tensor(out=pre_scale[:, 0, :], in0=mods[:, 1, :], scalar=1.0,
                                     in1=col("g_pre", 0, 8), op0=ALU.add,
                                     op1=ALU.mult).then_inc(mods_done, 1)

        GATES = (0, 3, 6)
        COLUMNS = ((1, 2), (2, 3), (4, 4), (5, 5))

        def ada_rest_pe(pe):
            pe.wait_ge(ada_used, 72)
            pe.wait_ge(b_evacuated, 2)
            for j, (chunk, _) in enumerate(COLUMNS):
                sum_columns(pe, acc[:, chunk, :], 8 * j).then_inc(column_sums, 1)
            for q in range(6):
                if q == 1:
                    pe.wait_ge(mods_done, 2)
                if q >= 2:
                    pe.wait_ge(gate_read, q - 1)
                c = slice((q % 2) * 512, (q % 2) * 512 + 512)
                pe.matmul(bank[6 + q % 2][:, :], ones[:, :], acc[:, GATES[q // 2], c],
                          start=True, stop=True).then_inc(gate_sums, 1)

        def ada_rest_dve(dve, order):
            dve.wait_ge(column_sums, 6)
            for j, (_, row) in enumerate(COLUMNS):
                chunk = 3 + (row - 2) % 2 + 3 * ((row - 2) // 2)
                order(dve.tensor_tensor(mods[:, row, :], bank[7][:, 8 * j:8 * j + 8],
                                        col("b_ada", 8 * chunk, 8), ALU.add))
            order(dve.scalar_tensor_tensor(out=pre_scale[:, 1, :], in0=mods[:, 3, :], scalar=1.0,
                                           in1=col("g_pre", 8, 8), op0=ALU.add, op1=ALU.mult))
            dve.scalar_tensor_tensor(out=pre_scale[:, 2, :], in0=mods[:, 5, :], scalar=1.0,
                                     in1=col("g_pre", 16, 8), op0=ALU.add,
                                     op1=ALU.mult).then_inc(mods_done, 1)
            dve.wait_ge(gate_bias, 32)
            for q in range(6):
                c = slice((q % 2) * 512, (q % 2) * 512 + 512)
                dve.wait_ge(gate_sums, q + 1)
                row = gate_rows[:, q // 2, c]
                then(dve, dve.tensor_tensor(row, bank[6 + q % 2][:, :], row, ALU.add),
                     gate_read, q + 1)
                order(dve.scalar_tensor_tensor(out=row, in0=row, scalar=1.0 if q // 2 == 1 else 0.5,
                                               in1=ada_ring[:, q // 2, c], op0=ALU.mult, op1=ALU.mult))

        def gate_rows_pool(pool):
            pool.wait_ge(ada_used, 72)
            pool.wait_ge(b_evacuated, 2)
            pool.dma_start(gate_rows[:, :, :], rows[0:3, :].partition_broadcast(P)).then_inc(gate_bias, 16)
            pool.dma_start(ada_ring[:, 0:3, :], rows[3:6, :].partition_broadcast(P)).then_inc(gate_bias, 16)

        DT, XR, YI, T0, T1, T2, SIN, SINH, TANH, REC, RAD, EM1, COSM1, COS, LR, LI, CR, CI, INV = range(19)
        angles_ready = sem("angles_ready")
        angles_done = sem("angles_done")
        params_done = sem("params_done")
        ssm_loaded = sem("ssm_loaded")
        b_ready = sem("b_ready")
        b_in_psum = sem("b_in_psum")
        b_evacuated = sem("b_evacuated")
        rot_ready = sem("rot_ready")
        c_rows_ready = sem("c_rows_ready")

        def pr(i):
            return par[:, i, :]

        def round_off(dve, order, arg, k, turns, hi, lo):
            order(dve.tensor_scalar(k, arg, turns, MAGIC, ALU.mult, ALU.add))
            order(dve.tensor_scalar(k, k, -MAGIC, None, ALU.add))
            order(dve.scalar_tensor_tensor(out=arg, in0=k, scalar=-hi, in1=arg, op0=ALU.mult, op1=ALU.add))
            order(dve.scalar_tensor_tensor(out=arg, in0=k, scalar=-lo, in1=arg, op0=ALU.mult, op1=ALU.add))

        def params_dve(dve, order):
            order(dve.tensor_copy(pr(T0), col("log_step", 0, 16)))
            round_off(dve, order, pr(T0), pr(T1), 1.0 / math.log(2.0), LN2_HI, LN2_LO)
            order(dve.tensor_scalar(pr(T2), pr(T0), 1.0 / 40320, None, ALU.mult))
            for n in (7, 6, 5, 4, 3, 2, 1):
                order(dve.scalar_tensor_tensor(out=pr(T2), in0=pr(T2), scalar=1.0 / math.factorial(n),
                                               in1=pr(T0), op0=ALU.add, op1=ALU.mult))
            order(dve.tensor_scalar(pr(T1), pr(T1), -126.0, 127.0, ALU.max, ALU.min))
            order(dve.tensor_scalar(pr(DT).bitcast(I32), pr(T1), 127.0, 8388608.0, ALU.add, ALU.mult))
            order(dve.scalar_tensor_tensor(out=pr(DT), in0=pr(T2), scalar=1.0, in1=pr(DT),
                                           op0=ALU.add, op1=ALU.mult))
            order(dve.tensor_tensor(pr(XR), pr(DT), col("a_re", 0, 16), ALU.mult))
            order(dve.tensor_tensor(pr(YI), pr(DT), col("a_im", 0, 16), ALU.mult))
            round_off(dve, order, pr(YI), pr(T1), 1.0 / TWO_PI, TWO_PI_HI, TWO_PI_LO)
            dve.tensor_scalar(pr(YI), pr(YI), PI_BELOW, -PI_BELOW, ALU.min,
                              ALU.max).then_inc(angles_ready, 1)
            dve.wait_ge(angles_done, 3)
            order(dve.tensor_scalar(pr(REC), pr(TANH), -1.0, 1.0, ALU.mult, ALU.add))
            order(dve.reciprocal(pr(REC), pr(REC)))
            order(dve.scalar_tensor_tensor(out=pr(RAD), in0=pr(TANH), scalar=1.0, in1=pr(REC),
                                           op0=ALU.add, op1=ALU.mult))
            order(dve.scalar_tensor_tensor(out=pr(EM1), in0=pr(TANH), scalar=2.0, in1=pr(REC),
                                           op0=ALU.mult, op1=ALU.mult))
            order(dve.scalar_tensor_tensor(out=pr(COSM1), in0=pr(SINH), scalar=-2.0, in1=pr(SINH),
                                           op0=ALU.mult, op1=ALU.mult))
            order(dve.tensor_scalar(pr(COS), pr(COSM1), 1.0, None, ALU.add))
            order(dve.tensor_tensor(pr(LR), pr(EM1), pr(COS), ALU.mult))
            order(dve.tensor_tensor(pr(LR), pr(LR), pr(COSM1), ALU.add))
            order(dve.tensor_tensor(pr(LI), pr(RAD), pr(SIN), ALU.mult))
            are, aim = col("a_re", 0, 16), col("a_im", 0, 16)
            order(dve.tensor_tensor(pr(T0), are, are, ALU.mult))
            order(dve.tensor_tensor(pr(T1), aim, aim, ALU.mult))
            order(dve.tensor_tensor(pr(INV), pr(T0), pr(T1), ALU.add))
            order(dve.reciprocal(pr(INV), pr(INV)))
            order(dve.tensor_tensor(pr(T0), pr(LR), are, ALU.mult))
            order(dve.tensor_tensor(pr(T1), pr(LI), aim, ALU.mult))
            order(dve.tensor_tensor(pr(T0), pr(T0), pr(T1), ALU.add))
            order(dve.tensor_tensor(pr(CR), pr(T0), pr(INV), ALU.mult))
            order(dve.tensor_tensor(pr(T0), pr(LI), are, ALU.mult))
            order(dve.tensor_tensor(pr(T1), pr(LR), aim, ALU.mult))
            order(dve.tensor_tensor(pr(T0), pr(T0), pr(T1), ALU.subtract))
            dve.tensor_tensor(pr(CI), pr(T0), pr(INV), ALU.mult).then_inc(params_done, 1)

        def params_act(act):
            act.wait_ge(angles_ready, 1)
            act.activation(pr(SIN), pr(YI), ACT.Sin).then_inc(angles_done, 1)
            act.activation(pr(SINH), pr(YI), ACT.Sin, scale=0.5).then_inc(angles_done, 1)
            act.activation(pr(TANH), pr(XR), ACT.Tanh, scale=0.5).then_inc(angles_done, 1)

        def wide(ap, *shape):
            return ap.unsqueeze(2).to_broadcast([ap.shape[0], 16, shape[0]])

        def params_pool(pool, order):
            pool.wait_ge(params_done, 1)
            pool.wait_ge(spectrum_stored, 32)
            pool.dma_start(ssm_raw[:, :, :], ssm_mats).then_inc(ssm_loaded, 16)
            order(pool.memset(b_rows[:, :, :], 0.0))
            order(pool.memset(c_rows[:, :, :, :], 0.0))
            pool.wait_ge(ssm_loaded, 16)
            B = [ssm_raw[:, j, :].rearrange("p (s h) -> p s h", h=16) for j in range(4)]
            prod = region(12288, 2, 256)
            pa, pb = [prod[:, j, :].rearrange("p (s h) -> p s h", h=16) for j in range(2)]
            for part, (u, v, op) in enumerate(((B[0], B[1], ALU.subtract), (B[1], B[0], ALU.add))):
                order(pool.tensor_tensor(pa, u, wide(pr(CR), 16), ALU.mult))
                order(pool.tensor_tensor(pb, v, wide(pr(CI), 16), ALU.mult))
                dst = b_rows[:, part, :].rearrange("p (s c) -> p s c", c=32)
                for half in range(2):
                    r, c = slice(64 * half, 64 * half + 64), slice(16 * half, 16 * half + 16)
                    order(pool.tensor_tensor(dst[r, :, c], pa[r, :, :], pb[r, :, :], op))
            pool.sem_inc(b_ready, 1)
            for part, (src, sign) in enumerate(((B[2], 1.0), (B[2], -1.0), (B[3], -1.0))):
                for half in range(2):
                    r, c = slice(64 * half, 64 * half + 64), slice(16 * half, 16 * half + 16)
                    order(pool.tensor_scalar(c_rows[r, part, :, c], src[r, :, :], sign, 1.0,
                                             ALU.mult, ALU.mult))
            rc, rs = rot[:, 0, :, :], rot[:, 1, :, :]
            order(pool.memset(rc[:, :, 0:1], 1.0))
            order(pool.memset(rs[:, :, 0:1], 0.0))
            c1, s1 = pr(COS), pr(SIN)
            w = 1
            while w < SEQ:
                tmp = rot_tmp[:, :, 0:w]
                new = slice(w, 2 * w)
                order(pool.tensor_tensor(rc[:, :, new], rc[:, :, 0:w], wide(c1, w), ALU.mult))
                order(pool.tensor_tensor(tmp, rs[:, :, 0:w], wide(s1, w), ALU.mult))
                order(pool.tensor_tensor(rc[:, :, new], rc[:, :, new], tmp, ALU.subtract))
                order(pool.tensor_tensor(rs[:, :, new], rc[:, :, 0:w], wide(s1, w), ALU.mult))
                order(pool.tensor_tensor(tmp, rs[:, :, 0:w], wide(c1, w), ALU.mult))
                order(pool.tensor_tensor(rs[:, :, new], rs[:, :, new], tmp, ALU.add))
                w *= 2
                if w < SEQ:
                    order(pool.tensor_tensor(pr(T0), c1, c1, ALU.mult))
                    order(pool.tensor_tensor(pr(T1), s1, s1, ALU.mult))
                    order(pool.tensor_tensor(pr(T2), c1, s1, ALU.mult))
                    order(pool.tensor_tensor(pr(DT), pr(T0), pr(T1), ALU.subtract))
                    order(pool.tensor_tensor(pr(XR), pr(T2), pr(T2), ALU.add))
                    order(pool.tensor_copy(pr(LR), pr(DT)))
                    order(pool.tensor_copy(pr(LI), pr(XR)))
                    c1, s1 = pr(LR), pr(LI)
            pool.sem_inc(rot_ready, 1)

        def turn_b_pe(pe):
            pe.wait_ge(b_ready, 1)
            for part in range(2):
                for q in range(4):
                    tr = pe.transpose(bank[6 + part][:, q * P:(q + 1) * P],
                                      b_rows[:, part, q * P:(q + 1) * P], ident[:, :])
                tr.then_inc(b_in_psum, 1)

        def turn_b_act(act):
            for part in range(2):
                act.wait_ge(b_in_psum, part + 1)
                act.activation(b_turned[:, part, :, :].rearrange("p q s -> p (q s)"),
                               bank[6 + part][:, :], ACT.Copy).then_inc(b_evacuated, 1)

        spec_loaded = sem("spec_loaded")
        decay_loaded = sem("decay_loaded")
        mlp_product = sem("mlp_product")
        mlp_arg = sem("mlp_arg")
        mlp_sin = sem("mlp_sin")
        taps_product = sem("taps_product")
        decay_done = sem("decay_done")
        taps_done = sem("taps_done")
        tap_squares = sem("tap_squares")
        tap_sums = sem("tap_sums")
        tap_root = sem("tap_root")
        even_odd = sem("even_odd")
        spec_product = sem("spec_product")
        spec_done = sem("spec_done")
        spectrum_stored = sem("spectrum_stored")
        dft = region(11264, 2, 2, SEQ)
        filter_out = region(14336, 2048)
        taps = region(16384, 4, 512)
        decays = region(18432, MT, 1024)
        eo = region(20480, 4, 512)
        spec = region(22528, 4, 512)
        root = region(24576, 512)
        tap_sq = region(25088, 2, 512)
        decay_rows = region(6144, 1024)
        mlp = region(13312, 1024)
        feat_t, mlp_ws = mlp[0:33, 0:256], mlp[0:64, 256:448]
        mlp_h, mlp_k = mlp[0:64, 448:704], mlp[0:64, 704:960]

        def spectrum_pe(pe):
            pe.wait_ge(spec_loaded, 16 * 5)
            for layer in range(3):
                if layer:
                    pe.wait_ge(mlp_sin, layer)
                    pe.matmul(bank[7][0:64, 0:SEQ], mlp[0:64, 256 + 64 * layer:320 + 64 * layer],
                              mlp_h, start=True, stop=True).then_inc(mlp_product, 1)
                else:
                    pe.matmul(bank[7][0:64, 0:SEQ], mlp[0:33, 256:320], feat_t,
                              start=True, stop=True).then_inc(mlp_product, 1)
            pe.wait_ge(mlp_sin, 3)
            for o in range(2):
                if o:
                    pe.wait_ge(spec_done, 4)
                for q in range(4):
                    m, d = q // 2, q % 2
                    pe.matmul(bank[q][:, :], mlp_h[:, m * P:(m + 1) * P],
                              filter_out[0:64, o * 1024 + d * 512:o * 1024 + d * 512 + 512],
                              start=True, stop=True).then_inc(taps_product, 1)
                for q in range(4):
                    pe.wait_ge(tap_squares, 4 * o + q + 1)
                    pe.matmul(bank[6][:, :], ones[:, :], tap_sq[:, q % 2, :], start=q == 0,
                              stop=q == 3).then_inc(tap_sums, 1)
                pe.wait_ge(even_odd, 4 * o + 4)
                for f in range(2):
                    for s in range(2):
                        for m in range(MT):
                            mm = pe.matmul(bank[2 * f + s][:, :], dft[:, s, m, f * P:(f + 1) * P],
                                           eo[:, 2 * m + s, :], start=m == 0, stop=m == MT - 1)
                        mm.then_inc(spec_product, 1)

        def spectrum_dve(dve, order, spare):
            for layer in range(3):
                dve.wait_ge(mlp_product, layer + 1)
                order(dve.tensor_scalar(mlp_h, bank[7][0:64, 0:SEQ], C[0:64, COLS["mlp_b"][0] + layer:COLS["mlp_b"][0] + layer + 1],
                                        C[0:64, COLS["sin_freq"][0] + layer:COLS["sin_freq"][0] + layer + 1],
                                        ALU.add, ALU.mult))
                round_off(dve, order, mlp_h, mlp_k, 1.0 / TWO_PI, TWO_PI_HI, TWO_PI_LO)
                dve.tensor_scalar(mlp_h, mlp_h, PI_BELOW, -PI_BELOW, ALU.min,
                                  ALU.max).then_inc(mlp_arg, 1)
                spare()
            for o in range(2):
                for q in range(4):
                    m, d = q // 2, q % 2
                    dve.wait_ge(taps_product, 4 * o + q + 1)
                    dve.wait_ge(decay_done, 2 * o + m + 1)
                    ins = dve.tensor_tensor(taps[:, q, :], bank[q][:, :],
                                            decays[:, m, d * 512:d * 512 + 512], ALU.mult)
                    if q == 1:
                        order(ins)
                        ins = dve.memset(taps[0:1, 1, :], 0.0)
                    ins.then_inc(taps_done, 1)
                    if q % 2:
                        spare()
                dve.wait_ge(taps_done, 4 * o + 4)
                for m in range(MT):
                    for s, op in enumerate((ALU.add, ALU.subtract)):
                        dve.tensor_tensor(eo[:, 2 * m + s, :], taps[:, 2 * m, :], taps[:, 2 * m + 1, :],
                                          op).then_inc(even_odd, 1)
                spare()
                dve.wait_ge(tap_root, o + 1)
                order(dve.reciprocal(root, root))
                if o:
                    dve.wait_ge(spectrum_stored, 16)
                for q in range(4):
                    dve.wait_ge(spec_product, 4 * o + q + 1)
                    dve.tensor_tensor(spec[:, q, :], bank[q][:, :], root, ALU.mult).then_inc(spec_done, 1)
                    if q % 2:
                        spare()

        def spectrum_act(act, order):
            for layer in range(3):
                act.wait_ge(mlp_arg, layer + 1)
                then(act, act.activation(mlp_h, mlp_h, ACT.Sin), mlp_sin, layer + 1)
            for o in range(2):
                act.wait_ge(decay_loaded, 16 * (o + 1))
                order(act.activation(decay_rows, decay_rows, ACT.Abs))
                if o:
                    act.wait_ge(taps_done, 4)
                for m in range(MT):
                    at = COLS["neg_t"][0] + m
                    act.activation(decays[:, m, :], decay_rows, ACT.Exp,
                                   scale=C[:, at:at + 1]).then_inc(decay_done, 1)
                if o == 0:
                    act.wait_ge(decay_done, 2)
                    act.dma_start(decay_rows, decay[1:2, :].partition_broadcast(P)).then_inc(decay_loaded, 16)
                for q in range(4):
                    act.wait_ge(taps_done, 4 * o + q + 1)
                    if 4 * o + q >= 2:
                        act.wait_ge(tap_sums, 4 * o + q - 1)
                    act.activation(tap_sq[:, q % 2, :], taps[:, q, :], ACT.Square).then_inc(tap_squares, 1)
                act.wait_ge(tap_sums, 4 * o + 4)
                if o:
                    act.wait_ge(spec_done, 4)
                act.activation(root, bank[6][:, :], ACT.Sqrt).then_inc(tap_root, 1)

        def spectrum_pool(pool):
            for o in range(2):
                pool.wait_ge(spec_done, 4 * o + 4)
                pool.dma_start(spectrum[o], spec[:, :, :]).then_inc(spectrum_stored, 16)
        u_t = region(4096, 4, SEQ)
        q_t = region(5120, 4, SEQ)
        y32 = region(5120, 4, SEQ)
        p_turned = region(6144, 2, 384)
        attn = region(6912, 2, 512)
        rot_in = region(7936, 2, 2, SEQ)
        rot_out = region(8960, 2, 4, SEQ)
        scores = region(0, 8, 384)
        near_sb = region(3072, 384)
        k_t = region(25088, SEQ)
        v_t = region(25344, SEQ)
        v_tok = region(25600, MT, P)
        sink_row = stat[:, 24:32]
        gate_in = region(0, 4, SEQ)
        rms_row = region(1024, SEQ)
        y_squares = region(1280, 2, SEQ)
        max3 = region(11008, 8, 3)
        m1_small = region(11040, 6, 16)
        NEGMAX, SUMS, SINK, RDEN = range(4)

        m1_product = sem("m1_product")
        m1_evac = sem("m1_evac")
        v_turned = sem("v_turned")
        v_ready = sem("v_ready")
        near_loaded = sem("near_loaded")
        sc_product = sem("sc_product")
        sc_biased = sem("sc_biased")
        sc_max = sem("sc_max")
        sc_exp = sem("sc_exp")
        p_in_psum = sem("p_in_psum")
        p_evac = sem("p_evac")
        pv_done = sem("pv_done")
        den_done = sem("den_done")
        attn_done = sem("attn_done")
        attn_squares = sem("attn_squares")
        attn_rstd = sem("attn_rstd")
        attn_scaled = sem("attn_scaled")
        attn_turned = sem("attn_turned")
        m_evac = sem("m_evac")
        m_hi = sem("m_hi")
        m_lo = sem("m_lo")
        bu_done = sem("bu_done")
        bu_read = sem("bu_read")
        states_done = sem("states_done")
        rot_done = sem("rot_done")
        y_done = sem("y_done")
        y_skip = sem("y_skip")
        gelu_done = sem("gelu_done")
        y_hi = sem("y_hi")
        y_lo = sem("y_lo")
        glu_done = sem("glu_done")
        sig_done = sem("sig_done")
        gated = sem("gated")
        gsq_done = sem("gsq_done")
        gsum_done = sem("gsum_done")
        root_done = sem("root_done")
        M1 = FIRST[("mix1", 0)]

        def m1_projection_pe(pe):
            for j in range(10):
                if j >= 2:
                    pe.wait_ge(m1_evac, j - 1)
                channel_product(pe, bank[4 + j % 2][:, 0:SEQ], M1 + j)

        def attention_pe(pe, head):
            kv, j = head // 4, head % 4
            r = slice(64 * kv, 64 * kv + 64)
            b = bank[4 + head % 2]
            if head >= 2:
                pe.wait_ge(sc_biased, head - 1)
            pe.matmul(b[:, 0:P], q_t[r, j, 0:P], k_t[r, 0:P], start=True, stop=True)
            pe.matmul(b[:, P:3 * P], q_t[r, j, P:SEQ], k_t[r, :], start=True,
                      stop=True).then_inc(sc_product, 1)

        def attention_values_pe(pe, head):
            pe.wait_ge(sc_exp, 2 * head + 2)
            b = bank[4 + head % 2]
            if head >= 2:
                pe.wait_ge(p_evac, head - 1)
            for c in range(3):
                tr = pe.transpose(b[:, c * P:(c + 1) * P], scores[:, head, c * P:(c + 1) * P], ident[:, :])
            tr.then_inc(p_in_psum, 1)

        def attention_out_pe(pe, head):
            kv = head // 4
            pe.wait_ge(p_evac, head + 1)
            v = slice(64 * kv, 64 * kv + 64)
            o = slice(64 * head, 64 * head + 64)
            p = p_turned[:, head % 2, :]
            pe.matmul(bank[0][:, o], p[:, 0:P], v_tok[:, 0, v], start=True, stop=True)
            pe.matmul(bank[1][:, o], p[:, P:2 * P], v_tok[:, 0, v], start=True, stop=False)
            pe.matmul(bank[1][:, o], p[:, 2 * P:3 * P], v_tok[:, 1, v], start=False,
                      stop=True).then_inc(pv_done, 1)

        def input_pe(pe, s):
            q, r = s // 4, slice(32 * (s % 4), 32 * (s % 4) + 32)
            if s >= 2:
                pe.wait_ge(bu_read, s - 1)
            for part in range(2):
                mm = pe.matmul(bank[2 + s % 2][:, part * SEQ:(part + 1) * SEQ], b_turned[r, part, q, :],
                               u_t[r, q, :], start=True, stop=True)
            mm.then_inc(bu_done, 1)

        def output_pe(pe, s):
            q, r = s // 4, slice(32 * (s % 4), 32 * (s % 4) + 32)
            pe.wait_ge(rot_done, 2 * s + 2)
            o = bank[6 + q // 2][r, (q % 2) * SEQ:(q % 2 + 1) * SEQ]
            for n, (part, term) in enumerate(((0, 0), (2, 1), (2, 2), (1, 3))):
                mm = pe.matmul(o, c_rows[:, part, s, :], rot_out[:, s % 2, term, :], start=n == 0,
                               stop=n == 3)
            mm.then_inc(y_done, 1)

        def mix1_pe(pe):
            m1_projection_pe(pe)
            pe.wait_ge(m1_evac, 10)
            for m in range(MT):
                tr = pe.transpose(bank[4][:, m * P:(m + 1) * P], v_t[:, m * P:(m + 1) * P], ident[:, :])
            tr.then_inc(v_turned, 1)
            pe.wait_ge(rot_ready, 1)
            input_pe(pe, 0)
            input_pe(pe, 1)
            pe.wait_ge(v_ready, 1)
            for s in range(STATE_TILES):
                if s < 8:
                    attention_pe(pe, s)
                elif s < 12:
                    if s == 8:
                        pe.wait_ge(sc_biased, 8)
                    for head in (2 * s - 16, 2 * s - 15):
                        attention_values_pe(pe, head)
                        if head:
                            attention_out_pe(pe, head - 1)
                elif s == 12:
                    attention_out_pe(pe, 7)
                elif s == 15:
                    turn_attention_pe(pe)
                if s + 2 < STATE_TILES:
                    input_pe(pe, s + 2)
                output_pe(pe, s)
            pe.wait_ge(y_lo, 4)
            pe.wait_ge(bu_read, 16)
            for n in range(4):
                slot_at = M1 + 10 + n // 2
                pe.wait_ge(lo_ready, slot_at + 1)
                mm = channel_product(pe, bank[2 + n // 2][:, (n % 2) * SEQ:(n % 2 + 1) * SEQ], slot_at,
                                     k_tiles=4, at=(n % 2) * 512, k0=4, used=n % 2 == 1)
            for n in range(4):
                pe.wait_ge(gsq_done, n + 1)
                pe.matmul(bank[4][:, 0:SEQ], ones[:, :], y_squares[:, n % 2, :], start=n == 0,
                          stop=n == 3).then_inc(gsum_done, 1)
            for k in range(KT):
                pe.wait_ge(m_lo, k // 2 + 1)
                token_product(pe, M1 + 12 + k, h_hi[:, k, :], h_lo[:, k, :], k == 0, k == KT - 1)

        def turn_attention_pe(pe):
            pe.wait_ge(attn_scaled, 2)
            for k in range(4):
                for m in range(MT):
                    tr = pe.transpose(bank[4 + k // 2][:, (k % 2) * SEQ + m * P:(k % 2) * SEQ + m * P + P],
                                      attn[:, m, k * P:(k + 1) * P], ident[:, :])
                if k % 2:
                    tr.then_inc(attn_turned, 1)

        def mix1_act(act, order):
            for j in range(10):
                split_hi(act, M1 + 3 + j)
                act.wait_ge(panel_used, M1 + j + 1)
                src = bank[4 + j % 2][:, 0:SEQ]
                if j < 4:
                    ins = act.activation(u_t[:, j, :], src, ACT.Copy)
                elif j < 8:
                    ins = act.activation(q_t[:, j - 4, :], src, ACT.Copy, scale=HD ** -0.5)
                else:
                    ins = act.activation(k_t if j == 8 else v_t, src, ACT.Copy)
                ins.then_inc(m1_evac, 1)
            act_panels(act, M1 + 13, 3)
            act.wait_ge(v_turned, 1)
            act.activation(v_tok[:, :, :].rearrange("p m c -> p (m c)"), bank[4][:, 0:SEQ],
                           ACT.Copy).then_inc(v_ready, 1)
            act.wait_ge(sc_max, 3)
            order(act.activation(m1_small[:, SINK, :], m1_small[:, SINK, :], ACT.Exp))
            for head in range(8):
                for b, c in ((0, slice(0, P)), (1, slice(P, 3 * P))):
                    i = 2 * head + b
                    act.activation(scores[:, head, c], scores[:, head, c], ACT.Exp,
                                   bias=m1_small[:, NEGMAX, i:i + 1],
                                   accum_out=m1_small[:, SUMS, i:i + 1]).then_inc(sc_exp, 1)
            for head in range(8):
                act.wait_ge(p_in_psum, head + 1)
                if head >= 2:
                    act.wait_ge(pv_done, head - 1)
                act.activation(p_turned[:, head % 2, :], bank[4 + head % 2][:, 0:384],
                               ACT.Copy).then_inc(p_evac, 1)
            for m in range(MT):
                act.wait_ge(attn_done, m + 1)
                act.activation(region(1024 * m, 512), attn[:, m, :], ACT.Square,
                               accum_out=stat[:, 32 + m:33 + m]).then_inc(attn_squares, 1)
            for k in range(4):
                act.wait_ge(attn_turned, k // 2 + 1)
                act.activation(h32[:, k, :], bank[4 + k // 2][:, (k % 2) * SEQ:(k % 2 + 1) * SEQ],
                               ACT.Copy, scale=col("g_attn", k)).then_inc(m_evac, 1)
            for b in range(2):
                act.wait_ge(m_evac, 2 * b + 2)
                act.activation(h_hi[:, 2 * b:2 * b + 2, :], h32[:, 2 * b:2 * b + 2, :],
                               ACT.Copy).then_inc(m_hi, 1)
            for b in range(2):
                act.wait_ge(y_skip, 2 * b + 2)
                r = slice(2 * b, 2 * b + 2)
                then(act, act.activation(y32[:, r, :], y32[:, r, :], ACT.Gelu_apprx_tanh), gelu_done, b + 1)
                act.activation(h_hi[:, 4 + 2 * b:6 + 2 * b, :], y32[:, r, :], ACT.Copy).then_inc(y_hi, 1)
            for n in range(4):
                act.wait_ge(panel_used, M1 + 11 + n // 2)
                act.activation(gate_in[:, n, :], bank[2 + n // 2][:, (n % 2) * SEQ:(n % 2 + 1) * SEQ],
                               ACT.Sigmoid, bias=col("b_glu", n)).then_inc(sig_done, 1)
            act_panels(act, M1 + 16, 2)
            for n in range(4):
                act.wait_ge(gated, n + 1)
                if n >= 2:
                    act.wait_ge(gsum_done, n - 1)
                act.activation(y_squares[:, n % 2, :], gate_in[:, n, :], ACT.Square).then_inc(gsq_done, 1)
            act.wait_ge(gsum_done, 4)
            order(act.activation(rms_row, bank[4][:, 0:SEQ], ACT.Copy, scale=1.0 / 512, bias=EPS))
            act.activation(rms_row, rms_row, ACT.Sqrt).then_inc(root_done, 1)
            for b in range(2, 4):
                act.wait_ge(m_evac, 2 * b + 2)
                act.activation(h_hi[:, 2 * b:2 * b + 2, :], h32[:, 2 * b:2 * b + 2, :],
                               ACT.Copy).then_inc(m_hi, 1)
            act_panels(act, M1 + 18, 5)

        def mix1_pool(pool, order):
            pool.wait_ge(x_done, 4)
            pool.dma_start(sink_row, sinks.partition_broadcast(P)).then_inc(near_loaded, 16)
            pool.wait_ge(h_lo_done, 4 * 1 + 4)
            pool.dma_start(near_sb, near).then_inc(near_loaded, 16)
            for s in range(STATE_TILES):
                pool.wait_ge(states_done, 2 * s + 2)
                if s >= 2:
                    pool.wait_ge(y_done, s - 1)
                z = rot_in[:, 1, :, :]
                for part in range(2):
                    r = rot[:, part, s, :].unsqueeze(1).to_broadcast([P, 2, SEQ])
                    pool.tensor_tensor(rot_out[:, s % 2, 2 * part:2 * part + 2, :], z, r,
                                       ALU.mult).then_inc(rot_done, 1)
                if s == 13:
                    for m in range(MT):
                        pool.wait_ge(attn_squares, m + 1)
                        ss = stat[:, 32 + m:33 + m]
                        order(pool.tensor_scalar(ss, ss, 1.0 / 512, EPS, ALU.mult, ALU.add))
                        pool.tensor_tensor(ss, ss, stat[:, MINUS_HALF:MINUS_HALF + 1],
                                           ALU.pow).then_inc(attn_rstd, 1)

        def states_dve(dve, order, s):
            w = bank[2 + s % 2]
            re, im = w[:, 0:SEQ], w[:, SEQ:2 * SEQ]
            c, sn = rot[:, 0, s, :], rot[:, 1, s, :]
            a, x = rot_in[:, 0, :, :], rot_in[:, 1, :, :]
            dve.wait_ge(bu_done, s + 1)
            if s:
                dve.wait_ge(rot_done, 2 * s)
            order(dve.tensor_tensor(a[:, 0, :], re, c, ALU.mult))
            order(dve.tensor_tensor(a[:, 1, :], im, c, ALU.mult))
            order(dve.tensor_tensor(x[:, 0, :], im, sn, ALU.mult))
            then(dve, dve.tensor_tensor(x[:, 1, :], re, sn, ALU.mult), bu_read, s + 1)
            order(dve.tensor_tensor(a[:, 0, :], a[:, 0, :], x[:, 0, :], ALU.add))
            order(dve.tensor_tensor(a[:, 1, :], a[:, 1, :], x[:, 1, :], ALU.subtract))
            r = par[:, RAD, s:s + 1].to_broadcast([P, SEQ])
            for part in range(2):
                dve.tensor_tensor_scan(x[:, part, :], r, a[:, part, :], 0.0, ALU.mult,
                                       ALU.add).then_inc(states_done, 1)

        def mix1_dve(dve, order):
            dve_panels(dve, M1 + 3, 13)
            dve.wait_ge(near_loaded, 32)
            dve.wait_ge(rot_ready, 1)

            def bias(head):
                dve.wait_ge(sc_product, head + 1)
                then(dve, dve.scalar_tensor_tensor(out=scores[:, head, :], in0=near_sb,
                                                   scalar=2.0 ** -(head + 1),
                                                   in1=bank[4 + head % 2][:, 0:384], op0=ALU.mult,
                                                   op1=ALU.add), sc_biased, head + 1)
                order(dve.tensor_reduce(max3[:, head, :],
                                        scores[:, head, :].rearrange("p (b k) -> p b k", b=3),
                                        AX.X, ALU.max))

            def maxima():
                mx = m1_small[:, NEGMAX, :].rearrange("p (h b) -> p h b", b=2)
                sx = m1_small[:, SINK, :].rearrange("p (h b) -> p h b", b=2)
                order(dve.tensor_tensor(max3[:, :, 1], max3[:, :, 1], max3[:, :, 2], ALU.max))
                for b in range(2):
                    order(dve.tensor_tensor(mx[:, :, b], max3[:, :, b], sink_row, ALU.max))
                for b in range(2):
                    dve.tensor_tensor(sx[:, :, b], sink_row, mx[:, :, b], ALU.subtract).then_inc(sc_max, 1)
                dve.wait_ge(sc_max, 2)
                dve.tensor_scalar(m1_small[:, NEGMAX, :], m1_small[:, NEGMAX, :], -1.0, None,
                                  ALU.mult).then_inc(sc_max, 1)

            def attention_out():
                dve.wait_ge(sc_exp, 16)
                order(dve.tensor_tensor(m1_small[:, RDEN, :], m1_small[:, SUMS, :], m1_small[:, SINK, :],
                                        ALU.add))
                order(dve.reciprocal(m1_small[:, RDEN, :], m1_small[:, RDEN, :]))
                dve.wait_ge(pv_done, 8)
                rd = m1_small[:, RDEN, :].rearrange("p (h b) -> p h b", b=2)
                for b in range(2):
                    r = rd[:, :, b].unsqueeze(2).to_broadcast([P, 8, HD])
                    dve.tensor_tensor(attn[:, b, :].rearrange("p (h d) -> p h d", d=HD),
                                      bank[b][:, :].rearrange("p (h d) -> p h d", d=HD), r,
                                      ALU.mult).then_inc(attn_done, 1)

            def skip(b):
                dve.wait_ge(y_done, 8 * b + 8)
                if b == 0:
                    dve.wait_ge(sc_product, 8)
                for j in range(2):
                    q = 2 * b + j
                    dve.scalar_tensor_tensor(out=y32[:, q, :], in0=u_t[:, q, :], scalar=col("ssm_d", q),
                                             in1=bank[6 + b][:, j * SEQ:(j + 1) * SEQ], op0=ALU.mult,
                                             op1=ALU.add).then_inc(y_skip, 1)

            for s in range(STATE_TILES):
                states_dve(dve, order, s)
                if s < 8:
                    bias(s)
                    if s == 7:
                        maxima()
                if s == 12:
                    attention_out()
                if s == 13:
                    skip(0)
                if s == 14:
                    for m in range(MT):
                        dve.wait_ge(attn_rstd, m + 1)
                        dve.tensor_scalar(attn[:, m, :], attn[:, m, :], stat[:, 32 + m:33 + m], None,
                                          ALU.mult).then_inc(attn_scaled, 1)
            skip(1)
            for b in range(2):
                dve.wait_ge(m_hi, b + 1)
                r = slice(2 * b, 2 * b + 2)
                dve.tensor_tensor(h_lo[:, r, :], h32[:, r, :], h_hi[:, r, :].bitcast(F32),
                                  ALU.subtract).then_inc(m_lo, 1)
            for b in range(2):
                for j in range(2):
                    dve.wait_ge(y_hi, b + 1)
                    k = 4 + 2 * b + j
                    dve.tensor_tensor(h_lo[:, k, :], y32[:, 2 * b + j, :], h_hi[:, k, :].bitcast(F32),
                                      ALU.subtract).then_inc(y_lo, 1)
            for n in range(4):
                dve.wait_ge(sig_done, n + 1)
                dve.tensor_tensor(gate_in[:, n, :], gate_in[:, n, :], y32[:, n, :],
                                  ALU.mult).then_inc(gated, 1)
            dve_panels(dve, M1 + 16, 2)
            dve.wait_ge(root_done, 1)
            order(dve.reciprocal(rms_row, rms_row))
            for n in range(4):
                dve.scalar_tensor_tensor(out=h32[:, 4 + n, :], in0=gate_in[:, n, :],
                                         scalar=col("g_ssm", n), in1=rms_row, op0=ALU.mult,
                                         op1=ALU.mult).then_inc(m_evac, 1)
            for b in range(2, 4):
                dve.wait_ge(m_hi, b + 1)
                r = slice(2 * b, 2 * b + 2)
                dve.tensor_tensor(h_lo[:, r, :], h32[:, r, :], h_hi[:, r, :].bitcast(F32),
                                  ALU.subtract).then_inc(m_lo, 1)
            dve_panels(dve, M1 + 18, 5)

        forward = region(4096, 2, MT, SEQ)
        inverse = region(5120, 2, MT, SEQ)
        averages = region(6144, 4 * MT, SEQ)
        pool_ws = region(8192, 4, P)
        filters = region(8704, 8, 512)
        a_tok = region(12800, MT, 512)
        averaged = region(13824, 4, SEQ)
        conv = region(14848, 12, SEQ)
        z_tok = region(17920, MT, 512)
        product = region(18944, 4, 512)
        terms = region(20992, 4, 512)
        z_sum = region(23040, 2, SEQ)

        m2_loaded = sem("m2_loaded")
        a_evac = sem("a_evac")
        conv_centre = sem("conv_centre")
        conv_done = sem("conv_done")
        averages_done = sem("averages_done")
        averages_evac = sem("averages_evac")
        grouped_done = sem("grouped_done")
        z_turned = sem("z_turned")
        z_evac = sem("z_evac")
        z_spectrum = sem("z_spectrum")
        spectra_product = sem("spectra_product")
        z_back = sem("z_back")
        z_done = sem("z_done")
        m2_evac = sem("m2_evac")
        m2_hi = sem("m2_hi")
        m2_lo = sem("m2_lo")
        M2 = FIRST[("mix2", 0)]

        def mix2_loads(pool):
            pool.wait_ge(x_done, 12)
            pool.dma_start(forward, pool_mats[4:6].rearrange("i p m t -> p i m t")).then_inc(m2_loaded, 16)
            pool.dma_start(inverse, pool_mats[6:8].rearrange("i p m t -> p i m t")).then_inc(m2_loaded, 16)
            pool.dma_start(averages.rearrange("p (i m) t -> p i m t", m=MT),
                           pool_mats[0:4].rearrange("i p m t -> p i m t")).then_inc(m2_loaded, 16)
            pool.dma_start(pool_ws, pool_w).then_inc(m2_loaded, 16)
            pool.dma_start(filters.rearrange("p (o q) c -> p o q c", o=2),
                           spectrum.rearrange("o p q c -> p o q c")).then_inc(m2_loaded, 16)

        def forward_pe(pe, first_bank, o):
            pe.wait_ge(z_evac, MT * (o + 1))
            for f in range(2):
                for s in range(2):
                    for m in range(MT):
                        mm = pe.matmul(bank[first_bank + 2 * f + s][:, :],
                                       forward[:, s, m, f * P:(f + 1) * P], z_tok[:, m, :],
                                       start=m == 0, stop=m == MT - 1)
                    mm.then_inc(z_spectrum, 1)

        def inverse_pe(pe, o):
            pe.wait_ge(spectra_product, 4 * o + 4)
            for c in range(4):
                for f in range(2):
                    for s in range(2):
                        mm = pe.matmul(bank[6 + c // 2][:, (c % 2) * SEQ:(c % 2 + 1) * SEQ],
                                       product[:, 2 * f + s, c * P:(c + 1) * P], inverse[:, s, f, :],
                                       start=f + s == 0, stop=f + s == 2)
                mm.then_inc(z_back, 1)

        def turn_z_pe(pe, first_bank):
            for m in range(MT):
                for c in range(4):
                    tr = pe.transpose(bank[first_bank + m][:, c * P:(c + 1) * P],
                                      conv[:, c, m * P:(m + 1) * P], ident[:, :])
                tr.then_inc(z_turned, 1)

        def mix2_pe(pe):
            for j in range(4):
                g = M2 + j
                pe.wait_ge(lo_ready, g + 1)
                for half in range(2):
                    k, w = 2 * j + half, slice(512 * half, 512 * half + 512)
                    for m in range(MT):
                        t = slice(m * P, (m + 1) * P)
                        mm = product3(pe, bank[m][:, :], w_hi[:, g % RING, w], w_lo[:, g % RING, w],
                                      h_hi[:, k, t], h_lo[:, k, t], k == 0, k == KT - 1,
                                      weights_move=True)
                mm.then_inc(panel_used, 1)

            def parts(lo, hi):
                for j in range(lo, hi):
                    if j >= 2:
                        pe.wait_ge(conv_done, j - 1)
                    channel_product(pe, bank[4 + j % 2][:, 0:SEQ], M2 + 4 + j)

            parts(0, 4)
            pe.wait_ge(m2_loaded, 16 * 5)
            pe.wait_ge(a_evac, 2)
            for g in range(4):
                for m in range(MT):
                    mm = pe.matmul(bank[6 + g // 2][:, (g % 2) * SEQ:(g % 2 + 1) * SEQ],
                                   a_tok[:, m, g * P:(g + 1) * P], averages[:, MT * g + m, :],
                                   start=m == 0, stop=m == MT - 1)
                if g % 2:
                    mm.then_inc(averages_done, 1)
            parts(4, 6)
            turn_z_pe(pe, 2)
            parts(6, 8)
            for g in range(4):
                if g % 2 == 0:
                    pe.wait_ge(averages_evac, g // 2 + 1)
                mm = pe.matmul(bank[6 + g // 2][:, (g % 2) * SEQ:(g % 2 + 1) * SEQ], pool_ws[:, g, :],
                               averaged[:, g, :], start=True, stop=True)
                if g % 2:
                    mm.then_inc(grouped_done, 1)
            forward_pe(pe, 0, 0)
            parts(8, 12)
            pe.wait_ge(m2_evac, 4)
            inverse_pe(pe, 0)
            pe.wait_ge(conv_done, 12)
            pe.wait_ge(z_done, 4)
            turn_z_pe(pe, 4)
            forward_pe(pe, 4, 1)
            for k in range(KT):
                if k == 4:
                    inverse_pe(pe, 1)
                pe.wait_ge(m2_lo, k // 2 + 1)
                token_product(pe, M2 + 16 + k, h_hi[:, k, :], h_lo[:, k, :], k == 0, k == KT - 1)

        def mix2_act(act, order):
            def centre(j):
                act.wait_ge(panel_used, M2 + 5 + j)
                tile = (j + 8) % 12
                act.activation(conv[:, j, :], bank[4 + j % 2][:, 0:SEQ], ACT.Identity,
                               scale=col("conv_w", 12 + tile),
                               bias=col("conv_b", tile)).then_inc(conv_centre, 1)

            def evac_z(first_bank, n):
                for m in range(MT):
                    act.wait_ge(z_turned, n + m + 1)
                    act.activation(z_tok[:, m, :], bank[first_bank + m][:, :], ACT.Copy).then_inc(z_evac, 1)

            def high(b):
                r = slice(2 * b, 2 * b + 2)
                act.activation(h_hi[:, r, :], h32[:, r, :], ACT.Copy).then_inc(m2_hi, 1)

            act_panels(act, M2 + 3, 4)
            act.wait_ge(panel_used, M2 + 4)
            for m in range(MT):
                act.activation(a_tok[:, m, :], bank[m][:, :], ACT.Copy).then_inc(a_evac, 1)
            for j in range(12):
                split_hi(act, M2 + 7 + j)
                centre(j)
                if j == 4:
                    for b in range(2):
                        act.wait_ge(averages_done, b + 1)
                        act.activation(averaged[:, 2 * b:2 * b + 2, :].rearrange("p g t -> p (g t)"),
                                       bank[6 + b][:, :], ACT.Copy).then_inc(averages_evac, 1)
                if j == 6:
                    evac_z(2, 0)
            for g in range(4):
                act.wait_ge(grouped_done, g // 2 + 1)
                act.activation(h32[:, g, :], bank[6 + g // 2][:, (g % 2) * SEQ:(g % 2 + 1) * SEQ],
                               ACT.Copy, scale=col("pool_scale", g)).then_inc(m2_evac, 1)
            act_panels(act, M2 + 19, 3)
            for b in range(2):
                act.wait_ge(m2_evac, 2 * b + 2)
                high(b)
            evac_z(4, 2)
            act_panels(act, M2 + 22, 4)
            for b in range(2, 4):
                act.wait_ge(z_done, 2 * b + 2)
                high(b)
            act_panels(act, M2 + 26, 1)

        def mix2_dve(dve, order):
            def taps_of(j):
                dve.wait_ge(conv_centre, j + 1)
                tile = (j + 8) % 12
                src, dst = bank[4 + j % 2], conv[:, j, :]
                order(dve.scalar_tensor_tensor(out=dst[:, 1:SEQ], in0=src[:, 0:SEQ - 1],
                                               scalar=col("conv_w", tile), in1=dst[:, 1:SEQ],
                                               op0=ALU.mult, op1=ALU.add))
                then(dve, dve.scalar_tensor_tensor(out=dst[:, 0:SEQ - 1], in0=src[:, 1:SEQ],
                                                   scalar=col("conv_w", 24 + tile),
                                                   in1=dst[:, 0:SEQ - 1], op0=ALU.mult, op1=ALU.add),
                     conv_done, j + 1)

            def multiply(o, first_bank, f):
                k = filters[:, 4 * o + 2 * f:4 * o + 2 * f + 2, :]
                for s in range(2):
                    dve.wait_ge(z_spectrum, 4 * o + 2 * f + s + 1)
                    z = bank[first_bank + 2 * f + s][:, :].unsqueeze(1).to_broadcast([P, 2, 512])
                    order(dve.tensor_tensor(terms[:, 2 * s:2 * s + 2, :], k, z, ALU.mult))
                dve.tensor_tensor(product[:, 2 * f, :], terms[:, 0, :], terms[:, 3, :],
                                  ALU.subtract).then_inc(spectra_product, 1)
                then(dve, dve.tensor_tensor(product[:, 2 * f + 1, :], terms[:, 1, :], terms[:, 2, :],
                                            ALU.add), spectra_product, 4 * o + 2 * f + 2)

            def gate(o):
                for c in range(4):
                    dve.wait_ge(z_back, 4 * o + c - c % 2 + 2)
                    order(dve.scalar_tensor_tensor(out=z_sum[:, c % 2, :], in0=conv[:, c, :],
                                                   scalar=col("bias", 4 * o + c),
                                                   in1=bank[6 + c // 2][:, (c % 2) * SEQ:(c % 2 + 1) * SEQ],
                                                   op0=ALU.mult, op1=ALU.add))
                    then(dve, dve.tensor_tensor(h32[:, 4 + c, :] if o else conv[:, c, :],
                                                z_sum[:, c % 2, :], conv[:, 4 + 4 * o + c, :],
                                                ALU.mult), z_done, 4 * o + c + 1)

            def low(b):
                dve.wait_ge(m2_hi, b + 1)
                r = slice(2 * b, 2 * b + 2)
                dve.tensor_tensor(h_lo[:, r, :], h32[:, r, :], h_hi[:, r, :].bitcast(F32),
                                  ALU.subtract).then_inc(m2_lo, 1)

            dve_panels(dve, M2 + 3, 4)
            for j in range(8):
                split_lo(dve, M2 + 7 + j)
                taps_of(j)
            dve.wait_ge(m2_loaded, 16 * 5)
            for f in range(2):
                multiply(0, 0, f)
                for j in (8 + 2 * f, 9 + 2 * f):
                    split_lo(dve, M2 + 7 + j)
                    taps_of(j)
            gate(0)
            dve_panels(dve, M2 + 19, 3)
            low(0)
            low(1)
            for f in range(2):
                multiply(1, 4, f)
            dve_panels(dve, M2 + 22, 4)
            gate(1)
            low(2)
            low(3)
            dve_panels(dve, M2 + 26, 1)

        QK = 96
        SCALE = QK ** -0.5
        q_rows = region(4096, MLA_HEADS, SEQ)
        k_rows = region(8192, MLA_HEADS, SEQ)
        values = region(12288, MT, D)
        probs = region(14336, 2, 512)
        probs_by_key = region(15360, 2, 512)
        attended = region(16384, MT, D)
        rope_t = region(18432, 2, SEQ)
        latent = region(18944, 3, SEQ)
        latent_sq = region(19712, 3, SEQ)
        latent_rms = region(20480, 2, SEQ)
        k_turn = region(20992, 2, SEQ)
        q_turn = region(21504, 2, 4, SEQ)
        soft = region(23552, 4, 2 * MLA_HEADS)
        MAX3, NEG3, SUM3, REC3 = range(4)

        rope_loaded = sem("rope_loaded")
        latent_squares = sem("latent_squares")
        latent_sums = sem("latent_sums")
        latent_root = sem("latent_root")
        latent_done = sem("latent_done")
        latent_hi = sem("latent_hi")
        latent_lo = sem("latent_lo")
        k_rope_done = sem("k_rope_done")
        q_evac = sem("q_evac")
        q_rope_read = sem("q_rope_read")
        q_rope_done = sem("q_rope_done")
        kv_act = sem("kv_act")
        kv_dve = sem("kv_dve")
        scored = sem("scored")
        soft_max = sem("soft_max")
        soft_exp = sem("soft_exp")
        probs_turned = sem("probs_turned")
        probs_evac = sem("probs_evac")
        head_done = sem("head_done")
        divided = sem("divided")
        attended_turned = sem("attended_turned")
        m3_hi = sem("m3_hi")
        m3_lo = sem("m3_lo")
        M3 = FIRST[("mix3", 0)]

        def mix3_loads(pool):
            pool.wait_ge(x_done, 20)
            pool.dma_start(rope_t, rope).then_inc(rope_loaded, 16)

        def mix3_pe(pe):
            for j in range(4):
                channel_product(pe, bank[(0, 0, 1, 2)[j]][:, SEQ * (j == 1):SEQ * (j == 1) + SEQ], M3 + j)
            for n in range(3):
                pe.wait_ge(latent_squares, 1 + n // 2)
                mm = pe.matmul(bank[3][:, SEQ * (n // 2):SEQ * (n // 2) + SEQ], ones[:, :],
                               latent_sq[:, n, :], start=n != 1, stop=n != 0)
            mm.then_inc(latent_sums, 1)
            pe.wait_ge(latent_lo, 1)
            for n in range(8):
                channel_product(pe, bank[4 + n // 2][:, SEQ * (n % 2):SEQ * (n % 2) + SEQ],
                                M3 + 4 + n // 4, k_tiles=2, at=256 * (n % 4), used=n % 4 == 3)
            pe.wait_ge(k_rope_done, 1)
            for n in range(8):
                channel_product(pe, bank[n // 2][:, SEQ * (n % 2):SEQ * (n % 2) + SEQ],
                                M3 + 6 + n // 4, k_tiles=2, at=256 * (n % 4), used=n % 4 == 3)
            for n in range(8):
                if n % 2 == 0:
                    pe.wait_ge(q_evac, n // 2 + 1)
                channel_product(pe, bank[4 + n // 2][:, SEQ * (n % 2):SEQ * (n % 2) + SEQ],
                                M3 + 8, k_tiles=1, at=P * n, k0=2, used=n == 7)
            pe.wait_ge(q_rope_read, 1)
            token_product(pe, M3 + 9, h_hi[:, 2, :], h_lo[:, 2, :], True, True)

            def score(h):
                if h >= 2:
                    pe.wait_ge(soft_exp, 2 * h - 2)
                for m in range(MT):
                    mm = pe.matmul(bank[4 + h % 2][:, SEQ * m:SEQ * m + SEQ],
                                   q_rows[0:QK, h, P * m:P * m + P], k_rows[0:QK, h, :],
                                   start=True, stop=True)
                mm.then_inc(scored, 1)

            def turn(h):
                pe.wait_ge(soft_exp, 2 * h + 2)
                if h >= 2:
                    pe.wait_ge(probs_evac, h - 1)
                for m in range(MT):
                    for c in range(MT):
                        tr = pe.transpose(bank[6 + h % 2][:, SEQ * c + P * m:SEQ * c + P * m + P],
                                          probs[:, h % 2, SEQ * m + P * c:SEQ * m + P * c + P], ident[:, :])
                tr.then_inc(probs_turned, 1)

            def weigh(h):
                pe.wait_ge(probs_evac, h + 1)
                for m in range(MT):
                    for c in range(MT):
                        mm = pe.matmul(bank[2 * m + h // 8][:, 64 * (h % 8):64 * (h % 8) + 64],
                                       probs_by_key[:, h % 2, SEQ * c + P * m:SEQ * c + P * m + P],
                                       values[:, c, 64 * h:64 * h + 64], start=c == 0, stop=c == 1)
                mm.then_inc(head_done, 1)

            pe.wait_ge(q_rope_done, 4)
            pe.wait_ge(kv_act, 4)
            pe.wait_ge(kv_dve, 4)
            score(0)
            score(1)
            for h in range(MLA_HEADS):
                turn(h)
                if h + 2 < MLA_HEADS:
                    score(h + 2)
                if h:
                    weigh(h - 1)
            weigh(MLA_HEADS - 1)
            for b in range(4):
                pe.wait_ge(divided, 2 + b // 2 * 2)
                for j in range(2):
                    for m in range(MT):
                        tr = pe.transpose(bank[4 + b][:, j * SEQ + m * P:j * SEQ + (m + 1) * P],
                                          attended[:, m, (2 * b + j) * P:(2 * b + j + 1) * P], ident[:, :])
                tr.then_inc(attended_turned, 1)
            pe.wait_ge(divided, 4)
            for k in range(KT):
                pe.wait_ge(m3_lo, k // 2 + 1)
                token_product(pe, M3 + 10 + k, h_hi[:, k, :], h_lo[:, k, :], k == 0, k == KT - 1)

        def by_head(rows, b, odd):
            return rows[0:64, 4 * b + odd:4 * b + odd + 3:2, :]

        def of_bank(b, odd):
            return bank[4 + b][64 * odd:64 * odd + 64, :].rearrange("p (t q) -> p t q", t=2)

        def mix3_act(act, order):
            act_panels(act, M3 + 3, 3)
            act.wait_ge(panel_used, M3 + 2)
            act.activation(latent_sq[:, 0:2, :].rearrange("p t q -> p (t q)"), bank[0][:, :],
                           ACT.Square).then_inc(latent_squares, 1)
            act.wait_ge(panel_used, M3 + 3)
            act.activation(latent_sq[:, 2, :], bank[1][:, 0:SEQ], ACT.Square).then_inc(latent_squares, 1)
            act.wait_ge(latent_sums, 1)
            for n, width in enumerate((256, 128)):
                order(act.activation(latent_rms[:, n, :], bank[3][:, SEQ * n:SEQ * n + SEQ], ACT.Copy,
                                     scale=1.0 / width, bias=EPS))
            act.activation(latent_rms[:, :, :], latent_rms[:, :, :], ACT.Sqrt).then_inc(latent_root, 1)
            act.wait_ge(latent_done, 3)
            act.activation(h_hi[:, 0:3, :], latent[:, :, :], ACT.Copy).then_inc(latent_hi, 1)
            act_panels(act, M3 + 6, 4)
            for b in range(4):
                act.wait_ge(panel_used, M3 + 5 + b // 2)
                order(act.activation(by_head(q_rows, b, 0), of_bank(b, 0), ACT.Copy))
                act.activation(by_head(q_rows, b, 1), of_bank(b, 1), ACT.Copy).then_inc(q_evac, 1)
            act.wait_ge(panel_used, M3 + 9)
            for b in range(2):
                for odd in range(2):
                    ins = act.activation(by_head(k_rows, b, odd), of_bank(b, odd), ACT.Copy)
                    if odd:
                        ins.then_inc(kv_act, 1)
                    else:
                        order(ins)
            act.wait_ge(panel_used, M3 + 10)
            for half in range(2):
                act.activation(values[:, 0, 512 * half:512 * half + 512], bank[half][:, :],
                               ACT.Copy).then_inc(kv_act, 1)
            for h in range(MLA_HEADS):
                act.wait_ge(soft_max, h + 1)
                if h >= 2:
                    act.wait_ge(probs_turned, h - 1)
                for m in range(MT):
                    i = 2 * h + m
                    act.activation(probs[:, h % 2, SEQ * m:SEQ * m + SEQ],
                                   bank[4 + h % 2][:, SEQ * m:SEQ * m + SEQ], ACT.Exp, scale=SCALE,
                                   bias=soft[:, NEG3, i:i + 1],
                                   accum_out=soft[:, SUM3, i:i + 1]).then_inc(soft_exp, 1)
                if h % 2 == 1 and h < 12:
                    split_hi(act, M3 + 10 + h // 2)
            for b in range(4):
                act.wait_ge(attended_turned, b + 1)
                act.activation(h_hi[:, 2 * b:2 * b + 2, :].rearrange("p k t -> p (k t)"),
                               bank[4 + b][:, :], ACT.Copy).then_inc(m3_hi, 1)
            act_panels(act, M3 + 16, 5)

        def mix3_dve(dve, order):
            cos, sin = rope_t[:, 0, :], rope_t[:, 1, :]
            dve_panels(dve, M3 + 3, 3)
            dve.wait_ge(rope_loaded, 16)
            dve.wait_ge(panel_used, M3 + 4)
            r, s = slice(64, 96), slice(96, 128)
            order(dve.tensor_tensor(k_turn[r, 0, :], bank[2][r, 0:SEQ], cos[r, :], ALU.mult))
            order(dve.tensor_tensor(k_turn[r, 1, :], bank[2][s, 0:SEQ], sin[s, :], ALU.mult))
            order(dve.tensor_tensor(k_turn[r, 0, :], k_turn[r, 0, :], k_turn[r, 1, :], ALU.add))
            dve.tensor_copy(k_rows[r, :, :], k_turn[r, 0, :].unsqueeze(1).to_broadcast(
                [32, MLA_HEADS, SEQ])).then_inc(k_rope_done, 1)
            dve.wait_ge(latent_root, 1)
            order(dve.reciprocal(latent_rms[:, :, :], latent_rms[:, :, :]))
            for n in range(3):
                dve.scalar_tensor_tensor(out=latent[:, n, :],
                                         in0=bank[n // 2][:, SEQ * (n % 2):SEQ * (n % 2) + SEQ],
                                         scalar=col("q_g", n) if n < 2 else col("kv_g"),
                                         in1=latent_rms[:, n // 2, :], op0=ALU.mult,
                                         op1=ALU.mult).then_inc(latent_done, 1)
            dve.wait_ge(latent_hi, 1)
            dve.tensor_tensor(h_lo[:, 0:3, :], latent[:, :, :], h_hi[:, 0:3, :].bitcast(F32),
                              ALU.subtract).then_inc(latent_lo, 1)
            dve_panels(dve, M3 + 6, 4)
            dve.wait_ge(panel_used, M3 + 8)
            for part, table in enumerate((cos, sin)):
                for b in range(2):
                    ins = dve.tensor_tensor(q_turn[:, part, 2 * b:2 * b + 2, :],
                                            bank[2 * part + b][:, :].rearrange("p (t q) -> p t q", t=2),
                                            table.unsqueeze(1).to_broadcast([P, 2, SEQ]), ALU.mult)
                    order(ins)
            dve.sem_inc(q_rope_read, 1)
            for j in range(4):
                rows = slice(32 * j, 32 * j + 32)
                dve.tensor_tensor(q_rows[64:96, j::4, :], q_turn[rows, 0, :, :], q_turn[rows, 1, :, :],
                                  ALU.add).then_inc(q_rope_done, 1)
            dve.wait_ge(panel_used, M3 + 9)
            for b in range(2, 4):
                for odd in range(2):
                    ins = dve.tensor_copy(by_head(k_rows, b, odd), of_bank(b, odd))
                    if odd:
                        ins.then_inc(kv_dve, 1)
                    else:
                        order(ins)
            dve.wait_ge(panel_used, M3 + 10)
            for half in range(2):
                dve.tensor_copy(values[:, 1, 512 * half:512 * half + 512],
                                bank[2 + half][:, :]).then_inc(kv_dve, 1)

            def turned_probs(h):
                dve.wait_ge(probs_turned, h + 1)
                if h >= 2:
                    dve.wait_ge(head_done, h - 1)
                dve.tensor_copy(probs_by_key[:, h % 2, :], bank[6 + h % 2][:, :]).then_inc(probs_evac, 1)

            for h in range(MLA_HEADS):
                dve.wait_ge(scored, h + 1)
                order(dve.tensor_reduce(soft[:, MAX3, 2 * h:2 * h + 2],
                                        bank[4 + h % 2][:, :].rearrange("p (m k) -> p m k", m=2),
                                        AX.X, ALU.max))
                dve.tensor_scalar(soft[:, NEG3, 2 * h:2 * h + 2], soft[:, MAX3, 2 * h:2 * h + 2],
                                  -SCALE, None, ALU.mult).then_inc(soft_max, 1)
                if h:
                    turned_probs(h - 1)
                if h % 2 == 1 and h < 12:
                    split_lo(dve, M3 + 10 + h // 2)
            turned_probs(MLA_HEADS - 1)
            dve.wait_ge(soft_exp, 2 * MLA_HEADS)
            order(dve.reciprocal(soft[:, REC3, :], soft[:, SUM3, :]))
            dve.wait_ge(head_done, MLA_HEADS)
            rec = soft[:, REC3, :].rearrange("p (h m) -> p h m", m=MT)
            for half in range(2):
                for m in range(MT):
                    dve.tensor_tensor(
                        attended[:, m, 512 * half:512 * half + 512].rearrange("p (h d) -> p h d", d=64),
                        bank[2 * m + half][:, :].rearrange("p (h d) -> p h d", d=64),
                        rec[:, 8 * half:8 * half + 8, m].unsqueeze(2).to_broadcast([P, 8, 64]),
                        ALU.mult).then_inc(divided, 1)
            for b in range(4):
                dve.wait_ge(m3_hi, b + 1)
                r = slice(2 * b, 2 * b + 2)
                dve.tensor_tensor(h_lo[:, r, :].rearrange("p k t -> p (k t)"), bank[4 + b][:, :],
                                  h_hi[:, r, :].bitcast(F32).rearrange("p k t -> p (k t)"),
                                  ALU.subtract).then_inc(m3_lo, 1)
            dve_panels(dve, M3 + 16, 5)

        stages = STAGES[:last_stage]

        block = ctx.enter_context(nc.Block())
        out_stored = sem("out_stored")
        final_loaded = sem("final_loaded")
        final_row = region(2048, D)

        @block.sync
        def _(sp):
            def load_panel(g0, i=0):
                slot = g0 % RING
                if g0 >= RING:
                    sp.wait_ge(lo_ready, g0 - (RING - 1) + RING * i)
                sp.dma_start(raw[:, slot, :], panels[g0 + RING * i]).then_inc(raw_loaded[slot], 16)

            def load_ada(a, i=0):
                slot = a % ADA_RING
                if a >= ADA_RING:
                    sp.wait_ge(ada_used, a - (ADA_RING - 1) + 8 * i)
                sp.dma_start(ada_ring[:, slot, :], ada[a + 8 * i]).then_inc(ada_loaded[slot], 16)

            sp.dma_start(C[:, :], cols).then_inc(small_loaded, 16)
            sp.dma_start(X[:, :, :], x_in.rearrange("(m p) d -> p m d", p=P)).then_inc(x_loaded, 16)
            for a in range(16):
                load_ada(a)
            for g in range(8):
                load_panel(g)
            with sp.Fori(0, 7) as i:
                for half in range(2):
                    for j in range(3):
                        load_panel(8 + 3 * half + j, i)
                    for j in range(4):
                        load_ada(16 + 4 * half + j, i)
            done, total = 8 + 7 * RING, min(last_panel(*stages[-1]) + 3, TOTAL)
            turns = (total - done) // RING
            if turns:
                with sp.Fori(0, turns) as i:
                    for j in range(RING):
                        load_panel(done + j, i)
            for g in range(done + RING * turns, total):
                load_panel(g)

        @block.gpsimd
        def _(pool):
            order = Order(pool, pool_order)
            pool.memset(ones[:, :], 1.0).then_inc(const_ready, 1)
            pool.memset(stat[:, MINUS_HALF - 1:MINUS_HALF + 1], -0.5).then_inc(const_ready, 1)
            pool.wait_ge(const_ready, 2)
            norm_pool(pool, 0, order)
            spectrum_pool(pool)
            params_pool(pool, order)
            gate_rows_pool(pool)
            for at, (kind, n) in enumerate(stages):
                if kind == "mix1":
                    mix1_pool(pool, order)
                if at < 3:
                    add_pool(pool, at, order)
                norm_pool(pool, at + 1, order)
                if at == 2:
                    mix2_loads(pool)
                if at == 4:
                    mix3_loads(pool)
                if at + 1 == len(stages):
                    pool.dma_start(final_row[:, :], rows[6:7, :].partition_broadcast(P)).then_inc(final_loaded, 16)
            for m in range(MT):
                pool.wait_ge(xhat_done, 2 * len(stages) + m + 1)
                pool.dma_start(out[m * P:(m + 1) * P, :], xhat[:, m, :]).then_inc(out_stored, 16)
            pool.wait_ge(out_stored, 32)

        @block.scalar
        def _(act):
            order = Order(act, act_order)
            act.dma_start(ident[:, :], tables[0]).then_inc(small_loaded, 16)
            act.dma_start(feat_t, feats).then_inc(spec_loaded, 16)
            act.dma_start(mlp_ws, mlp_w[:, 0:192]).then_inc(spec_loaded, 16)
            act.dma_start(filter_out[0:64, :], mlp_w[:, 192:2240]).then_inc(spec_loaded, 16)
            act.dma_start(dft[:, 0, :, :], pool_mats[4]).then_inc(spec_loaded, 16)
            act.dma_start(dft[:, 1, :, :], pool_mats[5]).then_inc(spec_loaded, 16)
            act.dma_start(decay_rows, decay[0:1, :].partition_broadcast(P)).then_inc(decay_loaded, 16)
            act.wait_ge(small_loaded, 32)
            act.activation(c_act, col("c", 0, 8), ACT.Silu).then_inc(c_ready, 1)
            norm_act_squares(act, 0)
            params_act(act)
            spectrum_act(act, order)
            act_panels(act, 0, 3)
            norm_act_rest(act, 0)
            for at, (kind, n) in enumerate(stages):
                if kind == "ffn":
                    ffn_act(act, n)
                elif kind == "mix1":
                    mix1_act(act, order)
                elif kind == "mix2":
                    mix2_act(act, order)
                else:
                    mix3_act(act, order)
                if at < 3:
                    add_act(act, kind, n, at)
                norm_act_squares(act, at + 1)
                if at + 1 < len(stages):
                    norm_act_rest(act, at + 1)

        @block.vector
        def _(dve):
            order = Order(dve, dve_order)
            ada_next = iter(range(16))

            def spare():
                a = next(ada_next, None)
                if a is not None:
                    ada_add(dve, a // 8, a % 8)

            dve.wait_ge(small_loaded, 32)
            params_dve(dve, order)
            dve.wait_ge(c_ready, 1)
            for _ in range(4):
                spare()
            spectrum_dve(dve, order, spare)
            for _ in range(16):
                spare()
            ada_first_dve(dve, order)
            dve_panels(dve, 0, 3)
            norm_dve(dve, 0)
            for at, (kind, n) in enumerate(stages):
                if kind == "ffn":
                    ffn_dve(dve, n)
                    if n == 0:
                        ada_rest_dve(dve, order)
                elif kind == "mix1":
                    mix1_dve(dve, order)
                elif kind == "mix2":
                    mix2_dve(dve, order)
                else:
                    mix3_dve(dve, order)
                add_dve(dve, kind, n, at if at < 3 else None, order)
                if at + 1 < len(stages):
                    norm_dve(dve, at + 1)
            dve.wait_ge(final_loaded, 16)
            last = len(stages)
            for m in range(MT):
                dve.wait_ge(rstd_done, 2 * last + m + 1)
                dve.scalar_tensor_tensor(out=xhat[:, m, :], in0=X[:, m, :],
                                         scalar=stat[:, RS + m:RS + m + 1], in1=final_row[:, :],
                                         op0=ALU.mult, op1=ALU.mult).then_inc(xhat_done, 1)

        @block.tensor
        def _(pe):
            pe.wait_ge(const_ready, 2)
            pe.wait_ge(small_loaded, 32)
            spectrum_pe(pe)
            ada_first_pe(pe)
            norm_pe(pe, 0)
            for at, (kind, n) in enumerate(stages):
                if kind == "ffn":
                    ffn_pe(pe, n)
                elif kind == "mix1":
                    mix1_pe(pe)
                elif kind == "mix2":
                    mix2_pe(pe)
                else:
                    mix3_pe(pe)
                if at + 1 < len(stages):
                    norm_pe(pe, at + 1)



def stream_of_panels(a):
    def columns(w):
        k, n = w.shape[0] // P, w.shape[1] // P
        return w.reshape(k, P, n, P).transpose(2, 1, 0, 3).reshape(n, P, k * P)

    def together(p, n):
        return p.reshape(-1, n, P, p.shape[2]).transpose(0, 2, 1, 3).reshape(-1, P, n * p.shape[2])

    def ffn(gate, up, down):
        g, u, d = columns(gate), columns(up), down.reshape(FT, P, D)
        order = [g[0], u[0]]
        for f in range(1, FT):
            order += [g[f], u[f], d[f - 1]]
        return np.stack(order + [d[FT - 1]])

    def mix1():
        w = a["w_in"][0]
        q = w[:, :512].reshape(D, 2, 4, HD).transpose(0, 2, 1, 3).reshape(D, 512)
        return [columns(w[:, 768:]), columns(q), columns(w[:, 512:768]),
                together(columns(a["ssm_w_glu"][0]), 2), a["w_out"][0].reshape(8, P, D)]

    def mix2():
        w = a["mix_w_in_2"][0]
        return [together(w[:, :512].reshape(8, P, 512), 2),
                columns(w[:, 1536:]), columns(w[:, 512:1536]), a["mix_w_out_2"][0].reshape(8, P, D)]

    def mix3():
        uq = a["mla_w_uq_2"][0].reshape(256, MLA_HEADS, 96)
        dkv, ukv = a["mla_w_dkv_2"][0], a["mla_w_ukv_2"][0].reshape(P, MLA_HEADS, P)
        swap = np.r_[16:32, 0:16]
        rope = uq[:, :, 64:]
        return [columns(a["mla_w_dq_2"][0]), columns(dkv[:, :P]),
                columns(np.concatenate([dkv[:, P:], dkv[:, P:][:, swap]] * 2, 1)),
                together(columns(uq[:, :, :64].reshape(256, 1024)), 4),
                together(columns(rope.reshape(256, 512)), 4),
                together(columns(rope[:, :, swap].reshape(256, 512)), 4),
                ukv[:, :, :64].reshape(1, P, D), ukv[:, :, 64:].reshape(1, P, D),
                a["mla_w_o_2"][0].reshape(8, P, D)]

    g, u, d = a["ffn_w_gate_2"], a["ffn_w_up_2"], a["ffn_w_down_2"]
    feed = [ffn(a["w1_gate"][0], a["w1_up"][0], a["w1_down"][0]),
            ffn(a["w2_gate"][0], a["w2_up"][0], a["w2_down"][0])]
    feed += [ffn(g[i, j], u[i, j], d[i, j]) for i in range(2) for j in range(2)]
    parts = []
    for kind, n in STAGES:
        parts += [feed[n]] if kind == "ffn" else {"mix1": mix1, "mix2": mix2, "mix3": mix3}[kind]()
    return np.concatenate(parts)


def small_columns(a):
    def cut(v):
        return v.reshape(-1, P).T

    def states(v):
        return v.reshape(STATE_TILES, P).T

    def short(v):
        return np.concatenate([v, np.zeros((P - 64,) + v.shape[1:], np.float32)])

    t = np.linspace(0.0, 1.0, SEQ, dtype=np.float32)
    parts = [("c", cut(a["c"])), ("b_ada", cut(a["b_ada"])),
             ("g_pre", np.concatenate([cut(a[n]) for n in ("g_pre_ff1", "g_pre_mix", "g_pre_ff2")], 1)),
             ("norm_g", cut(a["norm_g_2"])), ("pool_scale", cut(a["pool_scale_2"])),
             ("conv_b", cut(a["hyena_conv_b_2"])), ("conv_w", cut(a["hyena_conv_w_2"])),
             ("bias", cut(a["hyena_bias_2"])), ("g_attn", cut(a["g_attn_out"])),
             ("g_ssm", cut(a["g_ssm_out"])), ("ssm_d", cut(a["ssm_d"])), ("b_glu", cut(a["ssm_b_glu"])),
             ("q_g", cut(a["mla_q_norm_g_2"])), ("kv_g", cut(a["mla_kv_norm_g_2"])),
             ("a_re", states(a["ssm_a_re"])), ("a_im", states(a["ssm_a_im"])),
             ("log_step", states(np.repeat(a["ssm_log_step"][0], 64))),
             ("sin_freq", short(a["hyena_sin_freq_2"][0].T)),
             ("mlp_b", short(np.stack([a[f"hyena_ffn_b{i}_2"][0] for i in (1, 2, 3)], 1))),
             ("neg_t", cut(-t))]
    for (name, v), (key, (_, n)) in zip(parts, COLS.items()):
        assert name == key and v.shape == (P, n), (name, v.shape, n)
    return np.concatenate([v for _, v in parts], 1)


def shape_constants():
    t = np.arange(SEQ)
    angle = np.outer(t, 2 * t + 1) * (math.pi / 512)
    cos, sin = np.cos(angle), np.sin(angle)
    tiles = lambda m: m.reshape(MT, P, SEQ).transpose(1, 0, 2)
    mats = []
    for w in (2, 4, 8, 16):
        lo = np.clip(t - w // 2, 0, SEQ)
        hi = np.clip(t - w // 2 + w, 0, SEQ)
        s = t[:, None]
        mats.append(((s >= lo) & (s < hi)) / (hi - lo) - (s == t))
    mats += [cos, sin, cos.T / 256, sin.T / 256]
    pool_mats = np.stack([tiles(m) for m in mats]).astype(np.float32)
    inv = (10000.0 ** (-np.arange(0, 32, 2, dtype=np.float32) / 32)).astype(np.float32)
    ang = np.arange(SEQ, dtype=np.float32)[:, None] * inv[None, :]
    c, s = np.cos(ang.astype(np.float64)).T, np.sin(ang.astype(np.float64)).T
    rope = np.stack([np.tile(np.concatenate([c, c]), (4, 1)),
                     np.tile(np.concatenate([-s, s]), (4, 1))], 1).astype(np.float32)
    i, j = np.arange(P)[:, None], np.arange(2 * P)[None, :]
    dist = i + P - j
    near = np.where((dist >= 0) & (dist < P), -dist, -1e38).astype(np.float32)
    near = np.concatenate([near[:, P:], near], 1)
    bands = 16
    w = (2.0 * math.pi * np.arange(SEQ, dtype=np.float32) / SEQ).astype(np.float32)
    f = np.linspace(1e-4, bands - 1, bands, dtype=np.float32)
    phase = (w[:, None] * f[None, :]).astype(np.float64)
    z = np.concatenate([np.linspace(0.0, 1.0, SEQ)[:, None], np.cos(phase), -np.sin(phase)], 1)
    return {"tables": np.eye(P, dtype=np.float32)[None], "pool_mats": pool_mats, "rope": rope,
            "near": near, "feats": np.ascontiguousarray(z.T.astype(np.float32))}


def lay_out(a):
    a = {k: np.asarray(v) for k, v in a.items()}
    ada = a["w_ada"][0].reshape(KT, P, 9, D).transpose(2, 0, 1, 3).reshape(72, P, D)
    b_ada = a["b_ada"].reshape(9, D)
    rows = np.stack([b_ada[2], b_ada[5], b_ada[8], a["g_post_ff1"][0], a["g_post_mix"][0],
                     a["g_post_ff2"][0], a["final_norm_g_2"]])
    b = [a[n][0].reshape(STATE_TILES, P, 16).transpose(1, 0, 2).reshape(P, 256)
         for n in ("ssm_b_re", "ssm_b_im")]
    c = [a[n][0].reshape(STATE_TILES, 2, 16, 64).transpose(1, 3, 0, 2).reshape(P, 256)
         for n in ("ssm_c_re", "ssm_c_im")]
    mlp_w = np.zeros((64, 2240), np.float32)
    mlp_w[:33, 0:64] = a["hyena_ffn_w1_2"][0]
    mlp_w[:, 64:128] = a["hyena_ffn_w2_2"][0]
    mlp_w[:, 128:192] = a["hyena_ffn_w3_2"][0]
    mlp_w[:, 192:] = a["hyena_ffn_w_out_2"][0]
    got = {"panels": stream_of_panels(a), "ada": ada, "cols": small_columns(a), "rows": rows,
           "sinks": a["attn_sinks"], "ssm_mats": np.stack(b + c, 1),
           "pool_w": a["pool_w_2"][0].transpose(1, 0, 2), "decay": a["hyena_decay_2"][0].reshape(2, 1024),
           "mlp_w": mlp_w, "x_in": a["x"][0]}
    got.update(shape_constants())
    return {k: np.ascontiguousarray(v) for k, v in got.items()}


def kernel(last_stage=len(STAGES), **inputs):
    from concourse import bacc
    from concourse.bass_utils import run_bass_kernel_spmd

    nc = bacc.Bacc("TRN2", target_bir_lowering=False, num_devices=1)
    arrays = lay_out(inputs)
    args = {name: nc.dram_tensor(name, v.shape, F32, kind="ExternalInput").ap()
            for name, v in arrays.items()}
    out = nc.dram_tensor("out", (SEQ, D), F32, kind="ExternalOutput").ap()
    spectrum = nc.dram_tensor("spectrum", (2, P, 4, 512), F32, kind="Internal").ap()
    build_program(nc, out=out, spectrum=spectrum, last_stage=last_stage, **args)
    result = run_bass_kernel_spmd(nc, [arrays], core_ids=[0])
    return result.results[0]["out"].reshape(1, SEQ, D)
```

```python
import math
from contextlib import ExitStack

import numpy as np
import concourse.bass as bass
from concourse import mybir

F32 = mybir.dt.float32
F32R = mybir.dt.float32r
I32 = mybir.dt.int32
ALU = mybir.AluOpType
ACT = mybir.ActivationFunctionType
AX = mybir.AxisListType

P = 128
D = 1024
KT = D // P
SEQ = 256
MT = SEQ // P
FF = 2816
FT = FF // P
PANEL = 1024
RING = 6
EPS = 1e-6
HEADS, HD = 8, 64
STATE_TILES = 16
MLA_HEADS = 16
ADA_RING = 5
ADA_MIDDLE = (2, 3, 4, 6, 7)
ADA_FIRST = 2 * KT
ADA_GATE_1 = ADA_FIRST + len(ADA_MIDDLE) * KT
ADA_GATE_2 = ADA_GATE_1 + KT

FFN_PANELS = 3 * FT
MIX1_PANELS = 10 + 2 + 8
MIX2_PANELS = 4 + 12 + 8
MIX3_PANELS = 4 + 4 + 2 + 8
STAGES = [("ffn", 0), ("mix1", 0), ("ffn", 1), ("ffn", 2), ("mix2", 0), ("ffn", 3),
          ("ffn", 4), ("mix3", 0), ("ffn", 5)]
SIZE = {"ffn": FFN_PANELS, "mix1": MIX1_PANELS, "mix2": MIX2_PANELS, "mix3": MIX3_PANELS}
FIRST = {}
TOTAL = 0
for _s in STAGES:
    FIRST[_s] = TOTAL
    TOTAL += SIZE[_s[0]]

COLS = {}
_w = 0
for _name, _n in (("c", 8), ("b_ada", 72), ("g_pre", 24), ("norm_g", 48), ("pool_scale", 4),
                  ("conv_b", 12), ("conv_w", 36), ("bias", 8), ("g_attn", 4), ("g_ssm", 4),
                  ("ssm_d", 4), ("b_glu", 4), ("q_g", 2), ("kv_g", 1), ("a_re", 16), ("a_im", 16),
                  ("log_step", 16), ("sin_freq", 3), ("mlp_b", 3), ("neg_t", 2)):
    COLS[_name] = (_w, _n)
    _w += _n
N_COLS = _w

MAGIC = 12582912.0
TWO_PI = 2.0 * math.pi
TWO_PI_HI = 6.28125
TWO_PI_LO = TWO_PI - TWO_PI_HI
LN2_HI = 0.693359375
LN2_LO = math.log(2.0) - LN2_HI
PI_BELOW = 3.1415925


def build_program(nc, panels, ada, cols, rows, sinks, ssm_mats, tables, pool_mats, rope, near,
                  pool_w, decay, mlp_w, feats, x_in, out, spectrum, last_stage):
    ctx = ExitStack()
    with ctx:
        def sb(name, shape, dt=F32):
            return ctx.enter_context(nc.sbuf_tensor(name, shape, dt))

        def sem(name):
            return ctx.enter_context(nc.semaphore(name))

        X = sb("X", [P, MT, D])
        raw = sb("raw", [P, RING, PANEL])
        w_hi = sb("w_hi", [P, RING, PANEL], F32R)
        w_lo = sb("w_lo", [P, RING, PANEL], F32R)
        h_hi = sb("h_hi", [P, KT, SEQ], F32R)
        h_lo = sb("h_lo", [P, KT, SEQ], F32R)
        f_hi = sb("f_hi", [P, 2, SEQ], F32R)
        f_lo = sb("f_lo", [P, 2, SEQ], F32R)
        C = sb("C", [P, N_COLS])
        ident = sb("ident", [P, P])
        ones = sb("ones", [P, P])
        mods = sb("mods", [P, 6, KT])
        pre_scale = sb("pre_scale", [P, 3, KT])
        stat = sb("stat", [P, 64])
        par = sb("par", [P, 20, 16])
        ARENA = 26112
        arena = sb("arena", [P, ARENA])

        def region(at, *shape):
            size = int(np.prod(shape))
            assert at + size <= ARENA, (at, shape)
            v = arena[:, at:at + size]
            if len(shape) == 2:
                return v.rearrange("p (a b) -> p a b", b=shape[1])
            if len(shape) == 3:
                return v.rearrange("p (a b c) -> p a b c", b=shape[1], c=shape[2])
            return v

        gated_sum = region(0, MT, D)
        h32 = region(2048, KT, SEQ)
        squares = region(2048, 4, 512)
        acc = region(0, len(ADA_MIDDLE), D)
        acc0 = region(4096, 2, D)
        acc_gate_1 = region(13312, D)
        acc_gate_2 = region(4096, D)
        late_panel = region(5120, D)
        ada_ring = region(6144, ADA_RING, D)
        gate_rows = region(11264, 3, D)
        ssm_raw = region(11264, 4, 256)
        rot_tmp = region(11264, 16, 128)
        b_rows = region(13312, 2, 512)
        rot = region(14336, 2, STATE_TILES, SEQ)
        b_turned = region(22528, 2, 4, P)
        c_rows = region(23552, 3, STATE_TILES, 32)
        ffn_buf = region(25088, 4, SEQ)

        def col(name, i=0, n=1):
            at, _ = COLS[name]
            return C[:, at + i:at + i + n]

        bank = [ctx.enter_context(nc.psum_tensor(f"bank{i}", [P, 512], F32)) for i in range(8)]

        raw_loaded = [sem(f"raw_loaded{i}") for i in range(RING)]
        ada_loaded = [sem(f"ada_loaded{i}") for i in range(ADA_RING)]
        hi_ready = sem("hi_ready")
        lo_ready = sem("lo_ready")
        panel_used = sem("panel_used")
        ada_used = sem("ada_used")
        act_order = sem("act_order")
        dve_order = sem("dve_order")
        pool_order = sem("pool_order")

        class Order:
            def __init__(self, eng, s):
                self.eng, self.s, self.n = eng, s, 0

            def __call__(self, ins):
                self.n += 1
                ins.then_inc(self.s, 1)
                self.eng.wait_ge(self.s, self.n)

        def then(eng, ins, s, value):
            ins.then_inc(s, 1)
            eng.wait_ge(s, value)

        def split_hi(act, g0, i=0):
            slot = g0 % RING
            act.wait_ge(raw_loaded[slot], 16 * (g0 // RING + 1) + 16 * i)
            if g0 >= RING:
                act.wait_ge(panel_used, g0 - (RING - 1) + RING * i)
            act.activation(w_hi[:, slot, :], raw[:, slot, :], ACT.Copy).then_inc(hi_ready, 1)

        def split_lo(dve, g0, i=0):
            slot = g0 % RING
            dve.wait_ge(hi_ready, g0 + 1 + RING * i)
            dve.tensor_tensor(w_lo[:, slot, :], raw[:, slot, :], w_hi[:, slot, :].bitcast(F32),
                              ALU.subtract).then_inc(lo_ready, 1)

        def act_panels(act, first, n):
            for g in range(first, min(first + n, TOTAL)):
                split_hi(act, g)

        def dve_panels(dve, first, n):
            for g in range(first, min(first + n, TOTAL)):
                split_lo(dve, g)

        def product3(pe, out_ap, wh, wl, xh, xl, start, stop, weights_move=False):
            last = None
            for n, (w, x) in enumerate(((wh, xh), (wh, xl), (wl, xh))):
                a, b = (x, w) if weights_move else (w, x)
                last = pe.matmul(out_ap, a, b, start=start and n == 0, stop=stop and n == 2)
            return last

        def channel_product(pe, out_ap, g0, i=0, k_tiles=KT, at=0, k0=0, used=True, norm=None):
            slot = g0 % RING
            pe.wait_ge(lo_ready, g0 + 1 + RING * i)
            mm = None
            for k in range(k_tiles):
                w = slice(at + k * P, at + (k + 1) * P)
                if norm is not None:
                    pe.wait_ge(h_lo_done, KT * norm + k + 1)
                mm = product3(pe, out_ap, w_hi[:, slot, w], w_lo[:, slot, w], h_hi[:, k0 + k, :],
                              h_lo[:, k0 + k, :], k == 0, k == k_tiles - 1)
            if used:
                mm.then_inc(panel_used, 1)
            return mm

        def token_product(pe, g0, xh, xl, start, stop, i=0, result=True):
            slot = g0 % RING
            pe.wait_ge(lo_ready, g0 + 1 + RING * i)
            mm = None
            for m in range(MT):
                t = slice(m * P, (m + 1) * P)
                for n in range(2):
                    w = slice(n * 512, (n + 1) * 512)
                    mm = product3(pe, bank[2 * m + n][:, :], w_hi[:, slot, w], w_lo[:, slot, w],
                                  xh[:, t], xl[:, t], start, stop, weights_move=True)
                    if stop and result and 2 * m + n < 3:
                        mm.then_inc(result_ready, 1)
            mm.then_inc(panel_used, 1)

        result_ready = sem("result_ready")
        square_done = sem("square_done")
        rstd_done = sem("rstd_done")
        diag_done = sem("diag_done")
        turned = sem("turned")
        h_hi_done = sem("h_hi_done")
        h_lo_done = sem("h_lo_done")
        x_done = sem("x_done")
        SS, RS, RSS, RRS = 0, 4, 6, 10
        MINUS_HALF = 63
        diag = sb("diag", [P, MT, P])

        def norm_scalars(n):
            if n in (0, 1, 2):
                return pre_scale[:, n, :], mods[:, 2 * n, :]
            at, _ = COLS["norm_g"]
            return C[:, at + (n - 3) * KT:at + (n - 2) * KT], None

        def mean_square(act, q, source, at):
            return act.activation(squares[:, q, :], source, ACT.Square, scale=D ** -0.5,
                                  accum_out=stat[:, at + q:at + q + 1])

        def quarter(q):
            return slice((q % 2) * 512, (q % 2) * 512 + 512)

        def norm_act_squares(act, n):
            if n == 0:
                act.wait_ge(x_loaded, 16)
            for q in range(4):
                if n:
                    act.wait_ge(x_done, 4 * (n - 1) + q + 1)
                mean_square(act, q, X[:, q // 2, quarter(q)], SS).then_inc(square_done, 1)

        def norm_act_rest(act, n):
            sc, sh = norm_scalars(n)
            for k in range(KT):
                if k % 2 == 0:
                    act.wait_ge(turned, 4 * n + k // 2 + 1)
                ps = bank[4 + k // 2][:, (k % 2) * SEQ:(k % 2 + 1) * SEQ]
                act.activation(h_hi[:, k, :], ps, ACT.Identity, scale=sc[:, k:k + 1],
                               bias=0.0 if sh is None else sh[:, k:k + 1]).then_inc(h_hi_done, 1)

        def rstd_pool(pool, order, squares_at, rstd_at, m):
            two = stat[:, squares_at + 2 * m:squares_at + 2 * m + 2]
            rs = stat[:, rstd_at + m:rstd_at + m + 1]
            order(pool.tensor_scalar(rs, two[:, 0:1], two[:, 1:2], EPS, ALU.add, ALU.add))
            return pool.tensor_tensor(rs, rs, stat[:, MINUS_HALF:MINUS_HALF + 1], ALU.pow)

        def norm_pool(pool, n, order):
            for m in range(MT):
                pool.wait_ge(square_done, 4 * n + 2 * m + 2)
                rstd_pool(pool, order, SS, RS, m).then_inc(rstd_done, 1)

        def norm_dve(dve, n, order):
            for m in range(MT):
                dve.wait_ge(rstd_done, 2 * n + m + 1)
                dve.tensor_scalar(diag[:, m, :], ident[:, :], stat[:, RS + m:RS + m + 1], None,
                                  ALU.mult).then_inc(diag_done, 1)
            sc, sh = norm_scalars(n)
            for b in range(4):
                dve.wait_ge(h_hi_done, KT * n + 2 * b + 2)
                for k in (2 * b, 2 * b + 1):
                    ps = bank[4 + b][:, (k % 2) * SEQ:(k % 2 + 1) * SEQ]
                    hi = h_hi[:, k, :].bitcast(F32)
                    if sh is None:
                        ins = dve.scalar_tensor_tensor(out=h_lo[:, k, :], in0=ps, scalar=sc[:, k:k + 1],
                                                       in1=hi, op0=ALU.mult, op1=ALU.subtract)
                    else:
                        order(dve.tensor_scalar(h32[:, k, :], ps, sc[:, k:k + 1], sh[:, k:k + 1],
                                                ALU.mult, ALU.add))
                        ins = dve.tensor_tensor(h_lo[:, k, :], h32[:, k, :], hi, ALU.subtract)
                    ins.then_inc(h_lo_done, 1)

        def norm_pe(pe, n):
            for m in range(MT):
                pe.wait_ge(diag_done, 2 * n + m + 1)
                for k in range(KT):
                    at = (k % 2) * SEQ + m * P
                    mm = pe.matmul(bank[4 + k // 2][:, at:at + P], X[:, m, k * P:(k + 1) * P],
                                   diag[:, m, :], start=True, stop=True)
                    if m == MT - 1 and k % 2:
                        mm.then_inc(turned, 1)

        silu_done = sem("silu_done")
        hidden_done = sem("hidden_done")
        f_hi_done = sem("f_hi_done")
        f_lo_done = sem("f_lo_done")

        def up_bank(f):
            return bank[4 + f % 2 if f else 0]

        def ffn_pe(pe, n):
            base, s0 = FIRST[("ffn", n)], FT * n

            def up(f, i=0):
                g = base + max(3 * f - 1, 0)
                if s0 + f >= 2:
                    pe.wait_ge(hidden_done, s0 + f - 1 + 2 * i)
                channel_product(pe, up_bank(f)[:, 0:SEQ], g, i,
                                norm=STAGES.index(("ffn", n)) if f == 0 else None)
                channel_product(pe, up_bank(f)[:, SEQ:2 * SEQ], g + 1, i)

            def down(f, i=0, start=False, stop=False):
                pe.wait_ge(f_lo_done, s0 + f + 1 + 2 * i)
                g = base + (3 * FT - 1 if stop else 3 * f + 4)
                token_product(pe, g, f_hi[:, f % 2, :], f_lo[:, f % 2, :], start, stop, i)

            def tiles(lo, hi):
                with pe.Fori(lo, hi) as i:
                    up(2, i)
                    down(1, i)
                    up(3, i)
                    down(2, i)

            up(0)
            up(1)
            down(0, start=True)
            tiles(0, FT // 2 - 2)
            if n == 0:
                turn_b_pe(pe)
                ada_middle_pe(pe)
            if n == 1:
                gate_pe(pe, 2, acc_gate_2, (6, 7))
            tiles(FT // 2 - 2, FT // 2 - 1)
            down(FT - 1, stop=True)

        def ffn_act(act, n):
            base, s0 = FIRST[("ffn", n)], FT * n

            def hidden(f, i=0):
                act.wait_ge(panel_used, base + (3 * f + 1 if f else 2) + RING * i)
                act.activation(ffn_buf[:, f % 2, :], up_bank(f)[:, 0:SEQ],
                               ACT.Silu).then_inc(silu_done, 1)
                act.wait_ge(hidden_done, s0 + f + 1 + 2 * i)
                act.activation(f_hi[:, f % 2, :], ffn_buf[:, 2 + f % 2, :],
                               ACT.Copy).then_inc(f_hi_done, 1)

            def tiles(lo, hi):
                with act.Fori(lo, hi) as i:
                    for f in (2, 3):
                        for j in range(3):
                            split_hi(act, base + 3 * f + 2 + j, i)
                        hidden(f, i)

            act_panels(act, base + 3, 2)
            hidden(0)
            act_panels(act, base + 5, 3)
            hidden(1)
            tiles(0, FT // 2 - 2)
            if n == 0:
                turn_b_act(act)
            for f in (FT - 2, FT - 1):
                act_panels(act, base + 3 * f + 2, 3)
                hidden(f)
            act_panels(act, base + 3 * FT + 2, 1)

        def ffn_dve(dve, n, order):
            base, s0 = FIRST[("ffn", n)], FT * n

            def hidden(f, i=0):
                dve.wait_ge(silu_done, s0 + f + 1 + 2 * i)
                if s0 + f >= 2:
                    dve.wait_ge(f_lo_done, s0 + f - 1 + 2 * i)
                dve.tensor_tensor(ffn_buf[:, 2 + f % 2, :], ffn_buf[:, f % 2, :],
                                  up_bank(f)[:, SEQ:2 * SEQ], ALU.mult).then_inc(hidden_done, 1)
                dve.wait_ge(f_hi_done, s0 + f + 1 + 2 * i)
                dve.tensor_tensor(f_lo[:, f % 2, :], ffn_buf[:, 2 + f % 2, :],
                                  f_hi[:, f % 2, :].bitcast(F32), ALU.subtract).then_inc(f_lo_done, 1)

            def tiles(lo, hi, middle=False, late=False):
                with dve.Fori(lo, hi) as i:
                    for f in (2, 3):
                        for j in range(3):
                            split_lo(dve, base + 3 * f + 2 + j, i)
                        if middle:
                            for c in ((0, 1), (2, 3, 4))[f - 2]:
                                ada_add_middle(dve, c, i)
                        if late and f == 3:
                            ada_add_late(dve, i)
                        hidden(f, i)

            dve_panels(dve, base + 3, 2)
            hidden(0)
            dve_panels(dve, base + 5, 3)
            hidden(1)
            if n == 0:
                dve.wait_ge(acc_ready, 16)
                tiles(0, KT, middle=True)
                tiles(KT, FT // 2 - 2)
                ada_middle_dve(dve, order)
            elif n == 1:
                dve.wait_ge(acc_ready, 48)
                tiles(0, KT, late=True)
                tiles(KT, FT // 2 - 2)
                gate_dve(dve, 2, (6, 7), order)
            else:
                tiles(0, FT // 2 - 2)
            for f in (FT - 2, FT - 1):
                dve_panels(dve, base + 3 * f + 2, 3)
                hidden(f)
            dve_panels(dve, base + 3 * FT + 2, 1)

        result_squares = sem("result_squares")
        result_rstd = sem("result_rstd")
        times_gate = sem("times_gate")

        def last_panel(kind, n):
            return FIRST[(kind, n)] + SIZE[kind]

        def wait_result(eng, at, kind, n, q):
            if q < 3:
                eng.wait_ge(result_ready, 3 * at + q + 1)
            else:
                eng.wait_ge(panel_used, last_panel(kind, n))

        def add_act(act, kind, n, at):
            for q in range(4):
                wait_result(act, at, kind, n, q)
                mean_square(act, q, bank[q][:, :], RSS).then_inc(result_squares, 1)

        def add_pool(pool, at, order):
            for m in range(MT):
                pool.wait_ge(result_squares, 4 * at + 2 * m + 2)
                rstd_pool(pool, order, RSS, RRS, m).then_inc(result_rstd, 1)

        def add_dve(dve, kind, n, at):
            if at >= 3:
                for q in range(4):
                    wait_result(dve, at, kind, n, q)
                    x = X[:, q // 2, quarter(q)]
                    dve.scalar_tensor_tensor(out=x, in0=bank[q][:, :],
                                             scalar=0.5 if kind == "ffn" else 1.0, in1=x,
                                             op0=ALU.mult, op1=ALU.add).then_inc(x_done, 1)
                return
            for q in range(4):
                dve.wait_ge(result_squares, 4 * at + q + 1)
                dve.tensor_tensor(gated_sum[:, q // 2, quarter(q)], bank[q][:, :],
                                  gate_rows[:, at, quarter(q)], ALU.mult).then_inc(times_gate, 1)
            dve.wait_ge(times_gate, 4 * at + 4)
            for q in range(4):
                m = q // 2
                dve.wait_ge(result_rstd, 2 * at + m + 1)
                x = X[:, m, quarter(q)]
                dve.scalar_tensor_tensor(out=x, in0=gated_sum[:, m, quarter(q)],
                                         scalar=stat[:, RRS + m:RRS + m + 1], in1=x,
                                         op0=ALU.mult, op1=ALU.add).then_inc(x_done, 1)
        c_ready = sem("c_ready")
        x_loaded = sem("x_loaded")
        small_loaded = sem("small_loaded")
        const_ready = sem("const_ready")
        acc_ready = sem("acc_ready")
        gate_1_loaded = [sem(f"gate_1_loaded{i}") for i in range(ADA_RING)]
        late_loaded = sem("late_loaded")
        gain_loaded = sem("gain_loaded")
        column_sums = sem("column_sums")
        mods_done = sem("mods_done")
        gate_sums = sem("gate_sums")
        c_act = stat[:, 16:16 + KT]

        def ada_multiply_add(dve, a, dst, src, c):
            dve.wait_ge(ada_used, a)
            dve.scalar_tensor_tensor(out=dst, in0=src, scalar=c, in1=dst, op0=ALU.mult,
                                     op1=ALU.add).then_inc(ada_used, 1)

        def ada_add(dve, a, dst):
            slot, k = a % ADA_RING, a % KT
            dve.wait_ge(ada_loaded[slot], 16 * (a // ADA_RING + 1))
            if k == 0:
                dve.tensor_scalar(dst, ada_ring[:, slot, :], c_act[:, 0:1], None,
                                  ALU.mult).then_inc(ada_used, 1)
            else:
                ada_multiply_add(dve, a, dst, ada_ring[:, slot, :], c_act[:, k:k + 1])

        def ada_add_gate_1(dve, k):
            slot = k % ADA_RING
            dve.wait_ge(gate_1_loaded[slot], 16 * (k // ADA_RING + 1))
            ada_multiply_add(dve, ADA_GATE_1 + k, acc_gate_1, ada_ring[:, slot, :], c_act[:, k:k + 1])

        def ada_add_middle(dve, c, i):
            a = ADA_FIRST + c
            slot = a % ADA_RING
            dve.wait_ge(ada_loaded[slot], 16 * (a // ADA_RING + 1) + 16 * i)
            c_k = c_act.rearrange("p (k o) -> p k o", o=1)[:, i, :]
            ada_multiply_add(dve, a + ADA_RING * i, acc[:, c, :], ada_ring[:, slot, :], c_k)

        def ada_add_late(dve, i):
            dve.wait_ge(late_loaded, 16 + 16 * i)
            c = c_act.rearrange("p (k o) -> p k o", o=1)
            ada_multiply_add(dve, ADA_GATE_2 + i, acc_gate_2, late_panel, c[:, i, :])

        def sum_columns(pe, part, to, at):
            mm = None
            for k in range(KT):
                mm = pe.matmul(bank[to][:, at + k:at + k + 1], part[:, k * P:(k + 1) * P],
                               ones[:, 0:1], start=True, stop=True)
            return mm

        def ada_first_pe(pe):
            for c in range(2):
                pe.wait_ge(ada_used, 8 * c + 8)
                sum_columns(pe, acc0[:, c, :], 7, 8 * c).then_inc(column_sums, 1)

        def ada_first_dve(dve, order):
            dve.wait_ge(column_sums, 2)
            for j in range(2):
                order(dve.tensor_tensor(mods[:, j, :], bank[7][:, 8 * j:8 * j + 8],
                                        col("b_ada", 8 * j, 8), ALU.add))
            dve.scalar_tensor_tensor(out=pre_scale[:, 0, :], in0=mods[:, 1, :], scalar=1.0,
                                     in1=col("g_pre", 0, 8), op0=ALU.add,
                                     op1=ALU.mult).then_inc(mods_done, 1)

        def gate_pe(pe, r, part, banks, second_wait=None):
            pe.wait_ge(ada_used, (ADA_GATE_1, ADA_GATE_2, ADA_GATE_2 + KT)[r])
            for half, b in enumerate(banks):
                if half and second_wait:
                    pe.wait_ge(*second_wait)
                pe.matmul(bank[b][:, :], ones[:, :], part[:, half * 512:half * 512 + 512],
                          start=True, stop=True).then_inc(gate_sums, 1)

        def gate_dve(dve, r, banks, order):
            dve.wait_ge(gain_loaded, (32, 32, 48)[r])
            for half, b in enumerate(banks):
                dve.wait_ge(gate_sums, 2 * r + half + 1)
                row = gate_rows[:, r, half * 512:half * 512 + 512]
                order(dve.scalar_tensor_tensor(out=row, in0=bank[b][:, :], scalar=1.0 if r == 1 else 0.5,
                                               in1=row, op0=ALU.mult, op1=ALU.mult))

        def ada_middle_pe(pe):
            pe.wait_ge(ada_used, ADA_GATE_1)
            pe.wait_ge(b_evacuated, 2)
            for j in range(4):
                sum_columns(pe, acc[:, 1 + j, :], 6, 8 * j).then_inc(column_sums, 1)
            gate_pe(pe, 0, acc[:, 0, :], (7, 6), second_wait=(mods_done, 2))

        def ada_middle_dve(dve, order):
            dve.wait_ge(column_sums, 6)
            for j in range(4):
                order(dve.tensor_tensor(mods[:, 2 + j, :], bank[6][:, 8 * j:8 * j + 8],
                                        col("b_ada", 8 * ADA_MIDDLE[1 + j], 8), ALU.add))
            order(dve.scalar_tensor_tensor(out=pre_scale[:, 1, :], in0=mods[:, 3, :], scalar=1.0,
                                           in1=col("g_pre", 8, 8), op0=ALU.add, op1=ALU.mult))
            dve.scalar_tensor_tensor(out=pre_scale[:, 2, :], in0=mods[:, 5, :], scalar=1.0,
                                     in1=col("g_pre", 16, 8), op0=ALU.add,
                                     op1=ALU.mult).then_inc(mods_done, 1)
            gate_dve(dve, 0, (7, 6), order)

        def start_gate(pool, order, dst, r):
            order(pool.memset(dst, 0.0))
            pool.dma_start(dst[0:1, :], rows[r:r + 1, :]).then_inc(acc_ready, 16)

        def load_gain(pool, r):
            pool.dma_start(gate_rows[:, r, :], rows[3 + r:4 + r, :].partition_broadcast(P)).then_inc(
                gain_loaded, 16)

        def ada_middle_pool(pool, order):
            pool.wait_ge(h_lo_done, KT)
            order(pool.memset(acc[:, 1:, :], 0.0))
            start_gate(pool, order, acc[:, 0, :], 0)

        def load_gate_1(pool, lo, hi):
            for k in range(lo, hi):
                slot = k % ADA_RING
                pool.wait_ge(ada_used, ADA_GATE_1 + max(k - (ADA_RING - 1), 0))
                pool.dma_start(ada_ring[:, slot, :], ada[ADA_GATE_1 + k]).then_inc(gate_1_loaded[slot], 16)

        def gate_rows_pool(pool, order):
            pool.wait_ge(b_evacuated, 2)
            load_gain(pool, 0)
            load_gain(pool, 1)
            start_gate(pool, order, acc_gate_1, 1)
            load_gate_1(pool, 0, ADA_RING)

        def gate_2_pool(pool, order):
            pool.wait_ge(x_done, 8)
            load_gain(pool, 2)
            start_gate(pool, order, acc_gate_2, 2)
            with pool.Fori(0, KT) as i:
                pool.wait_ge(ada_used, ADA_GATE_2 + i)
                pool.dma_start(late_panel, ada[ADA_GATE_2 + i]).then_inc(late_loaded, 16)

        DT, XR, YI, T0, T1, T2, SIN, SINH, TANH, REC, RAD, EM1, COSM1, COS, LR, LI, CR, CI, INV = range(19)
        angles_ready = sem("angles_ready")
        angles_done = sem("angles_done")
        params_done = sem("params_done")
        ssm_loaded = sem("ssm_loaded")
        b_ready = sem("b_ready")
        b_in_psum = sem("b_in_psum")
        b_evacuated = sem("b_evacuated")
        rot_ready = sem("rot_ready")
        c_rows_ready = sem("c_rows_ready")

        def pr(i):
            return par[:, i, :]

        def round_off(dve, order, arg, k, turns, hi, lo):
            order(dve.tensor_scalar(k, arg, turns, MAGIC, ALU.mult, ALU.add))
            order(dve.tensor_scalar(k, k, -MAGIC, None, ALU.add))
            order(dve.scalar_tensor_tensor(out=arg, in0=k, scalar=-hi, in1=arg, op0=ALU.mult, op1=ALU.add))
            order(dve.scalar_tensor_tensor(out=arg, in0=k, scalar=-lo, in1=arg, op0=ALU.mult, op1=ALU.add))

        def params_dve(dve, order):
            order(dve.tensor_copy(pr(T0), col("log_step", 0, 16)))
            round_off(dve, order, pr(T0), pr(T1), 1.0 / math.log(2.0), LN2_HI, LN2_LO)
            order(dve.tensor_scalar(pr(T2), pr(T0), 1.0 / 40320, None, ALU.mult))
            for n in (7, 6, 5, 4, 3, 2, 1):
                order(dve.scalar_tensor_tensor(out=pr(T2), in0=pr(T2), scalar=1.0 / math.factorial(n),
                                               in1=pr(T0), op0=ALU.add, op1=ALU.mult))
            order(dve.tensor_scalar(pr(T1), pr(T1), -126.0, 127.0, ALU.max, ALU.min))
            order(dve.tensor_scalar(pr(DT).bitcast(I32), pr(T1), 127.0, 8388608.0, ALU.add, ALU.mult))
            order(dve.scalar_tensor_tensor(out=pr(DT), in0=pr(T2), scalar=1.0, in1=pr(DT),
                                           op0=ALU.add, op1=ALU.mult))
            order(dve.tensor_tensor(pr(XR), pr(DT), col("a_re", 0, 16), ALU.mult))
            order(dve.tensor_tensor(pr(YI), pr(DT), col("a_im", 0, 16), ALU.mult))
            round_off(dve, order, pr(YI), pr(T1), 1.0 / TWO_PI, TWO_PI_HI, TWO_PI_LO)
            dve.tensor_scalar(pr(YI), pr(YI), PI_BELOW, -PI_BELOW, ALU.min,
                              ALU.max).then_inc(angles_ready, 1)
            dve.wait_ge(angles_done, 3)
            order(dve.tensor_scalar(pr(REC), pr(TANH), -1.0, 1.0, ALU.mult, ALU.add))
            order(dve.reciprocal(pr(REC), pr(REC)))
            order(dve.scalar_tensor_tensor(out=pr(RAD), in0=pr(TANH), scalar=1.0, in1=pr(REC),
                                           op0=ALU.add, op1=ALU.mult))
            order(dve.scalar_tensor_tensor(out=pr(EM1), in0=pr(TANH), scalar=2.0, in1=pr(REC),
                                           op0=ALU.mult, op1=ALU.mult))
            order(dve.scalar_tensor_tensor(out=pr(COSM1), in0=pr(SINH), scalar=-2.0, in1=pr(SINH),
                                           op0=ALU.mult, op1=ALU.mult))
            order(dve.tensor_scalar(pr(COS), pr(COSM1), 1.0, None, ALU.add))
            order(dve.tensor_tensor(pr(LR), pr(EM1), pr(COS), ALU.mult))
            order(dve.tensor_tensor(pr(LR), pr(LR), pr(COSM1), ALU.add))
            order(dve.tensor_tensor(pr(LI), pr(RAD), pr(SIN), ALU.mult))
            are, aim = col("a_re", 0, 16), col("a_im", 0, 16)
            order(dve.tensor_tensor(pr(T0), are, are, ALU.mult))
            order(dve.tensor_tensor(pr(T1), aim, aim, ALU.mult))
            order(dve.tensor_tensor(pr(INV), pr(T0), pr(T1), ALU.add))
            order(dve.reciprocal(pr(INV), pr(INV)))
            order(dve.tensor_tensor(pr(T0), pr(LR), are, ALU.mult))
            order(dve.tensor_tensor(pr(T1), pr(LI), aim, ALU.mult))
            order(dve.tensor_tensor(pr(T0), pr(T0), pr(T1), ALU.add))
            order(dve.tensor_tensor(pr(CR), pr(T0), pr(INV), ALU.mult))
            order(dve.tensor_tensor(pr(T0), pr(LI), are, ALU.mult))
            order(dve.tensor_tensor(pr(T1), pr(LR), aim, ALU.mult))
            order(dve.tensor_tensor(pr(T0), pr(T0), pr(T1), ALU.subtract))
            dve.tensor_tensor(pr(CI), pr(T0), pr(INV), ALU.mult).then_inc(params_done, 1)

        def params_act(act):
            act.wait_ge(angles_ready, 1)
            act.activation(pr(SIN), pr(YI), ACT.Sin).then_inc(angles_done, 1)
            act.activation(pr(SINH), pr(YI), ACT.Sin, scale=0.5).then_inc(angles_done, 1)
            act.activation(pr(TANH), pr(XR), ACT.Tanh, scale=0.5).then_inc(angles_done, 1)

        def wide(ap, *shape):
            return ap.unsqueeze(2).to_broadcast([ap.shape[0], 16, shape[0]])

        def params_pool(pool, order):
            pool.wait_ge(params_done, 1)
            pool.wait_ge(spectrum_stored, 32)
            pool.dma_start(ssm_raw[:, :, :], ssm_mats).then_inc(ssm_loaded, 16)
            order(pool.memset(b_rows[:, :, :], 0.0))
            order(pool.memset(c_rows[:, :, :, :], 0.0))
            pool.wait_ge(ssm_loaded, 16)
            B = [ssm_raw[:, j, :].rearrange("p (s h) -> p s h", h=16) for j in range(4)]
            prod = region(12288, 2, 256)
            pa, pb = [prod[:, j, :].rearrange("p (s h) -> p s h", h=16) for j in range(2)]
            for part, (u, v, op) in enumerate(((B[0], B[1], ALU.subtract), (B[1], B[0], ALU.add))):
                order(pool.tensor_tensor(pa, u, wide(pr(CR), 16), ALU.mult))
                order(pool.tensor_tensor(pb, v, wide(pr(CI), 16), ALU.mult))
                dst = b_rows[:, part, :].rearrange("p (s c) -> p s c", c=32)
                for half in range(2):
                    r, c = slice(64 * half, 64 * half + 64), slice(16 * half, 16 * half + 16)
                    order(pool.tensor_tensor(dst[r, :, c], pa[r, :, :], pb[r, :, :], op))
            pool.sem_inc(b_ready, 1)
            for part, (src, sign) in enumerate(((B[2], 1.0), (B[2], -1.0), (B[3], -1.0))):
                for half in range(2):
                    r, c = slice(64 * half, 64 * half + 64), slice(16 * half, 16 * half + 16)
                    order(pool.tensor_scalar(c_rows[r, part, :, c], src[r, :, :], sign, 1.0,
                                             ALU.mult, ALU.mult))
            rc, rs = rot[:, 0, :, :], rot[:, 1, :, :]
            order(pool.memset(rc[:, :, 0:1], 1.0))
            order(pool.memset(rs[:, :, 0:1], 0.0))
            c1, s1 = pr(COS), pr(SIN)
            w = 1
            while w < SEQ:
                tmp = rot_tmp[:, :, 0:w]
                new = slice(w, 2 * w)
                order(pool.tensor_tensor(rc[:, :, new], rc[:, :, 0:w], wide(c1, w), ALU.mult))
                order(pool.tensor_tensor(tmp, rs[:, :, 0:w], wide(s1, w), ALU.mult))
                order(pool.tensor_tensor(rc[:, :, new], rc[:, :, new], tmp, ALU.subtract))
                order(pool.tensor_tensor(rs[:, :, new], rc[:, :, 0:w], wide(s1, w), ALU.mult))
                order(pool.tensor_tensor(tmp, rs[:, :, 0:w], wide(c1, w), ALU.mult))
                order(pool.tensor_tensor(rs[:, :, new], rs[:, :, new], tmp, ALU.add))
                w *= 2
                if w < SEQ:
                    order(pool.tensor_tensor(pr(T0), c1, c1, ALU.mult))
                    order(pool.tensor_tensor(pr(T1), s1, s1, ALU.mult))
                    order(pool.tensor_tensor(pr(T2), c1, s1, ALU.mult))
                    order(pool.tensor_tensor(pr(DT), pr(T0), pr(T1), ALU.subtract))
                    order(pool.tensor_tensor(pr(XR), pr(T2), pr(T2), ALU.add))
                    order(pool.tensor_copy(pr(LR), pr(DT)))
                    order(pool.tensor_copy(pr(LI), pr(XR)))
                    c1, s1 = pr(LR), pr(LI)
            pool.sem_inc(rot_ready, 1)

        def turn_b_pe(pe):
            pe.wait_ge(b_ready, 1)
            for part in range(2):
                for q in range(4):
                    tr = pe.transpose(bank[6 + part][:, q * P:(q + 1) * P],
                                      b_rows[:, part, q * P:(q + 1) * P], ident[:, :])
                tr.then_inc(b_in_psum, 1)

        def turn_b_act(act):
            for part in range(2):
                act.wait_ge(b_in_psum, part + 1)
                act.activation(b_turned[:, part, :, :].rearrange("p q s -> p (q s)"),
                               bank[6 + part][:, :], ACT.Copy).then_inc(b_evacuated, 1)

        spec_loaded = sem("spec_loaded")
        decay_loaded = sem("decay_loaded")
        mlp_product = sem("mlp_product")
        mlp_arg = sem("mlp_arg")
        mlp_sin = sem("mlp_sin")
        taps_product = sem("taps_product")
        decay_done = sem("decay_done")
        taps_done = sem("taps_done")
        tap_squares = sem("tap_squares")
        tap_sums = sem("tap_sums")
        tap_root = sem("tap_root")
        even_odd = sem("even_odd")
        spec_product = sem("spec_product")
        spec_done = sem("spec_done")
        spectrum_stored = sem("spectrum_stored")
        dft = region(11264, 2, 2, SEQ)
        filter_out = region(14336, 2048)
        taps = region(16384, 4, 512)
        decays = region(18432, MT, 1024)
        eo = region(20480, 4, 512)
        spec = region(22528, 4, 512)
        root = region(24576, 512)
        tap_sq = region(25088, 2, 512)
        decay_rows = region(0, 1024)
        mlp = region(13312, 1024)
        feat_t, mlp_ws = mlp[0:33, 0:256], mlp[0:64, 256:448]
        mlp_h, mlp_k = mlp[0:64, 448:704], mlp[0:64, 704:960]

        def spectrum_pe(pe):
            pe.wait_ge(spec_loaded, 16 * 5)
            for layer in range(3):
                if layer:
                    pe.wait_ge(mlp_sin, layer)
                    pe.matmul(bank[7][0:64, 0:SEQ], mlp[0:64, 256 + 64 * layer:320 + 64 * layer],
                              mlp_h, start=True, stop=True).then_inc(mlp_product, 1)
                else:
                    pe.matmul(bank[7][0:64, 0:SEQ], mlp[0:33, 256:320], feat_t,
                              start=True, stop=True).then_inc(mlp_product, 1)
            pe.wait_ge(mlp_sin, 3)
            for o in range(2):
                if o:
                    pe.wait_ge(spec_done, 4)
                for q in range(4):
                    m, d = q // 2, q % 2
                    pe.matmul(bank[q][:, :], mlp_h[:, m * P:(m + 1) * P],
                              filter_out[0:64, o * 1024 + d * 512:o * 1024 + d * 512 + 512],
                              start=True, stop=True).then_inc(taps_product, 1)
                for q in range(4):
                    pe.wait_ge(tap_squares, 4 * o + q + 1)
                    pe.matmul(bank[6][:, :], ones[:, :], tap_sq[:, q % 2, :], start=q == 0,
                              stop=q == 3).then_inc(tap_sums, 1)
                pe.wait_ge(even_odd, 4 * o + 4)
                for f in range(2):
                    for s in range(2):
                        for m in range(MT):
                            mm = pe.matmul(bank[2 * f + s][:, :], dft[:, s, m, f * P:(f + 1) * P],
                                           eo[:, 2 * m + s, :], start=m == 0, stop=m == MT - 1)
                        mm.then_inc(spec_product, 1)

        def spectrum_dve(dve, order, spare):
            for layer in range(3):
                dve.wait_ge(mlp_product, layer + 1)
                order(dve.tensor_scalar(mlp_h, bank[7][0:64, 0:SEQ], C[0:64, COLS["mlp_b"][0] + layer:COLS["mlp_b"][0] + layer + 1],
                                        C[0:64, COLS["sin_freq"][0] + layer:COLS["sin_freq"][0] + layer + 1],
                                        ALU.add, ALU.mult))
                round_off(dve, order, mlp_h, mlp_k, 1.0 / TWO_PI, TWO_PI_HI, TWO_PI_LO)
                dve.tensor_scalar(mlp_h, mlp_h, PI_BELOW, -PI_BELOW, ALU.min,
                                  ALU.max).then_inc(mlp_arg, 1)
                spare()
            for o in range(2):
                for q in range(4):
                    m, d = q // 2, q % 2
                    dve.wait_ge(taps_product, 4 * o + q + 1)
                    dve.wait_ge(decay_done, 2 * o + m + 1)
                    ins = dve.tensor_tensor(taps[:, q, :], bank[q][:, :],
                                            decays[:, m, d * 512:d * 512 + 512], ALU.mult)
                    if q == 1:
                        order(ins)
                        ins = dve.memset(taps[0:1, 1, :], 0.0)
                    ins.then_inc(taps_done, 1)
                    if q % 2:
                        spare()
                dve.wait_ge(taps_done, 4 * o + 4)
                for m in range(MT):
                    for s, op in enumerate((ALU.add, ALU.subtract)):
                        dve.tensor_tensor(eo[:, 2 * m + s, :], taps[:, 2 * m, :], taps[:, 2 * m + 1, :],
                                          op).then_inc(even_odd, 1)
                spare()
                dve.wait_ge(tap_root, o + 1)
                order(dve.reciprocal(root, root))
                if o:
                    dve.wait_ge(spectrum_stored, 16)
                for q in range(4):
                    dve.wait_ge(spec_product, 4 * o + q + 1)
                    dve.tensor_tensor(spec[:, q, :], bank[q][:, :], root, ALU.mult).then_inc(spec_done, 1)
                    if q % 2:
                        spare()

        def spectrum_act(act, order):
            for layer in range(3):
                act.wait_ge(mlp_arg, layer + 1)
                then(act, act.activation(mlp_h, mlp_h, ACT.Sin), mlp_sin, layer + 1)
            for o in range(2):
                act.wait_ge(decay_loaded, 16 * (o + 1))
                order(act.activation(decay_rows, decay_rows, ACT.Abs))
                if o:
                    act.wait_ge(taps_done, 4)
                for m in range(MT):
                    at = COLS["neg_t"][0] + m
                    act.activation(decays[:, m, :], decay_rows, ACT.Exp,
                                   scale=C[:, at:at + 1]).then_inc(decay_done, 1)
                if o == 0:
                    act.wait_ge(decay_done, 2)
                    act.dma_start(decay_rows, decay[1:2, :].partition_broadcast(P)).then_inc(decay_loaded, 16)
                for q in range(4):
                    act.wait_ge(taps_done, 4 * o + q + 1)
                    if 4 * o + q >= 2:
                        act.wait_ge(tap_sums, 4 * o + q - 1)
                    act.activation(tap_sq[:, q % 2, :], taps[:, q, :], ACT.Square).then_inc(tap_squares, 1)
                act.wait_ge(tap_sums, 4 * o + 4)
                if o:
                    act.wait_ge(spec_done, 4)
                act.activation(root, bank[6][:, :], ACT.Sqrt).then_inc(tap_root, 1)

        def spectrum_pool(pool):
            for o in range(2):
                pool.wait_ge(spec_done, 4 * o + 4)
                pool.dma_start(spectrum[o], spec[:, :, :]).then_inc(spectrum_stored, 16)
        u_t = region(4096, 4, SEQ)
        q_t = region(5120, 4, SEQ)
        y32 = region(5120, 4, SEQ)
        p_turned = region(6144, 2, 384)
        attn = region(6912, 2, 512)
        turned_back = region(7936, 2, SEQ)
        states = (region(8448, 2, SEQ), region(3456, 2, SEQ))
        rot_out = region(8960, 2, 4, SEQ)
        scores = region(0, 8, 384)
        near_sb = region(3072, 384)
        k_t = region(25088, SEQ)
        v_t = region(25344, SEQ)
        v_tok = region(25600, MT, P)
        sink_row = stat[:, 24:32]
        gate_in = region(0, 4, SEQ)
        rms_row = region(1024, SEQ)
        y_squares = region(1280, 2, SEQ)
        max3 = region(11008, 8, 3)
        m1_small = region(11040, 6, 16)
        NEGMAX, SUMS, SINK, RDEN = range(4)

        m1_product = sem("m1_product")
        m1_evac = sem("m1_evac")
        v_turned = sem("v_turned")
        v_ready = sem("v_ready")
        near_loaded = sem("near_loaded")
        sc_product = sem("sc_product")
        sc_biased = sem("sc_biased")
        sc_max = sem("sc_max")
        sc_exp = sem("sc_exp")
        p_in_psum = sem("p_in_psum")
        p_evac = sem("p_evac")
        pv_done = sem("pv_done")
        den_done = sem("den_done")
        attn_done = sem("attn_done")
        attn_squares = sem("attn_squares")
        attn_rstd = sem("attn_rstd")
        attn_scaled = sem("attn_scaled")
        attn_turned = sem("attn_turned")
        m_evac = sem("m_evac")
        m_hi = sem("m_hi")
        m_lo = sem("m_lo")
        bu_done = sem("bu_done")
        bu_read = sem("bu_read")
        states_done = sem("states_done")
        rot_done = sem("rot_done")
        y_done = sem("y_done")
        y_skip = sem("y_skip")
        gelu_done = sem("gelu_done")
        y_hi = sem("y_hi")
        y_lo = sem("y_lo")
        glu_done = sem("glu_done")
        sig_done = sem("sig_done")
        gated = sem("gated")
        gsq_done = sem("gsq_done")
        gsum_done = sem("gsum_done")
        root_done = sem("root_done")
        M1 = FIRST[("mix1", 0)]

        def m1_projection_pe(pe):
            for j in range(10):
                if j >= 2:
                    pe.wait_ge(m1_evac, j - 1)
                channel_product(pe, up_bank(j)[:, 0:SEQ], M1 + j, norm=1 if j == 0 else None)

        def attention_pe(pe, head):
            kv, j = head // 4, head % 4
            r = slice(64 * kv, 64 * kv + 64)
            b = bank[4 + head % 2]
            if head >= 2:
                pe.wait_ge(sc_biased, head - 1)
            pe.matmul(b[:, 0:P], q_t[r, j, 0:P], k_t[r, 0:P], start=True, stop=True)
            pe.matmul(b[:, P:3 * P], q_t[r, j, P:SEQ], k_t[r, :], start=True,
                      stop=True).then_inc(sc_product, 1)

        def attention_values_pe(pe, head):
            pe.wait_ge(sc_exp, 2 * head + 2)
            b = bank[4 + head % 2]
            if head >= 2:
                pe.wait_ge(p_evac, head - 1)
            for c in range(3):
                tr = pe.transpose(b[:, c * P:(c + 1) * P], scores[:, head, c * P:(c + 1) * P], ident[:, :])
            tr.then_inc(p_in_psum, 1)

        def attention_out_pe(pe, head):
            kv = head // 4
            pe.wait_ge(p_evac, head + 1)
            v = slice(64 * kv, 64 * kv + 64)
            o = slice(64 * head, 64 * head + 64)
            p = p_turned[:, head % 2, :]
            pe.matmul(bank[0][:, o], p[:, 0:P], v_tok[:, 0, v], start=True, stop=True)
            pe.matmul(bank[1][:, o], p[:, P:2 * P], v_tok[:, 0, v], start=True, stop=False)
            pe.matmul(bank[1][:, o], p[:, 2 * P:3 * P], v_tok[:, 1, v], start=False,
                      stop=True).then_inc(pv_done, 1)

        def input_pe(pe, s):
            q, r = s // 4, slice(32 * (s % 4), 32 * (s % 4) + 32)
            if s >= 2:
                pe.wait_ge(bu_read, s - 1)
            for part in range(2):
                mm = pe.matmul(bank[2 + s % 2][:, part * SEQ:(part + 1) * SEQ], b_turned[r, part, q, :],
                               u_t[r, q, :], start=True, stop=True)
            mm.then_inc(bu_done, 1)

        def output_pe(pe, s):
            q, r = s // 4, slice(32 * (s % 4), 32 * (s % 4) + 32)
            pe.wait_ge(rot_done, 2 * s + 2)
            o = bank[6 + q // 2][r, (q % 2) * SEQ:(q % 2 + 1) * SEQ]
            for n, (part, term) in enumerate(((0, 0), (2, 1), (2, 2), (1, 3))):
                mm = pe.matmul(o, c_rows[:, part, s, :], rot_out[:, s % 2, term, :], start=n == 0,
                               stop=n == 3)
            mm.then_inc(y_done, 1)

        def mix1_pe(pe):
            m1_projection_pe(pe)
            gate_pe(pe, 1, acc_gate_1, (0, 1))
            pe.wait_ge(m1_evac, 10)
            for m in range(MT):
                tr = pe.transpose(bank[4][:, m * P:(m + 1) * P], v_t[:, m * P:(m + 1) * P], ident[:, :])
            tr.then_inc(v_turned, 1)
            pe.wait_ge(rot_ready, 1)
            input_pe(pe, 0)
            input_pe(pe, 1)
            pe.wait_ge(v_ready, 1)
            for s in range(STATE_TILES):
                if s < 8:
                    attention_pe(pe, s)
                if 8 <= s < 12:
                    for head in (2 * s - 16, 2 * s - 15):
                        attention_values_pe(pe, head)
                if 9 <= s < 13:
                    for head in (2 * s - 18, 2 * s - 17):
                        attention_out_pe(pe, head)
                if s + 2 < STATE_TILES:
                    input_pe(pe, s + 2)
                if s:
                    output_pe(pe, s - 1)
            turn_attention_pe(pe)
            output_pe(pe, STATE_TILES - 1)
            pe.wait_ge(y_lo, 4)
            for n in range(4):
                channel_product(pe, bank[6 + n // 2][:, (n % 2) * SEQ:(n % 2 + 1) * SEQ],
                                M1 + 10 + n // 2, k_tiles=4, at=(n % 2) * 512, k0=4, used=n % 2 == 1)

            def out_product(k):
                pe.wait_ge(m_lo, k // 2 + 1)
                token_product(pe, M1 + 12 + k, h_hi[:, k, :], h_lo[:, k, :], k == 0, k == KT - 1)

            out_product(0)
            out_product(1)
            for n in range(4):
                pe.wait_ge(gsq_done, n + 1)
                pe.matmul(bank[4][:, 0:SEQ], ones[:, :], y_squares[:, n % 2, :], start=n == 0,
                          stop=n == 3).then_inc(gsum_done, 1)
            for k in range(2, KT):
                out_product(k)

        def turn_attention_pe(pe):
            pe.wait_ge(attn_scaled, 2)
            for k in range(4):
                for m in range(MT):
                    tr = pe.transpose(bank[4 + k // 2][:, (k % 2) * SEQ + m * P:(k % 2) * SEQ + m * P + P],
                                      attn[:, m, k * P:(k + 1) * P], ident[:, :])
                if k % 2:
                    tr.then_inc(attn_turned, 1)

        def mix1_act(act, order):
            for j in range(10):
                split_hi(act, M1 + 3 + j)
                act.wait_ge(panel_used, M1 + j + 1)
                src = up_bank(j)[:, 0:SEQ]
                if j < 4:
                    ins = act.activation(u_t[:, j, :], src, ACT.Copy)
                elif j < 8:
                    ins = act.activation(q_t[:, j - 4, :], src, ACT.Copy, scale=HD ** -0.5)
                else:
                    ins = act.activation(k_t if j == 8 else v_t, src, ACT.Copy)
                ins.then_inc(m1_evac, 1)
            act_panels(act, M1 + 13, 3)
            act.wait_ge(v_turned, 1)
            act.activation(v_tok[:, :, :].rearrange("p m c -> p (m c)"), bank[4][:, 0:SEQ],
                           ACT.Copy).then_inc(v_ready, 1)
            act.wait_ge(sc_max, 3)
            order(act.activation(m1_small[:, SINK, :], m1_small[:, SINK, :], ACT.Exp))
            for head in range(8):
                for b, c in ((0, slice(0, P)), (1, slice(P, 3 * P))):
                    i = 2 * head + b
                    act.activation(scores[:, head, c], scores[:, head, c], ACT.Exp,
                                   bias=m1_small[:, NEGMAX, i:i + 1],
                                   accum_out=m1_small[:, SUMS, i:i + 1]).then_inc(sc_exp, 1)
            for head in range(8):
                act.wait_ge(p_in_psum, head + 1)
                if head >= 2:
                    act.wait_ge(pv_done, head - 1)
                act.activation(p_turned[:, head % 2, :], bank[4 + head % 2][:, 0:384],
                               ACT.Copy).then_inc(p_evac, 1)
            for m in range(MT):
                act.wait_ge(attn_done, m + 1)
                act.activation(region(1024 * m, 512), attn[:, m, :], ACT.Square,
                               accum_out=stat[:, 32 + m:33 + m]).then_inc(attn_squares, 1)
            for k in range(4):
                act.wait_ge(attn_turned, k // 2 + 1)
                act.activation(h32[:, k, :], bank[4 + k // 2][:, (k % 2) * SEQ:(k % 2 + 1) * SEQ],
                               ACT.Copy, scale=col("g_attn", k)).then_inc(m_evac, 1)
            for b in range(2):
                act.wait_ge(m_evac, 2 * b + 2)
                act.activation(h_hi[:, 2 * b:2 * b + 2, :], h32[:, 2 * b:2 * b + 2, :],
                               ACT.Copy).then_inc(m_hi, 1)
            for b in range(2):
                act.wait_ge(y_skip, 2 * b + 2)
                r = slice(2 * b, 2 * b + 2)
                then(act, act.activation(y32[:, r, :], y32[:, r, :], ACT.Gelu_apprx_tanh), gelu_done, b + 1)
                act.activation(h_hi[:, 4 + 2 * b:6 + 2 * b, :], y32[:, r, :], ACT.Copy).then_inc(y_hi, 1)
            for n in range(4):
                act.wait_ge(panel_used, M1 + 11 + n // 2)
                act.activation(gate_in[:, n, :], bank[6 + n // 2][:, (n % 2) * SEQ:(n % 2 + 1) * SEQ],
                               ACT.Sigmoid, bias=col("b_glu", n)).then_inc(sig_done, 1)
            act_panels(act, M1 + 16, 2)
            for n in range(4):
                act.wait_ge(gated, n + 1)
                if n >= 2:
                    act.wait_ge(gsum_done, n - 1)
                act.activation(y_squares[:, n % 2, :], gate_in[:, n, :], ACT.Square).then_inc(gsq_done, 1)
            act.wait_ge(gsum_done, 4)
            order(act.activation(rms_row, bank[4][:, 0:SEQ], ACT.Copy, scale=1.0 / 512, bias=EPS))
            act.activation(rms_row, rms_row, ACT.Sqrt).then_inc(root_done, 1)
            act_panels(act, M1 + 18, 2)
            for b in range(2, 4):
                act.wait_ge(m_evac, 2 * b + 2)
                act.activation(h_hi[:, 2 * b:2 * b + 2, :], h32[:, 2 * b:2 * b + 2, :],
                               ACT.Copy).then_inc(m_hi, 1)
            act_panels(act, M1 + 20, 3)

        def mix1_pool(pool, order):
            pool.wait_ge(x_done, 4)
            load_gate_1(pool, ADA_RING, KT)
            pool.dma_start(sink_row, sinks.partition_broadcast(P)).then_inc(near_loaded, 16)
            pool.wait_ge(h_lo_done, 2 * KT)
            pool.dma_start(near_sb, near).then_inc(near_loaded, 16)
            for s in range(STATE_TILES):
                pool.wait_ge(states_done, 2 * s + 2)
                if s >= 2:
                    pool.wait_ge(y_done, s - 1)
                z = states[s % 2]
                for part in range(2):
                    r = rot[:, part, s, :].unsqueeze(1).to_broadcast([P, 2, SEQ])
                    pool.tensor_tensor(rot_out[:, s % 2, 2 * part:2 * part + 2, :], z, r,
                                       ALU.mult).then_inc(rot_done, 1)
                if s == 13:
                    for m in range(MT):
                        pool.wait_ge(attn_squares, m + 1)
                        ss = stat[:, 32 + m:33 + m]
                        order(pool.tensor_scalar(ss, ss, 1.0 / 512, EPS, ALU.mult, ALU.add))
                        pool.tensor_tensor(ss, ss, stat[:, MINUS_HALF:MINUS_HALF + 1],
                                           ALU.pow).then_inc(attn_rstd, 1)

        def states_dve(dve, order, s):
            w = bank[2 + s % 2][:, :].rearrange("p (i t) -> p i t", i=2)
            a, x = turned_back, states[s % 2]
            dve.wait_ge(bu_done, s + 1)
            if s:
                dve.wait_ge(states_done, 2 * s)
            if s >= 2:
                dve.wait_ge(rot_done, 2 * s - 2)
            for part, dst in ((0, a), (1, x)):
                r = rot[:, part, s, :].unsqueeze(1).to_broadcast([P, 2, SEQ])
                ins = dve.tensor_tensor(dst, w, r, ALU.mult)
                if part:
                    then(dve, ins, bu_read, s + 1)
                else:
                    order(ins)
            order(dve.tensor_tensor(a[:, 0, :], a[:, 0, :], x[:, 1, :], ALU.add))
            order(dve.tensor_tensor(a[:, 1, :], a[:, 1, :], x[:, 0, :], ALU.subtract))
            r = par[:, RAD, s:s + 1].to_broadcast([P, SEQ])
            for part in range(2):
                dve.tensor_tensor_scan(x[:, part, :], r, a[:, part, :], 0.0, ALU.mult,
                                       ALU.add).then_inc(states_done, 1)

        def mix1_dve(dve, order):
            dve.wait_ge(acc_ready, 32)
            for j in range(13):
                split_lo(dve, M1 + 3 + j)
                if j < KT:
                    ada_add_gate_1(dve, j)
            gate_dve(dve, 1, (0, 1), order)
            dve.wait_ge(near_loaded, 32)
            dve.wait_ge(rot_ready, 1)

            def bias(head):
                dve.wait_ge(sc_product, head + 1)
                then(dve, dve.scalar_tensor_tensor(out=scores[:, head, :], in0=near_sb,
                                                   scalar=2.0 ** -(head + 1),
                                                   in1=bank[4 + head % 2][:, 0:384], op0=ALU.mult,
                                                   op1=ALU.add), sc_biased, head + 1)
                order(dve.tensor_reduce(max3[:, head, :],
                                        scores[:, head, :].rearrange("p (b k) -> p b k", b=3),
                                        AX.X, ALU.max))

            def maxima():
                mx = m1_small[:, NEGMAX, :].rearrange("p (h b) -> p h b", b=2)
                sx = m1_small[:, SINK, :].rearrange("p (h b) -> p h b", b=2)
                order(dve.tensor_tensor(max3[:, :, 1], max3[:, :, 1], max3[:, :, 2], ALU.max))
                for b in range(2):
                    order(dve.tensor_tensor(mx[:, :, b], max3[:, :, b], sink_row, ALU.max))
                for b in range(2):
                    dve.tensor_tensor(sx[:, :, b], sink_row, mx[:, :, b], ALU.subtract).then_inc(sc_max, 1)
                dve.wait_ge(sc_max, 2)
                dve.tensor_scalar(m1_small[:, NEGMAX, :], m1_small[:, NEGMAX, :], -1.0, None,
                                  ALU.mult).then_inc(sc_max, 1)

            def attention_out():
                dve.wait_ge(sc_exp, 16)
                order(dve.tensor_tensor(m1_small[:, RDEN, :], m1_small[:, SUMS, :], m1_small[:, SINK, :],
                                        ALU.add))
                order(dve.reciprocal(m1_small[:, RDEN, :], m1_small[:, RDEN, :]))
                dve.wait_ge(pv_done, 8)
                rd = m1_small[:, RDEN, :].rearrange("p (h b) -> p h b", b=2)
                for b in range(2):
                    r = rd[:, :, b].unsqueeze(2).to_broadcast([P, 8, HD])
                    dve.tensor_tensor(attn[:, b, :].rearrange("p (h d) -> p h d", d=HD),
                                      bank[b][:, :].rearrange("p (h d) -> p h d", d=HD), r,
                                      ALU.mult).then_inc(attn_done, 1)

            def skip(b):
                dve.wait_ge(y_done, 8 * b + 8)
                if b == 0:
                    dve.wait_ge(sc_product, 8)
                for j in range(2):
                    q = 2 * b + j
                    dve.scalar_tensor_tensor(out=y32[:, q, :], in0=u_t[:, q, :], scalar=col("ssm_d", q),
                                             in1=bank[6 + b][:, j * SEQ:(j + 1) * SEQ], op0=ALU.mult,
                                             op1=ALU.add).then_inc(y_skip, 1)

            for s in range(STATE_TILES):
                states_dve(dve, order, s)
                if s < 8:
                    bias(s)
                    if s == 7:
                        maxima()
                if s == 12:
                    attention_out()
                if s == 13:
                    skip(0)
                if s == 14:
                    for m in range(MT):
                        dve.wait_ge(attn_rstd, m + 1)
                        dve.tensor_scalar(attn[:, m, :], attn[:, m, :], stat[:, 32 + m:33 + m], None,
                                          ALU.mult).then_inc(attn_scaled, 1)
            skip(1)
            for b in range(2):
                dve.wait_ge(m_hi, b + 1)
                r = slice(2 * b, 2 * b + 2)
                dve.tensor_tensor(h_lo[:, r, :], h32[:, r, :], h_hi[:, r, :].bitcast(F32),
                                  ALU.subtract).then_inc(m_lo, 1)
            for b in range(2):
                for j in range(2):
                    dve.wait_ge(y_hi, b + 1)
                    k = 4 + 2 * b + j
                    dve.tensor_tensor(h_lo[:, k, :], y32[:, 2 * b + j, :], h_hi[:, k, :].bitcast(F32),
                                      ALU.subtract).then_inc(y_lo, 1)
            for n in range(4):
                dve.wait_ge(sig_done, n + 1)
                dve.tensor_tensor(gate_in[:, n, :], gate_in[:, n, :], y32[:, n, :],
                                  ALU.mult).then_inc(gated, 1)
            dve_panels(dve, M1 + 16, 2)
            dve.wait_ge(root_done, 1)
            order(dve.reciprocal(rms_row, rms_row))
            for n in range(4):
                dve.scalar_tensor_tensor(out=h32[:, 4 + n, :], in0=gate_in[:, n, :],
                                         scalar=col("g_ssm", n), in1=rms_row, op0=ALU.mult,
                                         op1=ALU.mult).then_inc(m_evac, 1)
            dve_panels(dve, M1 + 18, 2)
            for b in range(2, 4):
                dve.wait_ge(m_hi, b + 1)
                r = slice(2 * b, 2 * b + 2)
                dve.tensor_tensor(h_lo[:, r, :], h32[:, r, :], h_hi[:, r, :].bitcast(F32),
                                  ALU.subtract).then_inc(m_lo, 1)
            dve_panels(dve, M1 + 20, 3)

        forward = region(4096, 2, MT, SEQ)
        inverse = region(5120, 2, MT, SEQ)
        averages = region(6144, 4 * MT, SEQ)
        pool_ws = region(8192, 4, P)
        filters = region(8704, 8, 512)
        a_tok = region(12800, MT, 512)
        averaged = region(13824, 4, SEQ)
        conv = region(14848, 12, SEQ)
        z_tok = region(17920, MT, 512)
        product = region(18944, 4, 512)
        terms = region(20992, 4, 512)
        z_sum = region(23040, 2, SEQ)

        m2_loaded = sem("m2_loaded")
        a_evac = sem("a_evac")
        conv_centre = sem("conv_centre")
        conv_done = sem("conv_done")
        averages_done = sem("averages_done")
        averages_evac = sem("averages_evac")
        grouped_done = sem("grouped_done")
        z_turned = sem("z_turned")
        z_evac = sem("z_evac")
        z_spectrum = sem("z_spectrum")
        spectra_product = sem("spectra_product")
        z_back = sem("z_back")
        z_done = sem("z_done")
        m2_evac = sem("m2_evac")
        m2_hi = sem("m2_hi")
        m2_lo = sem("m2_lo")
        M2 = FIRST[("mix2", 0)]

        def mix2_loads(pool):
            pool.wait_ge(x_done, 12)
            pool.dma_start(forward, pool_mats[4:6].rearrange("i p m t -> p i m t")).then_inc(m2_loaded, 16)
            pool.dma_start(inverse, pool_mats[6:8].rearrange("i p m t -> p i m t")).then_inc(m2_loaded, 16)
            pool.dma_start(averages.rearrange("p (i m) t -> p i m t", m=MT),
                           pool_mats[0:4].rearrange("i p m t -> p i m t")).then_inc(m2_loaded, 16)
            pool.dma_start(pool_ws, pool_w).then_inc(m2_loaded, 16)
            pool.dma_start(filters.rearrange("p (o q) c -> p o q c", o=2),
                           spectrum.rearrange("o p q c -> p o q c")).then_inc(m2_loaded, 16)

        def forward_pe(pe, first_bank, o):
            pe.wait_ge(z_evac, MT * (o + 1))
            for f in range(2):
                for s in range(2):
                    for m in range(MT):
                        mm = pe.matmul(bank[first_bank + 2 * f + s][:, :],
                                       forward[:, s, m, f * P:(f + 1) * P], z_tok[:, m, :],
                                       start=m == 0, stop=m == MT - 1)
                    mm.then_inc(z_spectrum, 1)

        def inverse_pe(pe, o):
            pe.wait_ge(spectra_product, 4 * o + 4)
            for c in range(4):
                for f in range(2):
                    for s in range(2):
                        mm = pe.matmul(bank[6 + c // 2][:, (c % 2) * SEQ:(c % 2 + 1) * SEQ],
                                       product[:, 2 * f + s, c * P:(c + 1) * P], inverse[:, s, f, :],
                                       start=f + s == 0, stop=f + s == 2)
                mm.then_inc(z_back, 1)

        def turn_z_pe(pe, first_bank):
            for m in range(MT):
                for c in range(4):
                    tr = pe.transpose(bank[first_bank + m][:, c * P:(c + 1) * P],
                                      conv[:, c, m * P:(m + 1) * P], ident[:, :])
                tr.then_inc(z_turned, 1)

        def mix2_pe(pe):
            for j in range(4):
                g = M2 + j
                pe.wait_ge(lo_ready, g + 1)
                for half in range(2):
                    k, w = 2 * j + half, slice(512 * half, 512 * half + 512)
                    pe.wait_ge(h_lo_done, KT * 4 + k + 1)
                    for m in range(MT):
                        t = slice(m * P, (m + 1) * P)
                        mm = product3(pe, bank[m][:, :], w_hi[:, g % RING, w], w_lo[:, g % RING, w],
                                      h_hi[:, k, t], h_lo[:, k, t], k == 0, k == KT - 1,
                                      weights_move=True)
                mm.then_inc(panel_used, 1)

            def parts(lo, hi):
                for j in range(lo, hi):
                    if j >= 2:
                        pe.wait_ge(conv_done, j - 1)
                    channel_product(pe, bank[4 + j % 2][:, 0:SEQ], M2 + 4 + j)

            parts(0, 4)
            pe.wait_ge(m2_loaded, 16 * 5)
            pe.wait_ge(a_evac, 2)
            for g in range(4):
                for m in range(MT):
                    mm = pe.matmul(bank[6 + g // 2][:, (g % 2) * SEQ:(g % 2 + 1) * SEQ],
                                   a_tok[:, m, g * P:(g + 1) * P], averages[:, MT * g + m, :],
                                   start=m == 0, stop=m == MT - 1)
                if g % 2:
                    mm.then_inc(averages_done, 1)
            parts(4, 6)
            turn_z_pe(pe, 2)
            parts(6, 8)
            for g in range(4):
                if g % 2 == 0:
                    pe.wait_ge(averages_evac, g // 2 + 1)
                mm = pe.matmul(bank[6 + g // 2][:, (g % 2) * SEQ:(g % 2 + 1) * SEQ], pool_ws[:, g, :],
                               averaged[:, g, :], start=True, stop=True)
                if g % 2:
                    mm.then_inc(grouped_done, 1)
            forward_pe(pe, 0, 0)
            parts(8, 12)
            pe.wait_ge(m2_evac, 4)
            inverse_pe(pe, 0)
            pe.wait_ge(conv_done, 12)
            pe.wait_ge(z_done, 4)
            turn_z_pe(pe, 4)
            forward_pe(pe, 4, 1)
            for k in range(KT):
                if k == 4:
                    inverse_pe(pe, 1)
                pe.wait_ge(m2_lo, k // 2 + 1)
                token_product(pe, M2 + 16 + k, h_hi[:, k, :], h_lo[:, k, :], k == 0, k == KT - 1)

        def mix2_act(act, order):
            def centre(j):
                act.wait_ge(panel_used, M2 + 5 + j)
                tile = (j + 8) % 12
                act.activation(conv[:, j, :], bank[4 + j % 2][:, 0:SEQ], ACT.Identity,
                               scale=col("conv_w", 12 + tile),
                               bias=col("conv_b", tile)).then_inc(conv_centre, 1)

            def evac_z(first_bank, n):
                for m in range(MT):
                    act.wait_ge(z_turned, n + m + 1)
                    act.activation(z_tok[:, m, :], bank[first_bank + m][:, :], ACT.Copy).then_inc(z_evac, 1)

            def high(b):
                r = slice(2 * b, 2 * b + 2)
                act.activation(h_hi[:, r, :], h32[:, r, :], ACT.Copy).then_inc(m2_hi, 1)

            act_panels(act, M2 + 3, 4)
            act.wait_ge(panel_used, M2 + 4)
            for m in range(MT):
                act.activation(a_tok[:, m, :], bank[m][:, :], ACT.Copy).then_inc(a_evac, 1)
            for j in range(12):
                split_hi(act, M2 + 7 + j)
                centre(j)
                if j == 4:
                    for b in range(2):
                        act.wait_ge(averages_done, b + 1)
                        act.activation(averaged[:, 2 * b:2 * b + 2, :].rearrange("p g t -> p (g t)"),
                                       bank[6 + b][:, :], ACT.Copy).then_inc(averages_evac, 1)
                if j == 6:
                    evac_z(2, 0)
            for g in range(4):
                act.wait_ge(grouped_done, g // 2 + 1)
                act.activation(h32[:, g, :], bank[6 + g // 2][:, (g % 2) * SEQ:(g % 2 + 1) * SEQ],
                               ACT.Copy, scale=col("pool_scale", g)).then_inc(m2_evac, 1)
            act_panels(act, M2 + 19, 3)
            for b in range(2):
                act.wait_ge(m2_evac, 2 * b + 2)
                high(b)
            evac_z(4, 2)
            act_panels(act, M2 + 22, 4)
            for b in range(2, 4):
                act.wait_ge(z_done, 2 * b + 2)
                high(b)
            act_panels(act, M2 + 26, 1)

        def mix2_dve(dve, order):
            def taps_of(j):
                dve.wait_ge(conv_centre, j + 1)
                tile = (j + 8) % 12
                src, dst = bank[4 + j % 2], conv[:, j, :]
                order(dve.scalar_tensor_tensor(out=dst[:, 1:SEQ], in0=src[:, 0:SEQ - 1],
                                               scalar=col("conv_w", tile), in1=dst[:, 1:SEQ],
                                               op0=ALU.mult, op1=ALU.add))
                then(dve, dve.scalar_tensor_tensor(out=dst[:, 0:SEQ - 1], in0=src[:, 1:SEQ],
                                                   scalar=col("conv_w", 24 + tile),
                                                   in1=dst[:, 0:SEQ - 1], op0=ALU.mult, op1=ALU.add),
                     conv_done, j + 1)

            def multiply(o, first_bank, f):
                k = filters[:, 4 * o + 2 * f:4 * o + 2 * f + 2, :]
                for s in range(2):
                    dve.wait_ge(z_spectrum, 4 * o + 2 * f + s + 1)
                    z = bank[first_bank + 2 * f + s][:, :].unsqueeze(1).to_broadcast([P, 2, 512])
                    order(dve.tensor_tensor(terms[:, 2 * s:2 * s + 2, :], k, z, ALU.mult))
                dve.tensor_tensor(product[:, 2 * f, :], terms[:, 0, :], terms[:, 3, :],
                                  ALU.subtract).then_inc(spectra_product, 1)
                then(dve, dve.tensor_tensor(product[:, 2 * f + 1, :], terms[:, 1, :], terms[:, 2, :],
                                            ALU.add), spectra_product, 4 * o + 2 * f + 2)

            def gate(o):
                for c in range(4):
                    dve.wait_ge(z_back, 4 * o + c - c % 2 + 2)
                    order(dve.scalar_tensor_tensor(out=z_sum[:, c % 2, :], in0=conv[:, c, :],
                                                   scalar=col("bias", 4 * o + c),
                                                   in1=bank[6 + c // 2][:, (c % 2) * SEQ:(c % 2 + 1) * SEQ],
                                                   op0=ALU.mult, op1=ALU.add))
                    then(dve, dve.tensor_tensor(h32[:, 4 + c, :] if o else conv[:, c, :],
                                                z_sum[:, c % 2, :], conv[:, 4 + 4 * o + c, :],
                                                ALU.mult), z_done, 4 * o + c + 1)

            def low(b):
                dve.wait_ge(m2_hi, b + 1)
                r = slice(2 * b, 2 * b + 2)
                dve.tensor_tensor(h_lo[:, r, :], h32[:, r, :], h_hi[:, r, :].bitcast(F32),
                                  ALU.subtract).then_inc(m2_lo, 1)

            dve_panels(dve, M2 + 3, 4)
            for j in range(8):
                split_lo(dve, M2 + 7 + j)
                taps_of(j)
            dve.wait_ge(m2_loaded, 16 * 5)
            for f in range(2):
                multiply(0, 0, f)
                for j in (8 + 2 * f, 9 + 2 * f):
                    split_lo(dve, M2 + 7 + j)
                    taps_of(j)
            gate(0)
            dve_panels(dve, M2 + 19, 3)
            low(0)
            low(1)
            for f in range(2):
                multiply(1, 4, f)
            dve_panels(dve, M2 + 22, 4)
            gate(1)
            low(2)
            low(3)
            dve_panels(dve, M2 + 26, 1)

        QK = 96
        SCALE = QK ** -0.5
        q_rows = region(4096, MLA_HEADS, SEQ)
        k_rows = region(8192, MLA_HEADS, SEQ)
        values = region(12288, MT, D)
        probs = region(14336, 2, 512)
        probs_by_key = region(15360, 2, 512)
        attended = region(16384, MT, D)
        rope_t = region(18432, 2, SEQ)
        latent = region(18944, 3, SEQ)
        latent_sq = region(19712, 3, SEQ)
        latent_rms = region(20480, 2, SEQ)
        k_turn = region(20992, 2, SEQ)
        q_turn = region(21504, 2, 4, SEQ)
        soft = region(23552, 4, 2 * MLA_HEADS)
        MAX3, NEG3, SUM3, REC3 = range(4)

        rope_loaded = sem("rope_loaded")
        latent_squares = sem("latent_squares")
        latent_sums = sem("latent_sums")
        latent_root = sem("latent_root")
        latent_done = sem("latent_done")
        latent_hi = sem("latent_hi")
        latent_lo = sem("latent_lo")
        k_rope_done = sem("k_rope_done")
        q_evac = sem("q_evac")
        q_rope_read = sem("q_rope_read")
        q_rope_done = sem("q_rope_done")
        kv_act = sem("kv_act")
        kv_dve = sem("kv_dve")
        scored = sem("scored")
        soft_max = sem("soft_max")
        soft_exp = sem("soft_exp")
        probs_turned = sem("probs_turned")
        probs_evac = sem("probs_evac")
        head_done = sem("head_done")
        divided = sem("divided")
        attended_turned = sem("attended_turned")
        m3_hi = sem("m3_hi")
        m3_lo = sem("m3_lo")
        M3 = FIRST[("mix3", 0)]

        def mix3_loads(pool):
            pool.wait_ge(x_done, 20)
            pool.dma_start(rope_t, rope).then_inc(rope_loaded, 16)

        def mix3_pe(pe):
            for j in range(4):
                channel_product(pe, bank[(0, 0, 1, 2)[j]][:, SEQ * (j == 1):SEQ * (j == 1) + SEQ],
                                M3 + j, norm=7 if j == 0 else None)
            for n in range(3):
                pe.wait_ge(latent_squares, 1 + n // 2)
                mm = pe.matmul(bank[3][:, SEQ * (n // 2):SEQ * (n // 2) + SEQ], ones[:, :],
                               latent_sq[:, n, :], start=n != 1, stop=n != 0)
            mm.then_inc(latent_sums, 1)
            pe.wait_ge(latent_lo, 1)
            for n in range(8):
                channel_product(pe, bank[4 + n // 2][:, SEQ * (n % 2):SEQ * (n % 2) + SEQ],
                                M3 + 4 + n // 4, k_tiles=2, at=256 * (n % 4), used=n % 4 == 3)
            pe.wait_ge(k_rope_done, 1)
            for n in range(8):
                channel_product(pe, bank[n // 2][:, SEQ * (n % 2):SEQ * (n % 2) + SEQ],
                                M3 + 6 + n // 4, k_tiles=2, at=256 * (n % 4), used=n % 4 == 3)
            for n in range(8):
                if n % 2 == 0:
                    pe.wait_ge(q_evac, n // 2 + 1)
                channel_product(pe, bank[4 + n // 2][:, SEQ * (n % 2):SEQ * (n % 2) + SEQ],
                                M3 + 8, k_tiles=1, at=P * n, k0=2, used=n == 7)
            pe.wait_ge(q_rope_read, 1)
            token_product(pe, M3 + 9, h_hi[:, 2, :], h_lo[:, 2, :], True, True, result=False)

            def score(h):
                if h >= 2:
                    pe.wait_ge(soft_exp, 2 * h - 2)
                for m in range(MT):
                    mm = pe.matmul(bank[4 + h % 2][:, SEQ * m:SEQ * m + SEQ],
                                   q_rows[0:QK, h, P * m:P * m + P], k_rows[0:QK, h, :],
                                   start=True, stop=True)
                mm.then_inc(scored, 1)

            def turn(h):
                pe.wait_ge(soft_exp, 2 * h + 2)
                if h >= 2:
                    pe.wait_ge(probs_evac, h - 1)
                for m in range(MT):
                    for c in range(MT):
                        tr = pe.transpose(bank[6 + h % 2][:, SEQ * c + P * m:SEQ * c + P * m + P],
                                          probs[:, h % 2, SEQ * m + P * c:SEQ * m + P * c + P], ident[:, :])
                tr.then_inc(probs_turned, 1)

            def weigh(h):
                pe.wait_ge(probs_evac, h + 1)
                for m in range(MT):
                    for c in range(MT):
                        mm = pe.matmul(bank[2 * m + h // 8][:, 64 * (h % 8):64 * (h % 8) + 64],
                                       probs_by_key[:, h % 2, SEQ * c + P * m:SEQ * c + P * m + P],
                                       values[:, c, 64 * h:64 * h + 64], start=c == 0, stop=c == 1)
                mm.then_inc(head_done, 1)

            pe.wait_ge(q_rope_done, 4)
            pe.wait_ge(kv_act, 4)
            pe.wait_ge(kv_dve, 4)
            score(0)
            score(1)
            for h in range(MLA_HEADS):
                turn(h)
                if h + 2 < MLA_HEADS:
                    score(h + 2)
                if h:
                    weigh(h - 1)
            weigh(MLA_HEADS - 1)
            for b in range(4):
                pe.wait_ge(divided, 2 + b // 2 * 2)
                for j in range(2):
                    for m in range(MT):
                        tr = pe.transpose(bank[4 + b][:, j * SEQ + m * P:j * SEQ + (m + 1) * P],
                                          attended[:, m, (2 * b + j) * P:(2 * b + j + 1) * P], ident[:, :])
                tr.then_inc(attended_turned, 1)
            pe.wait_ge(divided, 4)
            for k in range(KT):
                pe.wait_ge(m3_lo, k // 2 + 1)
                token_product(pe, M3 + 10 + k, h_hi[:, k, :], h_lo[:, k, :], k == 0, k == KT - 1)

        def by_head(rows, b, odd):
            return rows[0:64, 4 * b + odd:4 * b + odd + 3:2, :]

        def of_bank(b, odd):
            return bank[4 + b][64 * odd:64 * odd + 64, :].rearrange("p (t q) -> p t q", t=2)

        def mix3_act(act, order):
            act_panels(act, M3 + 3, 3)
            act.wait_ge(panel_used, M3 + 2)
            act.activation(latent_sq[:, 0:2, :].rearrange("p t q -> p (t q)"), bank[0][:, :],
                           ACT.Square).then_inc(latent_squares, 1)
            act.wait_ge(panel_used, M3 + 3)
            act.activation(latent_sq[:, 2, :], bank[1][:, 0:SEQ], ACT.Square).then_inc(latent_squares, 1)
            act.wait_ge(latent_sums, 1)
            for n, width in enumerate((256, 128)):
                order(act.activation(latent_rms[:, n, :], bank[3][:, SEQ * n:SEQ * n + SEQ], ACT.Copy,
                                     scale=1.0 / width, bias=EPS))
            act.activation(latent_rms[:, :, :], latent_rms[:, :, :], ACT.Sqrt).then_inc(latent_root, 1)
            act.wait_ge(latent_done, 3)
            act.activation(h_hi[:, 0:3, :], latent[:, :, :], ACT.Copy).then_inc(latent_hi, 1)
            act_panels(act, M3 + 6, 4)
            for b in range(4):
                act.wait_ge(panel_used, M3 + 5 + b // 2)
                order(act.activation(by_head(q_rows, b, 0), of_bank(b, 0), ACT.Copy))
                act.activation(by_head(q_rows, b, 1), of_bank(b, 1), ACT.Copy).then_inc(q_evac, 1)
            act.wait_ge(panel_used, M3 + 9)
            for b in range(2):
                for odd in range(2):
                    ins = act.activation(by_head(k_rows, b, odd), of_bank(b, odd), ACT.Copy)
                    if odd:
                        ins.then_inc(kv_act, 1)
                    else:
                        order(ins)
            act.wait_ge(panel_used, M3 + 10)
            for half in range(2):
                act.activation(values[:, 0, 512 * half:512 * half + 512], bank[half][:, :],
                               ACT.Copy).then_inc(kv_act, 1)
            for h in range(MLA_HEADS):
                act.wait_ge(soft_max, h + 1)
                if h >= 2:
                    act.wait_ge(probs_turned, h - 1)
                for m in range(MT):
                    i = 2 * h + m
                    act.activation(probs[:, h % 2, SEQ * m:SEQ * m + SEQ],
                                   bank[4 + h % 2][:, SEQ * m:SEQ * m + SEQ], ACT.Exp, scale=SCALE,
                                   bias=soft[:, NEG3, i:i + 1],
                                   accum_out=soft[:, SUM3, i:i + 1]).then_inc(soft_exp, 1)
                if h % 2 == 1 and h < 12:
                    split_hi(act, M3 + 10 + h // 2)
            for b in range(4):
                act.wait_ge(attended_turned, b + 1)
                act.activation(h_hi[:, 2 * b:2 * b + 2, :].rearrange("p k t -> p (k t)"),
                               bank[4 + b][:, :], ACT.Copy).then_inc(m3_hi, 1)
            act_panels(act, M3 + 16, 5)

        def mix3_dve(dve, order):
            cos, sin = rope_t[:, 0, :], rope_t[:, 1, :]
            dve_panels(dve, M3 + 3, 3)
            dve.wait_ge(rope_loaded, 16)
            dve.wait_ge(panel_used, M3 + 4)
            r, s = slice(64, 96), slice(96, 128)
            order(dve.tensor_tensor(k_turn[r, 0, :], bank[2][r, 0:SEQ], cos[r, :], ALU.mult))
            order(dve.tensor_tensor(k_turn[r, 1, :], bank[2][s, 0:SEQ], sin[s, :], ALU.mult))
            order(dve.tensor_tensor(k_turn[r, 0, :], k_turn[r, 0, :], k_turn[r, 1, :], ALU.add))
            dve.tensor_copy(k_rows[r, :, :], k_turn[r, 0, :].unsqueeze(1).to_broadcast(
                [32, MLA_HEADS, SEQ])).then_inc(k_rope_done, 1)
            dve.wait_ge(latent_root, 1)
            order(dve.reciprocal(latent_rms[:, :, :], latent_rms[:, :, :]))
            for n in range(3):
                dve.scalar_tensor_tensor(out=latent[:, n, :],
                                         in0=bank[n // 2][:, SEQ * (n % 2):SEQ * (n % 2) + SEQ],
                                         scalar=col("q_g", n) if n < 2 else col("kv_g"),
                                         in1=latent_rms[:, n // 2, :], op0=ALU.mult,
                                         op1=ALU.mult).then_inc(latent_done, 1)
            dve.wait_ge(latent_hi, 1)
            dve.tensor_tensor(h_lo[:, 0:3, :], latent[:, :, :], h_hi[:, 0:3, :].bitcast(F32),
                              ALU.subtract).then_inc(latent_lo, 1)
            dve_panels(dve, M3 + 6, 4)
            dve.wait_ge(panel_used, M3 + 8)
            for part, table in enumerate((cos, sin)):
                for b in range(2):
                    ins = dve.tensor_tensor(q_turn[:, part, 2 * b:2 * b + 2, :],
                                            bank[2 * part + b][:, :].rearrange("p (t q) -> p t q", t=2),
                                            table.unsqueeze(1).to_broadcast([P, 2, SEQ]), ALU.mult)
                    order(ins)
            dve.sem_inc(q_rope_read, 1)
            for j in range(4):
                rows = slice(32 * j, 32 * j + 32)
                dve.tensor_tensor(q_rows[64:96, j::4, :], q_turn[rows, 0, :, :], q_turn[rows, 1, :, :],
                                  ALU.add).then_inc(q_rope_done, 1)
            dve.wait_ge(panel_used, M3 + 9)
            for b in range(2, 4):
                for odd in range(2):
                    ins = dve.tensor_copy(by_head(k_rows, b, odd), of_bank(b, odd))
                    if odd:
                        ins.then_inc(kv_dve, 1)
                    else:
                        order(ins)
            dve.wait_ge(panel_used, M3 + 10)
            for half in range(2):
                dve.tensor_copy(values[:, 1, 512 * half:512 * half + 512],
                                bank[2 + half][:, :]).then_inc(kv_dve, 1)

            def turned_probs(h):
                dve.wait_ge(probs_turned, h + 1)
                if h >= 2:
                    dve.wait_ge(head_done, h - 1)
                dve.tensor_copy(probs_by_key[:, h % 2, :], bank[6 + h % 2][:, :]).then_inc(probs_evac, 1)

            for h in range(MLA_HEADS):
                dve.wait_ge(scored, h + 1)
                order(dve.tensor_reduce(soft[:, MAX3, 2 * h:2 * h + 2],
                                        bank[4 + h % 2][:, :].rearrange("p (m k) -> p m k", m=2),
                                        AX.X, ALU.max))
                dve.tensor_scalar(soft[:, NEG3, 2 * h:2 * h + 2], soft[:, MAX3, 2 * h:2 * h + 2],
                                  -SCALE, None, ALU.mult).then_inc(soft_max, 1)
                if h:
                    turned_probs(h - 1)
                if h % 2 == 1 and h < 12:
                    split_lo(dve, M3 + 10 + h // 2)
            turned_probs(MLA_HEADS - 1)
            dve.wait_ge(soft_exp, 2 * MLA_HEADS)
            order(dve.reciprocal(soft[:, REC3, :], soft[:, SUM3, :]))
            dve.wait_ge(head_done, MLA_HEADS)
            rec = soft[:, REC3, :].rearrange("p (h m) -> p h m", m=MT)
            for half in range(2):
                for m in range(MT):
                    dve.tensor_tensor(
                        attended[:, m, 512 * half:512 * half + 512].rearrange("p (h d) -> p h d", d=64),
                        bank[2 * m + half][:, :].rearrange("p (h d) -> p h d", d=64),
                        rec[:, 8 * half:8 * half + 8, m].unsqueeze(2).to_broadcast([P, 8, 64]),
                        ALU.mult).then_inc(divided, 1)
            for b in range(4):
                dve.wait_ge(m3_hi, b + 1)
                r = slice(2 * b, 2 * b + 2)
                dve.tensor_tensor(h_lo[:, r, :].rearrange("p k t -> p (k t)"), bank[4 + b][:, :],
                                  h_hi[:, r, :].bitcast(F32).rearrange("p k t -> p (k t)"),
                                  ALU.subtract).then_inc(m3_lo, 1)
            dve_panels(dve, M3 + 16, 5)

        stages = STAGES[:last_stage]

        block = ctx.enter_context(nc.Block())
        out_stored = sem("out_stored")
        final_done = sem("final_done")
        final_loaded = sem("final_loaded")
        final_row = region(13824, D)
        final = region(0, MT, D)

        @block.sync
        def _(sp):
            def load_panel(g0, i=0):
                slot = g0 % RING
                if g0 >= RING:
                    sp.wait_ge(lo_ready, g0 - (RING - 1) + RING * i)
                sp.dma_start(raw[:, slot, :], panels[g0 + RING * i]).then_inc(raw_loaded[slot], 16)

            def load_ada(a, i=0):
                slot = a % ADA_RING
                if a >= ADA_RING:
                    sp.wait_ge(ada_used, a - (ADA_RING - 1) + ADA_RING * i)
                sp.dma_start(ada_ring[:, slot, :], ada[a + ADA_RING * i]).then_inc(ada_loaded[slot], 16)

            sp.dma_start(C[:, :], cols).then_inc(small_loaded, 16)
            sp.dma_start(X[:, :, :], x_in.rearrange("(m p) d -> p m d", p=P)).then_inc(x_loaded, 16)
            for a in range(ADA_FIRST):
                load_ada(a)
            for g in range(8):
                load_panel(g)
            with sp.Fori(0, KT) as i:
                for half, chunks in enumerate(((0, 1), (2, 3, 4))):
                    for j in range(3):
                        load_panel(8 + 3 * half + j, i)
                    for c in chunks:
                        load_ada(ADA_FIRST + c, i)
            done, total = 8 + KT * RING, min(last_panel(*stages[-1]) + 3, TOTAL)
            turns = (total - done) // RING
            if turns:
                with sp.Fori(0, turns) as i:
                    for j in range(RING):
                        load_panel(done + j, i)
            for g in range(done + RING * turns, total):
                load_panel(g)

        @block.gpsimd
        def _(pool):
            order = Order(pool, pool_order)
            pool.memset(ones[:, :], 1.0).then_inc(const_ready, 1)
            pool.memset(stat[:, MINUS_HALF - 1:MINUS_HALF + 1], -0.5).then_inc(const_ready, 1)
            pool.wait_ge(const_ready, 2)
            norm_pool(pool, 0, order)
            spectrum_pool(pool)
            ada_middle_pool(pool, order)
            params_pool(pool, order)
            gate_rows_pool(pool, order)
            for at, (kind, n) in enumerate(stages):
                if kind == "mix1":
                    mix1_pool(pool, order)
                if at < 3:
                    add_pool(pool, at, order)
                norm_pool(pool, at + 1, order)
                if at == 1:
                    gate_2_pool(pool, order)
                if at == 2:
                    mix2_loads(pool)
                if at == 4:
                    mix3_loads(pool)
                if at + 1 == len(stages):
                    pool.dma_start(final_row[:, :], rows[6:7, :].partition_broadcast(P)).then_inc(final_loaded, 16)
            for m in range(MT):
                pool.wait_ge(final_done, m + 1)
                pool.dma_start(out[m * P:(m + 1) * P, :], final[:, m, :]).then_inc(out_stored, 16)
            pool.wait_ge(out_stored, 32)

        @block.scalar
        def _(act):
            order = Order(act, act_order)
            act.dma_start(ident[:, :], tables[0]).then_inc(small_loaded, 16)
            act.dma_start(feat_t, feats).then_inc(spec_loaded, 16)
            act.dma_start(mlp_ws, mlp_w[:, 0:192]).then_inc(spec_loaded, 16)
            act.dma_start(filter_out[0:64, :], mlp_w[:, 192:2240]).then_inc(spec_loaded, 16)
            act.dma_start(dft[:, 0, :, :], pool_mats[4]).then_inc(spec_loaded, 16)
            act.dma_start(dft[:, 1, :, :], pool_mats[5]).then_inc(spec_loaded, 16)
            act.dma_start(decay_rows, decay[0:1, :].partition_broadcast(P)).then_inc(decay_loaded, 16)
            act.wait_ge(small_loaded, 32)
            act.activation(c_act, col("c", 0, 8), ACT.Silu).then_inc(c_ready, 1)
            norm_act_squares(act, 0)
            params_act(act)
            spectrum_act(act, order)
            act_panels(act, 0, 3)
            norm_act_rest(act, 0)
            for at, (kind, n) in enumerate(stages):
                if kind == "ffn":
                    ffn_act(act, n)
                elif kind == "mix1":
                    mix1_act(act, order)
                elif kind == "mix2":
                    mix2_act(act, order)
                else:
                    mix3_act(act, order)
                if at < 3:
                    add_act(act, kind, n, at)
                norm_act_squares(act, at + 1)
                if at + 1 < len(stages):
                    norm_act_rest(act, at + 1)

        @block.vector
        def _(dve):
            order = Order(dve, dve_order)
            ada_next = iter(range(ADA_FIRST))

            def spare():
                a = next(ada_next, None)
                if a is not None:
                    ada_add(dve, a, acc0[:, a // KT, :])

            dve.wait_ge(small_loaded, 32)
            params_dve(dve, order)
            dve.wait_ge(c_ready, 1)
            for _ in range(4):
                spare()
            spectrum_dve(dve, order, spare)
            for _ in range(ADA_FIRST):
                spare()
            ada_first_dve(dve, order)
            dve_panels(dve, 0, 3)
            norm_dve(dve, 0, order)
            for at, (kind, n) in enumerate(stages):
                if kind == "ffn":
                    ffn_dve(dve, n, order)
                elif kind == "mix1":
                    mix1_dve(dve, order)
                elif kind == "mix2":
                    mix2_dve(dve, order)
                else:
                    mix3_dve(dve, order)
                add_dve(dve, kind, n, at)
                if at + 1 < len(stages):
                    norm_dve(dve, at + 1, order)
            dve.wait_ge(final_loaded, 16)
            last = len(stages)
            for m in range(MT):
                dve.wait_ge(rstd_done, 2 * last + m + 1)
                dve.scalar_tensor_tensor(out=final[:, m, :], in0=X[:, m, :],
                                         scalar=stat[:, RS + m:RS + m + 1], in1=final_row[:, :],
                                         op0=ALU.mult, op1=ALU.mult).then_inc(final_done, 1)

        @block.tensor
        def _(pe):
            pe.wait_ge(const_ready, 2)
            pe.wait_ge(small_loaded, 32)
            spectrum_pe(pe)
            ada_first_pe(pe)
            norm_pe(pe, 0)
            for at, (kind, n) in enumerate(stages):
                if kind == "ffn":
                    ffn_pe(pe, n)
                elif kind == "mix1":
                    mix1_pe(pe)
                elif kind == "mix2":
                    mix2_pe(pe)
                else:
                    mix3_pe(pe)
                if at + 1 < len(stages):
                    norm_pe(pe, at + 1)



def stream_of_panels(a):
    def columns(w):
        k, n = w.shape[0] // P, w.shape[1] // P
        return w.reshape(k, P, n, P).transpose(2, 1, 0, 3).reshape(n, P, k * P)

    def together(p, n):
        return p.reshape(-1, n, P, p.shape[2]).transpose(0, 2, 1, 3).reshape(-1, P, n * p.shape[2])

    def ffn(gate, up, down):
        g, u, d = columns(gate), columns(up), down.reshape(FT, P, D)
        order = [g[0], u[0]]
        for f in range(1, FT):
            order += [g[f], u[f], d[f - 1]]
        return np.stack(order + [d[FT - 1]])

    def mix1():
        w = a["w_in"][0]
        q = w[:, :512].reshape(D, 2, 4, HD).transpose(0, 2, 1, 3).reshape(D, 512)
        return [columns(w[:, 768:]), columns(q), columns(w[:, 512:768]),
                together(columns(a["ssm_w_glu"][0]), 2), a["w_out"][0].reshape(8, P, D)]

    def mix2():
        w = a["mix_w_in_2"][0]
        return [together(w[:, :512].reshape(8, P, 512), 2),
                columns(w[:, 1536:]), columns(w[:, 512:1536]), a["mix_w_out_2"][0].reshape(8, P, D)]

    def mix3():
        uq = a["mla_w_uq_2"][0].reshape(256, MLA_HEADS, 96)
        dkv, ukv = a["mla_w_dkv_2"][0], a["mla_w_ukv_2"][0].reshape(P, MLA_HEADS, P)
        swap = np.r_[16:32, 0:16]
        rope = uq[:, :, 64:]
        return [columns(a["mla_w_dq_2"][0]), columns(dkv[:, :P]),
                columns(np.concatenate([dkv[:, P:], dkv[:, P:][:, swap]] * 2, 1)),
                together(columns(uq[:, :, :64].reshape(256, 1024)), 4),
                together(columns(rope.reshape(256, 512)), 4),
                together(columns(rope[:, :, swap].reshape(256, 512)), 4),
                ukv[:, :, :64].reshape(1, P, D), ukv[:, :, 64:].reshape(1, P, D),
                a["mla_w_o_2"][0].reshape(8, P, D)]

    g, u, d = a["ffn_w_gate_2"], a["ffn_w_up_2"], a["ffn_w_down_2"]
    feed = [ffn(a["w1_gate"][0], a["w1_up"][0], a["w1_down"][0]),
            ffn(a["w2_gate"][0], a["w2_up"][0], a["w2_down"][0])]
    feed += [ffn(g[i, j], u[i, j], d[i, j]) for i in range(2) for j in range(2)]
    parts = []
    for kind, n in STAGES:
        parts += [feed[n]] if kind == "ffn" else {"mix1": mix1, "mix2": mix2, "mix3": mix3}[kind]()
    return np.concatenate(parts)


def small_columns(a):
    def cut(v):
        return v.reshape(-1, P).T

    def states(v):
        return v.reshape(STATE_TILES, P).T

    def short(v):
        return np.concatenate([v, np.zeros((P - 64,) + v.shape[1:], np.float32)])

    t = np.linspace(0.0, 1.0, SEQ, dtype=np.float32)
    parts = [("c", cut(a["c"])), ("b_ada", cut(a["b_ada"])),
             ("g_pre", np.concatenate([cut(a[n]) for n in ("g_pre_ff1", "g_pre_mix", "g_pre_ff2")], 1)),
             ("norm_g", cut(a["norm_g_2"])), ("pool_scale", cut(a["pool_scale_2"])),
             ("conv_b", cut(a["hyena_conv_b_2"])), ("conv_w", cut(a["hyena_conv_w_2"])),
             ("bias", cut(a["hyena_bias_2"])), ("g_attn", cut(a["g_attn_out"])),
             ("g_ssm", cut(a["g_ssm_out"])), ("ssm_d", cut(a["ssm_d"])), ("b_glu", cut(a["ssm_b_glu"])),
             ("q_g", cut(a["mla_q_norm_g_2"])), ("kv_g", cut(a["mla_kv_norm_g_2"])),
             ("a_re", states(a["ssm_a_re"])), ("a_im", states(a["ssm_a_im"])),
             ("log_step", states(np.repeat(a["ssm_log_step"][0], 64))),
             ("sin_freq", short(a["hyena_sin_freq_2"][0].T)),
             ("mlp_b", short(np.stack([a[f"hyena_ffn_b{i}_2"][0] for i in (1, 2, 3)], 1))),
             ("neg_t", cut(-t))]
    for (name, v), (key, (_, n)) in zip(parts, COLS.items()):
        assert name == key and v.shape == (P, n), (name, v.shape, n)
    return np.concatenate([v for _, v in parts], 1)


def shape_constants():
    t = np.arange(SEQ)
    angle = np.outer(t, 2 * t + 1) * (math.pi / 512)
    cos, sin = np.cos(angle), np.sin(angle)
    tiles = lambda m: m.reshape(MT, P, SEQ).transpose(1, 0, 2)
    mats = []
    for w in (2, 4, 8, 16):
        lo = np.clip(t - w // 2, 0, SEQ)
        hi = np.clip(t - w // 2 + w, 0, SEQ)
        s = t[:, None]
        mats.append(((s >= lo) & (s < hi)) / (hi - lo) - (s == t))
    mats += [cos, sin, cos.T / 256, sin.T / 256]
    pool_mats = np.stack([tiles(m) for m in mats]).astype(np.float32)
    inv = (10000.0 ** (-np.arange(0, 32, 2, dtype=np.float32) / 32)).astype(np.float32)
    ang = np.arange(SEQ, dtype=np.float32)[:, None] * inv[None, :]
    c, s = np.cos(ang.astype(np.float64)).T, np.sin(ang.astype(np.float64)).T
    rope = np.stack([np.tile(np.concatenate([c, c]), (4, 1)),
                     np.tile(np.concatenate([-s, s]), (4, 1))], 1).astype(np.float32)
    i, j = np.arange(P)[:, None], np.arange(2 * P)[None, :]
    dist = i + P - j
    near = np.where((dist >= 0) & (dist < P), -dist, -1e38).astype(np.float32)
    near = np.concatenate([near[:, P:], near], 1)
    bands = 16
    w = (2.0 * math.pi * np.arange(SEQ, dtype=np.float32) / SEQ).astype(np.float32)
    f = np.linspace(1e-4, bands - 1, bands, dtype=np.float32)
    phase = (w[:, None] * f[None, :]).astype(np.float64)
    z = np.concatenate([np.linspace(0.0, 1.0, SEQ)[:, None], np.cos(phase), -np.sin(phase)], 1)
    return {"tables": np.eye(P, dtype=np.float32)[None], "pool_mats": pool_mats, "rope": rope,
            "near": near, "feats": np.ascontiguousarray(z.T.astype(np.float32))}


def lay_out(a):
    a = {k: np.asarray(v) for k, v in a.items()}
    ada = a["w_ada"][0].reshape(KT, P, 9, D).transpose(2, 0, 1, 3)
    ada = np.concatenate([ada[0], ada[1], ada[list(ADA_MIDDLE)].transpose(1, 0, 2, 3).reshape(-1, P, D),
                          ada[5], ada[8]])
    b_ada = a["b_ada"].reshape(9, D)
    rows = np.stack([b_ada[2], b_ada[5], b_ada[8], a["g_post_ff1"][0], a["g_post_mix"][0],
                     a["g_post_ff2"][0], a["final_norm_g_2"]])
    b = [a[n][0].reshape(STATE_TILES, P, 16).transpose(1, 0, 2).reshape(P, 256)
         for n in ("ssm_b_re", "ssm_b_im")]
    c = [a[n][0].reshape(STATE_TILES, 2, 16, 64).transpose(1, 3, 0, 2).reshape(P, 256)
         for n in ("ssm_c_re", "ssm_c_im")]
    mlp_w = np.zeros((64, 2240), np.float32)
    mlp_w[:33, 0:64] = a["hyena_ffn_w1_2"][0]
    mlp_w[:, 64:128] = a["hyena_ffn_w2_2"][0]
    mlp_w[:, 128:192] = a["hyena_ffn_w3_2"][0]
    mlp_w[:, 192:] = a["hyena_ffn_w_out_2"][0]
    got = {"panels": stream_of_panels(a), "ada": ada, "cols": small_columns(a), "rows": rows,
           "sinks": a["attn_sinks"], "ssm_mats": np.stack(b + c, 1),
           "pool_w": a["pool_w_2"][0].transpose(1, 0, 2), "decay": a["hyena_decay_2"][0].reshape(2, 1024),
           "mlp_w": mlp_w, "x_in": a["x"][0]}
    got.update(shape_constants())
    return {k: np.ascontiguousarray(v) for k, v in got.items()}


def kernel(last_stage=len(STAGES), **inputs):
    from concourse import bacc
    from concourse.bass_utils import run_bass_kernel_spmd

    nc = bacc.Bacc("TRN2", target_bir_lowering=False, num_devices=1)
    arrays = lay_out(inputs)
    args = {name: nc.dram_tensor(name, v.shape, F32, kind="ExternalInput").ap()
            for name, v in arrays.items()}
    out = nc.dram_tensor("out", (SEQ, D), F32, kind="ExternalOutput").ap()
    spectrum = nc.dram_tensor("spectrum", (2, P, 4, 512), F32, kind="Internal").ap()
    build_program(nc, out=out, spectrum=spectrum, last_stage=last_stage, **args)
    result = run_bass_kernel_spmd(nc, [arrays], core_ids=[0])
    return result.results[0]["out"].reshape(1, SEQ, D)
```

```python
import math
from contextlib import ExitStack

import numpy as np
import concourse.bass as bass
from concourse import mybir

F32 = mybir.dt.float32
F32R = mybir.dt.float32r
I32 = mybir.dt.int32
ALU = mybir.AluOpType
ACT = mybir.ActivationFunctionType
AX = mybir.AxisListType

P = 128
D = 1024
KT = D // P
SEQ = 256
MT = SEQ // P
FF = 2816
FT = FF // P
PANEL = 1024
RING = 6
EPS = 1e-6
HEADS, HD = 8, 64
STATE_TILES = 16
MLA_HEADS = 16
ADA_RING = 5
ADA_MIDDLE = (2, 3, 4, 6, 7)
ADA_FIRST = 2 * KT
ADA_GATE_1 = ADA_FIRST + len(ADA_MIDDLE) * KT
ADA_GATE_2 = ADA_GATE_1 + KT

FFN_PANELS = 3 * FT
MIX1_PANELS = 10 + 2 + 8
MIX2_PANELS = 4 + 12 + 8
MIX3_PANELS = 4 + 4 + 2 + 8
STAGES = [("ffn", 0), ("mix1", 0), ("ffn", 1), ("ffn", 2), ("mix2", 0), ("ffn", 3),
          ("ffn", 4), ("mix3", 0), ("ffn", 5)]
SIZE = {"ffn": FFN_PANELS, "mix1": MIX1_PANELS, "mix2": MIX2_PANELS, "mix3": MIX3_PANELS}
FIRST = {}
TOTAL = 0
for _s in STAGES:
    FIRST[_s] = TOTAL
    TOTAL += SIZE[_s[0]]

COLS = {}
_w = 0
for _name, _n in (("c", 8), ("b_ada", 72), ("g_pre", 24), ("norm_g", 48), ("pool_scale", 4),
                  ("conv_b", 12), ("conv_w", 36), ("bias", 8), ("g_attn", 4), ("g_ssm", 4),
                  ("ssm_d", 4), ("b_glu", 4), ("q_g", 2), ("kv_g", 1), ("a_re", 16), ("a_im", 16),
                  ("log_step", 16), ("sin_freq", 3), ("mlp_b", 3), ("neg_t", 2)):
    COLS[_name] = (_w, _n)
    _w += _n
N_COLS = _w

MAGIC = 12582912.0
TWO_PI = 2.0 * math.pi
TWO_PI_HI = 6.28125
TWO_PI_LO = TWO_PI - TWO_PI_HI
LN2_HI = 0.693359375
LN2_LO = math.log(2.0) - LN2_HI
PI_BELOW = 3.1415925


def build_program(nc, panels, ada, cols, rows, sinks, ssm_mats, tables, pool_mats, rope, near,
                  pool_w, decay, mlp_w, feats, x_in, out, spectrum, last_stage):
    ctx = ExitStack()
    with ctx:
        def sb(name, shape, dt=F32):
            return ctx.enter_context(nc.sbuf_tensor(name, shape, dt))

        def sem(name):
            return ctx.enter_context(nc.semaphore(name))

        X = sb("X", [P, MT, D])
        raw = sb("raw", [P, RING, PANEL])
        w_hi = sb("w_hi", [P, RING, PANEL], F32R)
        w_lo = sb("w_lo", [P, RING, PANEL], F32R)
        h_hi = sb("h_hi", [P, KT, SEQ], F32R)
        h_lo = sb("h_lo", [P, KT, SEQ], F32R)
        f_hi = sb("f_hi", [P, 2, SEQ], F32R)
        f_lo = sb("f_lo", [P, 2, SEQ], F32R)
        C = sb("C", [P, N_COLS])
        ident = sb("ident", [P, P])
        ones = sb("ones", [P, P])
        mods = sb("mods", [P, 6, KT])
        pre_scale = sb("pre_scale", [P, 3, KT])
        stat = sb("stat", [P, 64])
        par = sb("par", [P, 20, 16])
        ARENA = 26112
        arena = sb("arena", [P, ARENA])

        def region(at, *shape):
            size = int(np.prod(shape))
            assert at + size <= ARENA, (at, shape)
            v = arena[:, at:at + size]
            if len(shape) == 2:
                return v.rearrange("p (a b) -> p a b", b=shape[1])
            if len(shape) == 3:
                return v.rearrange("p (a b c) -> p a b c", b=shape[1], c=shape[2])
            return v

        gated_sum = region(0, MT, D)
        h32 = region(2048, KT, SEQ)
        squares = region(2048, 4, 512)
        acc = region(0, len(ADA_MIDDLE), D)
        acc0 = region(4096, 2, D)
        acc_gate_1 = region(13312, D)
        acc_gate_2 = region(4096, D)
        late_panel = region(5120, D)
        ada_ring = region(6144, ADA_RING, D)
        gate_rows = region(11264, 3, D)
        ssm_raw = region(11264, 4, 256)
        rot_tmp = region(11264, 16, 128)
        b_rows = region(13312, 2, 512)
        rot = region(14336, 2, STATE_TILES, SEQ)
        b_turned = region(22528, 2, 4, P)
        c_rows = region(23552, 3, STATE_TILES, 32)
        ffn_buf = region(25088, 4, SEQ)

        def col(name, i=0, n=1):
            at, _ = COLS[name]
            return C[:, at + i:at + i + n]

        bank = [ctx.enter_context(nc.psum_tensor(f"bank{i}", [P, 512], F32)) for i in range(8)]

        raw_loaded = [sem(f"raw_loaded{i}") for i in range(RING)]
        ada_loaded = [sem(f"ada_loaded{i}") for i in range(ADA_RING)]
        hi_ready = sem("hi_ready")
        lo_ready = sem("lo_ready")
        panel_used = sem("panel_used")
        ada_used = sem("ada_used")
        act_order = sem("act_order")
        dve_order = sem("dve_order")
        pool_order = sem("pool_order")

        class Order:
            def __init__(self, eng, s):
                self.eng, self.s, self.n = eng, s, 0

            def __call__(self, ins):
                self.n += 1
                ins.then_inc(self.s, 1)
                self.eng.wait_ge(self.s, self.n)

        def then(eng, ins, s, value):
            ins.then_inc(s, 1)
            eng.wait_ge(s, value)

        def split_hi(act, g0, i=0):
            slot = g0 % RING
            act.wait_ge(raw_loaded[slot], 16 * (g0 // RING + 1) + 16 * i)
            if g0 >= RING:
                act.wait_ge(panel_used, g0 - (RING - 1) + RING * i)
            act.activation(w_hi[:, slot, :], raw[:, slot, :], ACT.Copy).then_inc(hi_ready, 1)

        def split_lo(dve, g0, i=0):
            slot = g0 % RING
            dve.wait_ge(hi_ready, g0 + 1 + RING * i)
            dve.tensor_tensor(w_lo[:, slot, :], raw[:, slot, :], w_hi[:, slot, :].bitcast(F32),
                              ALU.subtract).then_inc(lo_ready, 1)

        def act_panels(act, first, n):
            for g in range(first, min(first + n, TOTAL)):
                split_hi(act, g)

        def dve_panels(dve, first, n):
            for g in range(first, min(first + n, TOTAL)):
                split_lo(dve, g)

        def product3(pe, out_ap, wh, wl, xh, xl, start, stop, weights_move=False):
            last = None
            for n, (w, x) in enumerate(((wh, xh), (wh, xl), (wl, xh))):
                a, b = (x, w) if weights_move else (w, x)
                last = pe.matmul(out_ap, a, b, start=start and n == 0, stop=stop and n == 2)
            return last

        def channel_product(pe, out_ap, g0, i=0, k_tiles=KT, at=0, k0=0, used=True, norm=None):
            slot = g0 % RING
            pe.wait_ge(lo_ready, g0 + 1 + RING * i)
            mm = None
            for k in range(k_tiles):
                w = slice(at + k * P, at + (k + 1) * P)
                if norm is not None:
                    pe.wait_ge(h_lo_done, KT * norm + k + 1)
                mm = product3(pe, out_ap, w_hi[:, slot, w], w_lo[:, slot, w], h_hi[:, k0 + k, :],
                              h_lo[:, k0 + k, :], k == 0, k == k_tiles - 1)
            if used:
                mm.then_inc(panel_used, 1)
            return mm

        def token_product(pe, g0, xh, xl, start, stop, i=0, result=True):
            slot = g0 % RING
            pe.wait_ge(lo_ready, g0 + 1 + RING * i)
            mm = None
            for m in range(MT):
                t = slice(m * P, (m + 1) * P)
                for n in range(2):
                    w = slice(n * 512, (n + 1) * 512)
                    mm = product3(pe, bank[2 * m + n][:, :], w_hi[:, slot, w], w_lo[:, slot, w],
                                  xh[:, t], xl[:, t], start, stop, weights_move=True)
                    if stop and result and 2 * m + n < 3:
                        mm.then_inc(result_ready, 1)
            mm.then_inc(panel_used, 1)

        result_ready = sem("result_ready")
        square_done = sem("square_done")
        rstd_done = sem("rstd_done")
        diag_done = sem("diag_done")
        turned = sem("turned")
        h_hi_done = sem("h_hi_done")
        h_lo_done = sem("h_lo_done")
        x_done = sem("x_done")
        SS, RS, RSS, RRS = 0, 4, 6, 10
        MINUS_HALF = 60
        diag = sb("diag", [P, MT, P])

        def norm_scalars(n):
            if n in (0, 1, 2):
                return pre_scale[:, n, :], mods[:, 2 * n, :]
            at, _ = COLS["norm_g"]
            return C[:, at + (n - 3) * KT:at + (n - 2) * KT], None

        def mean_square(act, q, source, at):
            return act.activation(squares[:, q, :], source, ACT.Square, scale=D ** -0.5,
                                  accum_out=stat[:, at + q:at + q + 1])

        def quarter(q):
            return slice((q % 2) * 512, (q % 2) * 512 + 512)

        def norm_act_squares(act, n):
            if n == 0:
                act.wait_ge(x_loaded, 16)
            for q in range(4):
                if n:
                    act.wait_ge(x_done, 4 * (n - 1) + q + 1)
                mean_square(act, q, X[:, q // 2, quarter(q)], SS).then_inc(square_done, 1)

        def norm_act_rest(act, n):
            sc, sh = norm_scalars(n)
            for k in range(KT):
                if k % 2 == 0:
                    act.wait_ge(turned, 4 * n + k // 2 + 1)
                ps = bank[4 + k // 2][:, (k % 2) * SEQ:(k % 2 + 1) * SEQ]
                act.activation(h_hi[:, k, :], ps, ACT.Identity, scale=sc[:, k:k + 1],
                               bias=0.0 if sh is None else sh[:, k:k + 1]).then_inc(h_hi_done, 1)

        def rstd_pool(pool, order, squares_at, rstd_at, m):
            two = stat[:, squares_at + 2 * m:squares_at + 2 * m + 2]
            rs = stat[:, rstd_at + m:rstd_at + m + 1]
            order(pool.tensor_scalar(rs, two[:, 0:1], two[:, 1:2], EPS, ALU.add, ALU.add))
            return pool.tensor_tensor(rs, rs, stat[:, MINUS_HALF:MINUS_HALF + 1], ALU.pow)

        def norm_pool(pool, n, order):
            for m in range(MT):
                pool.wait_ge(square_done, 4 * n + 2 * m + 2)
                rstd_pool(pool, order, SS, RS, m).then_inc(rstd_done, 1)

        def norm_dve(dve, n, order):
            for m in range(MT):
                dve.wait_ge(rstd_done, 2 * n + m + 1)
                dve.tensor_scalar(diag[:, m, :], ident[:, :], stat[:, RS + m:RS + m + 1], None,
                                  ALU.mult).then_inc(diag_done, 1)
            sc, sh = norm_scalars(n)
            for b in range(4):
                dve.wait_ge(h_hi_done, KT * n + 2 * b + 2)
                for k in (2 * b, 2 * b + 1):
                    ps = bank[4 + b][:, (k % 2) * SEQ:(k % 2 + 1) * SEQ]
                    hi = h_hi[:, k, :].bitcast(F32)
                    if sh is None:
                        ins = dve.scalar_tensor_tensor(out=h_lo[:, k, :], in0=ps, scalar=sc[:, k:k + 1],
                                                       in1=hi, op0=ALU.mult, op1=ALU.subtract)
                    else:
                        order(dve.tensor_scalar(h32[:, k, :], ps, sc[:, k:k + 1], sh[:, k:k + 1],
                                                ALU.mult, ALU.add))
                        ins = dve.tensor_tensor(h_lo[:, k, :], h32[:, k, :], hi, ALU.subtract)
                    ins.then_inc(h_lo_done, 1)

        def norm_pe(pe, n):
            for m in range(MT):
                pe.wait_ge(diag_done, 2 * n + m + 1)
                for k in range(KT):
                    at = (k % 2) * SEQ + m * P
                    mm = pe.matmul(bank[4 + k // 2][:, at:at + P], X[:, m, k * P:(k + 1) * P],
                                   diag[:, m, :], start=True, stop=True)
                    if m == MT - 1 and k % 2:
                        mm.then_inc(turned, 1)

        silu_done = sem("silu_done")
        hidden_done = sem("hidden_done")
        f_hi_done = sem("f_hi_done")
        f_lo_done = sem("f_lo_done")

        def up_bank(f):
            return bank[4 + f % 2 if f else 0]

        def ffn_pe(pe, n):
            base, s0 = FIRST[("ffn", n)], FT * n

            def up(f, i=0):
                g = base + max(3 * f - 1, 0)
                if s0 + f >= 2:
                    pe.wait_ge(hidden_done, s0 + f - 1 + 2 * i)
                channel_product(pe, up_bank(f)[:, 0:SEQ], g, i,
                                norm=STAGES.index(("ffn", n)) if f == 0 else None)
                channel_product(pe, up_bank(f)[:, SEQ:2 * SEQ], g + 1, i)

            def down(f, i=0, start=False, stop=False):
                pe.wait_ge(f_lo_done, s0 + f + 1 + 2 * i)
                g = base + (3 * FT - 1 if stop else 3 * f + 4)
                token_product(pe, g, f_hi[:, f % 2, :], f_lo[:, f % 2, :], start, stop, i)

            def tiles(lo, hi):
                with pe.Fori(lo, hi) as i:
                    up(2, i)
                    down(1, i)
                    up(3, i)
                    down(2, i)

            up(0)
            up(1)
            down(0, start=True)
            tiles(0, FT // 2 - 2)
            if n == 0:
                turn_b_pe(pe)
                ada_middle_pe(pe)
            if n == 1:
                gate_pe(pe, 2, acc_gate_2, (6, 7))
            tiles(FT // 2 - 2, FT // 2 - 1)
            down(FT - 1, stop=True)

        def ffn_act(act, n):
            base, s0 = FIRST[("ffn", n)], FT * n

            def hidden(f, i=0):
                act.wait_ge(panel_used, base + (3 * f + 1 if f else 2) + RING * i)
                act.activation(ffn_buf[:, f % 2, :], up_bank(f)[:, 0:SEQ],
                               ACT.Silu).then_inc(silu_done, 1)
                act.wait_ge(hidden_done, s0 + f + 1 + 2 * i)
                act.activation(f_hi[:, f % 2, :], ffn_buf[:, 2 + f % 2, :],
                               ACT.Copy).then_inc(f_hi_done, 1)

            def tiles(lo, hi):
                with act.Fori(lo, hi) as i:
                    for f in (2, 3):
                        for j in range(3):
                            split_hi(act, base + 3 * f + 2 + j, i)
                        hidden(f, i)

            act_panels(act, base + 3, 2)
            hidden(0)
            act_panels(act, base + 5, 3)
            hidden(1)
            tiles(0, FT // 2 - 2)
            if n == 0:
                turn_b_act(act)
            for f in (FT - 2, FT - 1):
                act_panels(act, base + 3 * f + 2, 3)
                hidden(f)
            act_panels(act, base + 3 * FT + 2, 1)

        def ffn_dve(dve, n, order):
            base, s0 = FIRST[("ffn", n)], FT * n

            def hidden(f, i=0, between=None):
                dve.wait_ge(silu_done, s0 + f + 1 + 2 * i)
                if s0 + f >= 2:
                    dve.wait_ge(f_lo_done, s0 + f - 1 + 2 * i)
                dve.tensor_tensor(ffn_buf[:, 2 + f % 2, :], ffn_buf[:, f % 2, :],
                                  up_bank(f)[:, SEQ:2 * SEQ], ALU.mult).then_inc(hidden_done, 1)
                if between:
                    between()
                dve.wait_ge(f_hi_done, s0 + f + 1 + 2 * i)
                dve.tensor_tensor(f_lo[:, f % 2, :], ffn_buf[:, 2 + f % 2, :],
                                  f_hi[:, f % 2, :].bitcast(F32), ALU.subtract).then_inc(f_lo_done, 1)

            def tiles(lo, hi, middle=False, late=False):
                with dve.Fori(lo, hi) as i:
                    for f in (2, 3):
                        for j in range(3):
                            split_lo(dve, base + 3 * f + 2 + j, i)
                        if middle:
                            hidden(f, i, between=lambda: ada_add_middle(dve, (0, 2)[f - 2], i))
                            for c in ((1,), (3, 4))[f - 2]:
                                ada_add_middle(dve, c, i)
                        elif late and f == 3:
                            hidden(f, i, between=lambda: ada_add_late(dve, i))
                        else:
                            hidden(f, i)

            dve_panels(dve, base + 3, 2)
            hidden(0)
            dve_panels(dve, base + 5, 3)
            hidden(1)
            if n == 0:
                dve.wait_ge(acc_ready, 16)
                tiles(0, KT, middle=True)
                tiles(KT, FT // 2 - 2)
                ada_middle_dve(dve, order)
            elif n == 1:
                dve.wait_ge(acc_ready, 48)
                tiles(0, KT, late=True)
                tiles(KT, FT // 2 - 2)
                gate_dve(dve, 2, (6, 7), order)
            else:
                tiles(0, FT // 2 - 2)
            for f in (FT - 2, FT - 1):
                dve_panels(dve, base + 3 * f + 2, 3)
                hidden(f)
            dve_panels(dve, base + 3 * FT + 2, 1)

        result_squares = sem("result_squares")
        result_rstd = sem("result_rstd")
        times_gate = sem("times_gate")

        def last_panel(kind, n):
            return FIRST[(kind, n)] + SIZE[kind]

        def wait_result(eng, at, kind, n, q):
            if q < 3:
                eng.wait_ge(result_ready, 3 * at + q + 1)
            else:
                eng.wait_ge(panel_used, last_panel(kind, n))

        def add_act(act, kind, n, at):
            for q in range(4):
                wait_result(act, at, kind, n, q)
                mean_square(act, q, bank[q][:, :], RSS).then_inc(result_squares, 1)

        def add_pool(pool, at, order):
            for m in range(MT):
                pool.wait_ge(result_squares, 4 * at + 2 * m + 2)
                rstd_pool(pool, order, RSS, RRS, m).then_inc(result_rstd, 1)

        def add_dve(dve, kind, n, at):
            if at >= 3:
                for q in range(4):
                    wait_result(dve, at, kind, n, q)
                    x = X[:, q // 2, quarter(q)]
                    dve.scalar_tensor_tensor(out=x, in0=bank[q][:, :],
                                             scalar=0.5 if kind == "ffn" else 1.0, in1=x,
                                             op0=ALU.mult, op1=ALU.add).then_inc(x_done, 1)
                return
            for q in range(4):
                dve.wait_ge(result_squares, 4 * at + q + 1)
                dve.tensor_tensor(gated_sum[:, q // 2, quarter(q)], bank[q][:, :],
                                  gate_rows[:, at, quarter(q)], ALU.mult).then_inc(times_gate, 1)
            dve.wait_ge(times_gate, 4 * at + 4)
            for q in range(4):
                m = q // 2
                dve.wait_ge(result_rstd, 2 * at + m + 1)
                x = X[:, m, quarter(q)]
                dve.scalar_tensor_tensor(out=x, in0=gated_sum[:, m, quarter(q)],
                                         scalar=stat[:, RRS + m:RRS + m + 1], in1=x,
                                         op0=ALU.mult, op1=ALU.add).then_inc(x_done, 1)
        c_ready = sem("c_ready")
        x_loaded = sem("x_loaded")
        small_loaded = sem("small_loaded")
        const_ready = sem("const_ready")
        acc_ready = sem("acc_ready")
        gate_1_loaded = [sem(f"gate_1_loaded{i}") for i in range(ADA_RING)]
        late_loaded = sem("late_loaded")
        gain_loaded = sem("gain_loaded")
        column_sums = sem("column_sums")
        mods_done = sem("mods_done")
        gate_sums = sem("gate_sums")
        c_act = stat[:, 16:16 + KT]

        def ada_multiply_add(dve, a, dst, src, c):
            dve.wait_ge(ada_used, a)
            dve.scalar_tensor_tensor(out=dst, in0=src, scalar=c, in1=dst, op0=ALU.mult,
                                     op1=ALU.add).then_inc(ada_used, 1)

        def ada_add(dve, a, dst):
            slot, k = a % ADA_RING, a % KT
            dve.wait_ge(ada_loaded[slot], 16 * (a // ADA_RING + 1))
            if k == 0:
                dve.tensor_scalar(dst, ada_ring[:, slot, :], c_act[:, 0:1], None,
                                  ALU.mult).then_inc(ada_used, 1)
            else:
                ada_multiply_add(dve, a, dst, ada_ring[:, slot, :], c_act[:, k:k + 1])

        def ada_add_gate_1(dve, k):
            slot = k % ADA_RING
            dve.wait_ge(gate_1_loaded[slot], 16 * (k // ADA_RING + 1))
            ada_multiply_add(dve, ADA_GATE_1 + k, acc_gate_1, ada_ring[:, slot, :], c_act[:, k:k + 1])

        def ada_add_middle(dve, c, i):
            a = ADA_FIRST + c
            slot = a % ADA_RING
            dve.wait_ge(ada_loaded[slot], 16 * (a // ADA_RING + 1) + 16 * i)
            c_k = c_act.rearrange("p (k o) -> p k o", o=1)[:, i, :]
            ada_multiply_add(dve, a + ADA_RING * i, acc[:, c, :], ada_ring[:, slot, :], c_k)

        def ada_add_late(dve, i):
            dve.wait_ge(late_loaded, 16 + 16 * i)
            c = c_act.rearrange("p (k o) -> p k o", o=1)
            ada_multiply_add(dve, ADA_GATE_2 + i, acc_gate_2, late_panel, c[:, i, :])

        def sum_columns(pe, part, to, at):
            mm = None
            for k in range(KT):
                mm = pe.matmul(bank[to][:, at + k:at + k + 1], part[:, k * P:(k + 1) * P],
                               ones[:, 0:1], start=True, stop=True)
            return mm

        def ada_first_pe(pe):
            for c in range(2):
                pe.wait_ge(ada_used, 8 * c + 8)
                sum_columns(pe, acc0[:, c, :], 7, 8 * c).then_inc(column_sums, 1)

        def ada_first_dve(dve, order):
            dve.wait_ge(column_sums, 2)
            for j in range(2):
                order(dve.tensor_tensor(mods[:, j, :], bank[7][:, 8 * j:8 * j + 8],
                                        col("b_ada", 8 * j, 8), ALU.add))
            dve.scalar_tensor_tensor(out=pre_scale[:, 0, :], in0=mods[:, 1, :], scalar=1.0,
                                     in1=col("g_pre", 0, 8), op0=ALU.add,
                                     op1=ALU.mult).then_inc(mods_done, 1)

        def gate_pe(pe, r, part, banks, second_wait=None):
            pe.wait_ge(ada_used, (ADA_GATE_1, ADA_GATE_2, ADA_GATE_2 + KT)[r])
            for half, b in enumerate(banks):
                if half and second_wait:
                    pe.wait_ge(*second_wait)
                pe.matmul(bank[b][:, :], ones[:, :], part[:, half * 512:half * 512 + 512],
                          start=True, stop=True).then_inc(gate_sums, 1)

        def gate_dve(dve, r, banks, order):
            dve.wait_ge(gain_loaded, (32, 32, 48)[r])
            for half, b in enumerate(banks):
                dve.wait_ge(gate_sums, 2 * r + half + 1)
                row = gate_rows[:, r, half * 512:half * 512 + 512]
                order(dve.scalar_tensor_tensor(out=row, in0=bank[b][:, :], scalar=1.0 if r == 1 else 0.5,
                                               in1=row, op0=ALU.mult, op1=ALU.mult))

        def ada_middle_pe(pe):
            pe.wait_ge(ada_used, ADA_GATE_1)
            pe.wait_ge(b_evacuated, 2)
            for j in range(4):
                sum_columns(pe, acc[:, 1 + j, :], 6, 8 * j).then_inc(column_sums, 1)
            gate_pe(pe, 0, acc[:, 0, :], (7, 6), second_wait=(mods_done, 2))

        def ada_middle_dve(dve, order):
            dve.wait_ge(column_sums, 6)
            for j in range(4):
                order(dve.tensor_tensor(mods[:, 2 + j, :], bank[6][:, 8 * j:8 * j + 8],
                                        col("b_ada", 8 * ADA_MIDDLE[1 + j], 8), ALU.add))
            order(dve.scalar_tensor_tensor(out=pre_scale[:, 1, :], in0=mods[:, 3, :], scalar=1.0,
                                           in1=col("g_pre", 8, 8), op0=ALU.add, op1=ALU.mult))
            dve.scalar_tensor_tensor(out=pre_scale[:, 2, :], in0=mods[:, 5, :], scalar=1.0,
                                     in1=col("g_pre", 16, 8), op0=ALU.add,
                                     op1=ALU.mult).then_inc(mods_done, 1)
            gate_dve(dve, 0, (7, 6), order)

        def start_gate(pool, order, dst, r):
            order(pool.memset(dst, 0.0))
            pool.dma_start(dst[0:1, :], rows[r:r + 1, :]).then_inc(acc_ready, 16)

        def load_gain(pool, r):
            pool.dma_start(gate_rows[:, r, :], rows[3 + r:4 + r, :].partition_broadcast(P)).then_inc(
                gain_loaded, 16)

        def ada_middle_pool(pool, order):
            pool.wait_ge(h_lo_done, KT)
            order(pool.memset(acc[:, 1:, :], 0.0))
            start_gate(pool, order, acc[:, 0, :], 0)

        def load_gate_1(pool, lo, hi):
            for k in range(lo, hi):
                slot = k % ADA_RING
                pool.wait_ge(ada_used, ADA_GATE_1 + max(k - (ADA_RING - 1), 0))
                pool.dma_start(ada_ring[:, slot, :], ada[ADA_GATE_1 + k]).then_inc(gate_1_loaded[slot], 16)

        def gate_rows_pool(pool, order):
            pool.wait_ge(b_evacuated, 2)
            load_gain(pool, 0)
            load_gain(pool, 1)
            start_gate(pool, order, acc_gate_1, 1)
            load_gate_1(pool, 0, ADA_RING)

        def gate_2_pool(pool, order):
            pool.wait_ge(x_done, 8)
            load_gain(pool, 2)
            start_gate(pool, order, acc_gate_2, 2)
            with pool.Fori(0, KT) as i:
                pool.wait_ge(ada_used, ADA_GATE_2 + i)
                pool.dma_start(late_panel, ada[ADA_GATE_2 + i]).then_inc(late_loaded, 16)

        DT, XR, YI, T0, T1, T2, SIN, SINH, TANH, REC, RAD, EM1, COSM1, COS, LR, LI, CR, CI, INV = range(19)
        angles_ready = sem("angles_ready")
        angles_done = sem("angles_done")
        params_done = sem("params_done")
        ssm_loaded = sem("ssm_loaded")
        b_ready = sem("b_ready")
        b_in_psum = sem("b_in_psum")
        b_evacuated = sem("b_evacuated")
        rot_ready = sem("rot_ready")

        def pr(i):
            return par[:, i, :]

        def round_off(dve, order, arg, k, turns, hi, lo):
            order(dve.tensor_scalar(k, arg, turns, MAGIC, ALU.mult, ALU.add))
            order(dve.tensor_scalar(k, k, -MAGIC, None, ALU.add))
            order(dve.scalar_tensor_tensor(out=arg, in0=k, scalar=-hi, in1=arg, op0=ALU.mult, op1=ALU.add))
            order(dve.scalar_tensor_tensor(out=arg, in0=k, scalar=-lo, in1=arg, op0=ALU.mult, op1=ALU.add))

        def params_dve(dve, order):
            order(dve.tensor_copy(pr(T0), col("log_step", 0, 16)))
            round_off(dve, order, pr(T0), pr(T1), 1.0 / math.log(2.0), LN2_HI, LN2_LO)
            order(dve.tensor_scalar(pr(T2), pr(T0), 1.0 / 40320, None, ALU.mult))
            for n in (7, 6, 5, 4, 3, 2, 1):
                order(dve.scalar_tensor_tensor(out=pr(T2), in0=pr(T2), scalar=1.0 / math.factorial(n),
                                               in1=pr(T0), op0=ALU.add, op1=ALU.mult))
            order(dve.tensor_scalar(pr(T1), pr(T1), -126.0, 127.0, ALU.max, ALU.min))
            order(dve.tensor_scalar(pr(DT).bitcast(I32), pr(T1), 127.0, 8388608.0, ALU.add, ALU.mult))
            order(dve.scalar_tensor_tensor(out=pr(DT), in0=pr(T2), scalar=1.0, in1=pr(DT),
                                           op0=ALU.add, op1=ALU.mult))
            order(dve.tensor_tensor(pr(XR), pr(DT), col("a_re", 0, 16), ALU.mult))
            order(dve.tensor_tensor(pr(YI), pr(DT), col("a_im", 0, 16), ALU.mult))
            round_off(dve, order, pr(YI), pr(T1), 1.0 / TWO_PI, TWO_PI_HI, TWO_PI_LO)
            dve.tensor_scalar(pr(YI), pr(YI), PI_BELOW, -PI_BELOW, ALU.min,
                              ALU.max).then_inc(angles_ready, 1)

        def params_rest_dve(dve, order):
            dve.wait_ge(angles_done, 3)
            order(dve.tensor_scalar(pr(REC), pr(TANH), -1.0, 1.0, ALU.mult, ALU.add))
            order(dve.reciprocal(pr(REC), pr(REC)))
            order(dve.scalar_tensor_tensor(out=pr(RAD), in0=pr(TANH), scalar=1.0, in1=pr(REC),
                                           op0=ALU.add, op1=ALU.mult))
            order(dve.scalar_tensor_tensor(out=pr(EM1), in0=pr(TANH), scalar=2.0, in1=pr(REC),
                                           op0=ALU.mult, op1=ALU.mult))
            order(dve.scalar_tensor_tensor(out=pr(COSM1), in0=pr(SINH), scalar=-2.0, in1=pr(SINH),
                                           op0=ALU.mult, op1=ALU.mult))
            order(dve.tensor_scalar(pr(COS), pr(COSM1), 1.0, None, ALU.add))
            order(dve.tensor_tensor(pr(LR), pr(EM1), pr(COS), ALU.mult))
            order(dve.tensor_tensor(pr(LR), pr(LR), pr(COSM1), ALU.add))
            order(dve.tensor_tensor(pr(LI), pr(RAD), pr(SIN), ALU.mult))
            are, aim = col("a_re", 0, 16), col("a_im", 0, 16)
            order(dve.tensor_tensor(pr(T0), are, are, ALU.mult))
            order(dve.tensor_tensor(pr(T1), aim, aim, ALU.mult))
            order(dve.tensor_tensor(pr(INV), pr(T0), pr(T1), ALU.add))
            order(dve.reciprocal(pr(INV), pr(INV)))
            order(dve.tensor_tensor(pr(T0), pr(LR), are, ALU.mult))
            order(dve.tensor_tensor(pr(T1), pr(LI), aim, ALU.mult))
            order(dve.tensor_tensor(pr(T0), pr(T0), pr(T1), ALU.add))
            order(dve.tensor_tensor(pr(CR), pr(T0), pr(INV), ALU.mult))
            order(dve.tensor_tensor(pr(T0), pr(LI), are, ALU.mult))
            order(dve.tensor_tensor(pr(T1), pr(LR), aim, ALU.mult))
            order(dve.tensor_tensor(pr(T0), pr(T0), pr(T1), ALU.subtract))
            dve.tensor_tensor(pr(CI), pr(T0), pr(INV), ALU.mult).then_inc(params_done, 1)

        def params_act(act):
            act.wait_ge(angles_ready, 1)
            act.activation(pr(SIN), pr(YI), ACT.Sin).then_inc(angles_done, 1)
            act.activation(pr(SINH), pr(YI), ACT.Sin, scale=0.5).then_inc(angles_done, 1)

        def params_rest_act(act):
            act.activation(pr(TANH), pr(XR), ACT.Tanh, scale=0.5).then_inc(angles_done, 1)

        def wide(ap, *shape):
            return ap.unsqueeze(2).to_broadcast([ap.shape[0], 16, shape[0]])

        def params_pool(pool, order):
            pool.wait_ge(params_done, 1)
            pool.wait_ge(spectrum_stored, 32)
            pool.dma_start(ssm_raw[:, :, :], ssm_mats).then_inc(ssm_loaded, 16)
            order(pool.memset(b_rows[:, :, :], 0.0))
            order(pool.memset(c_rows[:, :, :, :], 0.0))
            pool.wait_ge(ssm_loaded, 16)
            B = [ssm_raw[:, j, :].rearrange("p (s h) -> p s h", h=16) for j in range(4)]
            prod = region(12288, 2, 256)
            pa, pb = [prod[:, j, :].rearrange("p (s h) -> p s h", h=16) for j in range(2)]
            for part, (u, v, op) in enumerate(((B[0], B[1], ALU.subtract), (B[1], B[0], ALU.add))):
                order(pool.tensor_tensor(pa, u, wide(pr(CR), 16), ALU.mult))
                order(pool.tensor_tensor(pb, v, wide(pr(CI), 16), ALU.mult))
                dst = b_rows[:, part, :].rearrange("p (s c) -> p s c", c=32)
                for half in range(2):
                    r, c = slice(64 * half, 64 * half + 64), slice(16 * half, 16 * half + 16)
                    order(pool.tensor_tensor(dst[r, :, c], pa[r, :, :], pb[r, :, :], op))
            pool.sem_inc(b_ready, 1)
            for part, (src, sign) in enumerate(((B[2], 1.0), (B[2], -1.0), (B[3], -1.0))):
                for half in range(2):
                    r, c = slice(64 * half, 64 * half + 64), slice(16 * half, 16 * half + 16)
                    order(pool.tensor_scalar(c_rows[r, part, :, c], src[r, :, :], sign, 1.0,
                                             ALU.mult, ALU.mult))
            rc, rs = rot[:, 0, :, :], rot[:, 1, :, :]
            order(pool.memset(rc[:, :, 0:1], 1.0))
            order(pool.memset(rs[:, :, 0:1], 0.0))
            c1, s1 = pr(COS), pr(SIN)
            w = 1
            while w < SEQ:
                tmp = rot_tmp[:, :, 0:w]
                new = slice(w, 2 * w)
                order(pool.tensor_tensor(rc[:, :, new], rc[:, :, 0:w], wide(c1, w), ALU.mult))
                order(pool.tensor_tensor(tmp, rs[:, :, 0:w], wide(s1, w), ALU.mult))
                order(pool.tensor_tensor(rc[:, :, new], rc[:, :, new], tmp, ALU.subtract))
                order(pool.tensor_tensor(rs[:, :, new], rc[:, :, 0:w], wide(s1, w), ALU.mult))
                order(pool.tensor_tensor(tmp, rs[:, :, 0:w], wide(c1, w), ALU.mult))
                order(pool.tensor_tensor(rs[:, :, new], rs[:, :, new], tmp, ALU.add))
                w *= 2
                if w < SEQ:
                    order(pool.tensor_tensor(pr(T0), c1, c1, ALU.mult))
                    order(pool.tensor_tensor(pr(T1), s1, s1, ALU.mult))
                    order(pool.tensor_tensor(pr(T2), c1, s1, ALU.mult))
                    order(pool.tensor_tensor(pr(DT), pr(T0), pr(T1), ALU.subtract))
                    order(pool.tensor_tensor(pr(XR), pr(T2), pr(T2), ALU.add))
                    order(pool.tensor_copy(pr(LR), pr(DT)))
                    order(pool.tensor_copy(pr(LI), pr(XR)))
                    c1, s1 = pr(LR), pr(LI)
            pool.sem_inc(rot_ready, 1)

        def turn_b_pe(pe):
            pe.wait_ge(b_ready, 1)
            for part in range(2):
                for q in range(4):
                    tr = pe.transpose(bank[6 + part][:, q * P:(q + 1) * P],
                                      b_rows[:, part, q * P:(q + 1) * P], ident[:, :])
                tr.then_inc(b_in_psum, 1)

        def turn_b_act(act):
            for part in range(2):
                act.wait_ge(b_in_psum, part + 1)
                act.activation(b_turned[:, part, :, :].rearrange("p q s -> p (q s)"),
                               bank[6 + part][:, :], ACT.Copy).then_inc(b_evacuated, 1)

        spec_loaded = sem("spec_loaded")
        decay_loaded = sem("decay_loaded")
        mlp_product = sem("mlp_product")
        mlp_arg = sem("mlp_arg")
        mlp_sin = sem("mlp_sin")
        taps_product = sem("taps_product")
        decay_done = sem("decay_done")
        taps_done = sem("taps_done")
        tap_squares = sem("tap_squares")
        tap_sums = sem("tap_sums")
        filter_sums = sem("filter_sums")
        squares_added = sem("squares_added")
        filter_scaled = sem("filter_scaled")
        even_odd = sem("even_odd")
        spec_product = sem("spec_product")
        spec_done = sem("spec_done")
        spectrum_stored = sem("spectrum_stored")
        dft = region(11264, 2, 2, SEQ)
        filter_out = region(14336, 2048)
        taps = region(16384, 4, 512)
        decays = region(18432, MT, 1024)
        eo = region(20480, 4, 512)
        spec = region(22528, 4, 512)
        filter_scale = stat[:, 48:56]
        tap_sq = [region(at, 512) for at in (24576, 25088, 25600, 1024)]
        decay_rows = region(0, 1024)
        mlp = region(13312, 1024)
        feat_t, mlp_ws = mlp[0:33, 0:256], mlp[0:64, 256:448]
        mlp_h, mlp_k = mlp[0:64, 448:704], mlp[0:64, 704:960]

        def filter_sums_pe(pe, o):
            pe.wait_ge(squares_added, o + 1)
            for c in range(4):
                mm = pe.matmul(bank[6][:, 4 * o + c:4 * o + c + 1], tap_sq[0][:, c * P:(c + 1) * P],
                               ones[:, 0:1], start=True, stop=True)
            mm.then_inc(tap_sums, 1)

        TAP_BANKS = ((0, 1, 2, 3), (4, 5, 7, 0))
        SPEC_BANKS = (1, 2, 3, 0)

        def spectrum_pe(pe):
            pe.wait_ge(spec_loaded, 16 * 2)
            for layer in range(3):
                if layer:
                    pe.wait_ge(mlp_sin, layer)
                    pe.matmul(bank[7][0:64, 0:SEQ], mlp[0:64, 256 + 64 * layer:320 + 64 * layer],
                              mlp_h, start=True, stop=True).then_inc(mlp_product, 1)
                else:
                    pe.matmul(bank[7][0:64, 0:SEQ], mlp[0:33, 256:320], feat_t,
                              start=True, stop=True).then_inc(mlp_product, 1)
            pe.wait_ge(mlp_sin, 3)
            pe.wait_ge(spec_loaded, 16 * 5)
            for o in range(2):
                for q in range(4):
                    m, d = q // 2, q % 2
                    if (o, q) == (1, 3):
                        pe.wait_ge(taps_done, 1)
                    pe.matmul(bank[TAP_BANKS[o][q]][:, :], mlp_h[:, m * P:(m + 1) * P],
                              filter_out[0:64, o * 1024 + d * 512:o * 1024 + d * 512 + 512],
                              start=True, stop=True).then_inc(taps_product, 1)
            for o in range(2):
                if o:
                    filter_sums_pe(pe, 0)
                pe.wait_ge(even_odd, 4 * o + 4)
                for q in range(4):
                    pe.wait_ge(*((spec_done, q + 1) if o else (taps_done, (2, 3, 4, 8)[q])))
                    f, s = q // 2, q % 2
                    for m in range(MT):
                        mm = pe.matmul(bank[SPEC_BANKS[q]][:, :], dft[:, s, m, f * P:(f + 1) * P],
                                       eo[:, 2 * m + s, :], start=m == 0, stop=m == MT - 1)
                    mm.then_inc(spec_product, 1)
            filter_sums_pe(pe, 1)

        def spectrum_dve(dve, order, spare):
            for layer in range(3):
                dve.wait_ge(mlp_product, layer + 1)
                order(dve.tensor_scalar(mlp_h, bank[7][0:64, 0:SEQ], col("mlp_b", layer)[0:64, :],
                                        col("sin_freq", layer)[0:64, :], ALU.add, ALU.mult))
                round_off(dve, order, mlp_h, mlp_k, 1.0 / TWO_PI, TWO_PI_HI, TWO_PI_LO)
                dve.tensor_scalar(mlp_h, mlp_h, PI_BELOW, -PI_BELOW, ALU.min,
                                  ALU.max).then_inc(mlp_arg, 1)
                if layer == 0:
                    params_dve(dve, order)
                    dve.wait_ge(c_ready, 1)
                else:
                    spare()
            params_rest_dve(dve, order)
            for _ in range(3):
                spare()
            for o in range(2):
                for q in range(4):
                    m, d = q // 2, q % 2
                    dve.wait_ge(taps_product, 4 * o + q + 1)
                    dve.wait_ge(decay_done, 2 * o + m + 1)
                    if o:
                        dve.wait_ge(even_odd, 4)
                        dve.wait_ge(tap_squares, 4)
                    ins = dve.tensor_tensor(taps[:, q, :], bank[TAP_BANKS[o][q]][:, :],
                                            decays[:, m, d * 512:d * 512 + 512], ALU.mult)
                    if q == 1:
                        order(ins)
                        ins = dve.memset(taps[0:1, 1, :], 0.0)
                    ins.then_inc(taps_done, 1)
                    if q == 1:
                        spare()
                for _ in range(3 * o):
                    spare()
                dve.wait_ge(taps_done, 4 * o + 4)
                if o:
                    dve.wait_ge(spec_product, 4)
                for m in range(MT):
                    dve.tensor_tensor(eo[:, 2 * m + 1, :], taps[:, 2 * m, :], taps[:, 2 * m + 1, :],
                                      ALU.subtract).then_inc(even_odd, 1)
                for _ in range(3):
                    spare()

        def filter_sums_dve(dve):
            dve.wait_ge(tap_sums, 2)
            dve.tensor_copy(filter_scale, bank[6][:, 0:8]).then_inc(filter_sums, 1)

        def spectrum_act(act, order):
            for layer in range(3):
                act.wait_ge(mlp_arg, layer + 1)
                then(act, act.activation(mlp_h, mlp_h, ACT.Sin), mlp_sin, layer + 1)
                if layer == 0:
                    params_act(act)
            params_rest_act(act)

            def decay_factors(o):
                act.wait_ge(decay_loaded, 16 * (o + 1))
                order(act.activation(decay_rows, decay_rows, ACT.Abs))
                if o:
                    act.wait_ge(taps_done, 4)
                for m in range(MT):
                    at = COLS["neg_t"][0] + m
                    act.activation(decays[:, m, :], decay_rows, ACT.Exp,
                                   scale=C[:, at:at + 1]).then_inc(decay_done, 1)

            decay_factors(0)
            act.wait_ge(decay_done, 2)
            act.dma_start(decay_rows, decay[1:2, :].partition_broadcast(P)).then_inc(decay_loaded, 16)
            for o in range(2):
                if o:
                    act.wait_ge(tap_sums, 1)
                for q in range(4):
                    act.wait_ge(taps_done, 4 * o + q + 1)
                    act.activation(tap_sq[q], taps[:, q, :], ACT.Square).then_inc(tap_squares, 1)
                if o == 0:
                    decay_factors(1)
            for o in range(2):
                if o:
                    act_panels(act, 0, 3)
                    act.wait_ge(spectrum_stored, 16)
                for q in range(4):
                    act.wait_ge(spec_product, 4 * o + q + 1)
                    act.activation(spec[:, q, :], bank[SPEC_BANKS[q]][:, :], ACT.Copy).then_inc(spec_done, 1)

        def spectrum_pool(pool, order):
            def even(o):
                pool.wait_ge(taps_done, 4 * o + 4)
                if o:
                    pool.wait_ge(spec_product, 4)
                for m in range(MT):
                    pool.tensor_tensor(eo[:, 2 * m, :], taps[:, 2 * m, :], taps[:, 2 * m + 1, :],
                                       ALU.add).then_inc(even_odd, 1)

            def add_squares(o):
                pool.wait_ge(tap_squares, 4 * o + 4)
                order(pool.tensor_tensor(tap_sq[0], tap_sq[0], tap_sq[1], ALU.add))
                order(pool.tensor_tensor(tap_sq[2], tap_sq[2], tap_sq[3], ALU.add))
                pool.tensor_tensor(tap_sq[0], tap_sq[0], tap_sq[2], ALU.add).then_inc(squares_added, 1)

            def store(o):
                pool.wait_ge(spec_done, 4 * o + 4)
                pool.dma_start(spectrum[o], spec[:, :, :]).then_inc(spectrum_stored, 16)

            even(0)
            add_squares(0)
            even(1)
            store(0)
            add_squares(1)
            store(1)
            pool.wait_ge(filter_sums, 1)
            for o in range(2):
                f = filter_scale[:, 4 * o:4 * o + 4]
                pool.tensor_tensor(f, f, stat[:, MINUS_HALF:MINUS_HALF + 4], ALU.pow).then_inc(filter_scaled, 1)

        u_t = region(4096, 4, SEQ)
        q_t = region(5120, 4, SEQ)
        y32 = region(5120, 4, SEQ)
        p_turned = region(6144, 2, 384)
        attn = region(6912, 2, 512)
        turned_back = region(7936, 2, SEQ)
        states = (region(8448, 2, SEQ), region(3456, 2, SEQ))
        rot_out = region(8960, 2, 4, SEQ)
        scores = region(0, 8, 384)
        near_sb = region(3072, 384)
        k_t = region(25088, SEQ)
        v_t = region(25344, SEQ)
        v_tok = region(25600, MT, P)
        sink_row = stat[:, 24:32]
        gate_in = region(0, 4, SEQ)
        rms_col = stat[:, 40:44]
        rms_diag = region(4096, 4, P)
        y_squares = region(1024, 4, SEQ)
        max3 = region(11008, 8, 3)
        m1_small = region(11040, 6, 16)
        NEGMAX, SUMS, SINK, RDEN = range(4)

        m1_evac = sem("m1_evac")
        v_turned = sem("v_turned")
        v_ready = sem("v_ready")
        near_loaded = sem("near_loaded")
        sc_product = sem("sc_product")
        sc_biased = sem("sc_biased")
        sc_max = sem("sc_max")
        sc_exp = sem("sc_exp")
        p_in_psum = sem("p_in_psum")
        p_evac = sem("p_evac")
        pv_done = sem("pv_done")
        attn_done = sem("attn_done")
        attn_squares = sem("attn_squares")
        attn_rstd = sem("attn_rstd")
        attn_scaled = sem("attn_scaled")
        attn_turned = sem("attn_turned")
        m_evac = sem("m_evac")
        m_hi = sem("m_hi")
        m_lo = sem("m_lo")
        bu_done = sem("bu_done")
        bu_read = sem("bu_read")
        states_done = sem("states_done")
        rot_done = sem("rot_done")
        y_done = sem("y_done")
        y_skip = sem("y_skip")
        gelu_done = sem("gelu_done")
        y_hi = sem("y_hi")
        y_lo = sem("y_lo")
        sig_done = sem("sig_done")
        gated = sem("gated")
        gsq_done = sem("gsq_done")
        gsum_done = sem("gsum_done")
        rms_mean = sem("rms_mean")
        rms_pow = sem("rms_pow")
        rms_diag_done = sem("rms_diag_done")
        rms_rows = sem("rms_rows")
        M1 = FIRST[("mix1", 0)]

        def pow_pool(pool, n):
            c = rms_col[:, 0:n]
            pool.tensor_tensor(c, c, stat[:, MINUS_HALF:MINUS_HALF + n], ALU.pow).then_inc(rms_pow, 1)

        def diagonals_dve(dve, n, ready, done):
            dve.wait_ge(*ready)
            for j in range(n):
                dve.tensor_scalar(rms_diag[:, j, :], ident[:, :], rms_col[:, j:j + 1], None,
                                  ALU.mult).then_inc(done, 1)

        def rows_pe(pe, to, n, ready, done):
            pe.wait_ge(ready[0], ready[1] * n)
            for j in range(n):
                mm = pe.matmul(to[:, j * P:(j + 1) * P], ones[:, :], rms_diag[:, j, :], start=True, stop=True)
            mm.then_inc(done, 1)

        def m1_projection_pe(pe, j):
            if j >= 2:
                pe.wait_ge(m1_evac, j - 1)
            channel_product(pe, up_bank(j)[:, 0:SEQ], M1 + j, norm=1 if j == 0 else None)

        def attention_pe(pe, head):
            kv, j = head // 4, head % 4
            r = slice(64 * kv, 64 * kv + 64)
            b = bank[4 + head % 2]
            if head >= 2:
                pe.wait_ge(sc_biased, head - 1)
            pe.matmul(b[:, 0:P], q_t[r, j, 0:P], k_t[r, 0:P], start=True, stop=True)
            pe.matmul(b[:, P:3 * P], q_t[r, j, P:SEQ], k_t[r, :], start=True,
                      stop=True).then_inc(sc_product, 1)

        def attention_values_pe(pe, head):
            pe.wait_ge(sc_exp, 2 * head + 2)
            b = bank[4 + head % 2]
            if head >= 2:
                pe.wait_ge(p_evac, head - 1)
            for c in range(3):
                tr = pe.transpose(b[:, c * P:(c + 1) * P], scores[:, head, c * P:(c + 1) * P], ident[:, :])
            tr.then_inc(p_in_psum, 1)

        def attention_out_pe(pe, head):
            kv = head // 4
            pe.wait_ge(p_evac, head + 1)
            v = slice(64 * kv, 64 * kv + 64)
            o = slice(64 * head, 64 * head + 64)
            p = p_turned[:, head % 2, :]
            pe.matmul(bank[0][:, o], p[:, 0:P], v_tok[:, 0, v], start=True, stop=True)
            pe.matmul(bank[1][:, o], p[:, P:2 * P], v_tok[:, 0, v], start=True, stop=False)
            pe.matmul(bank[1][:, o], p[:, 2 * P:3 * P], v_tok[:, 1, v], start=False,
                      stop=True).then_inc(pv_done, 1)

        def input_pe(pe, s):
            q, r = s // 4, slice(32 * (s % 4), 32 * (s % 4) + 32)
            if s >= 2:
                pe.wait_ge(bu_read, s - 1)
            for part in range(2):
                mm = pe.matmul(bank[2 + s % 2][:, part * SEQ:(part + 1) * SEQ], b_turned[r, part, q, :],
                               u_t[r, q, :], start=True, stop=True)
            mm.then_inc(bu_done, 1)

        def output_pe(pe, s):
            q, r = s // 4, slice(32 * (s % 4), 32 * (s % 4) + 32)
            pe.wait_ge(rot_done, 2 * s + 2)
            o = bank[6 + q // 2][r, (q % 2) * SEQ:(q % 2 + 1) * SEQ]
            for n, (part, term) in enumerate(((0, 0), (2, 1), (2, 2), (1, 3))):
                mm = pe.matmul(o, c_rows[:, part, s, :], rot_out[:, s % 2, term, :], start=n == 0,
                               stop=n == 3)
            mm.then_inc(y_done, 1)

        def mix1_pe(pe):
            for j in range(6):
                m1_projection_pe(pe, j)
            pe.wait_ge(rot_ready, 1)
            pe.wait_ge(m1_evac, 4)
            input_pe(pe, 0)
            input_pe(pe, 1)
            for s in range(STATE_TILES):
                if s < 4:
                    m1_projection_pe(pe, 6 + s)
                if s == 4:
                    pe.wait_ge(m1_evac, 10)
                    for m in range(MT):
                        tr = pe.transpose(bank[4][:, m * P:(m + 1) * P], v_t[:, m * P:(m + 1) * P],
                                          ident[:, :])
                    tr.then_inc(v_turned, 1)
                    gate_pe(pe, 1, acc_gate_1, (0, 1))
                    pe.wait_ge(v_ready, 1)
                if 4 <= s < 8:
                    attention_pe(pe, 2 * s - 8)
                    attention_pe(pe, 2 * s - 7)
                if s == 8:
                    pe.wait_ge(sc_biased, 8)
                if 8 <= s < 12:
                    for head in (2 * s - 16, 2 * s - 15):
                        attention_values_pe(pe, head)
                if 9 <= s < 13:
                    for head in (2 * s - 18, 2 * s - 17):
                        attention_out_pe(pe, head)
                if s + 2 < STATE_TILES:
                    input_pe(pe, s + 2)
                if s:
                    output_pe(pe, s - 1)
            turn_attention_pe(pe)
            output_pe(pe, STATE_TILES - 1)
            pe.wait_ge(y_lo, 4)
            for n in range(4):
                channel_product(pe, bank[6 + n // 2][:, (n % 2) * SEQ:(n % 2 + 1) * SEQ],
                                M1 + 10 + n // 2, k_tiles=4, at=(n % 2) * 512, k0=4, used=n % 2 == 1)

            def out_product(k):
                pe.wait_ge(m_lo, k // 2 + 1)
                token_product(pe, M1 + 12 + k, h_hi[:, k, :], h_lo[:, k, :], k == 0, k == KT - 1)

            out_product(0)
            out_product(1)
            pe.wait_ge(gsq_done, 4)
            for m in range(MT):
                for n in range(4):
                    mm = pe.matmul(bank[4][:, m:m + 1], y_squares[:, n, m * P:(m + 1) * P],
                                   ones[:, 0:1], start=n == 0, stop=n == 3)
            mm.then_inc(gsum_done, 1)
            rows_pe(pe, bank[4], MT, (rms_diag_done, 1), rms_rows)
            for k in range(2, KT):
                out_product(k)

        def turn_attention_pe(pe):
            pe.wait_ge(attn_scaled, 2)
            for k in range(4):
                for m in range(MT):
                    tr = pe.transpose(bank[4 + k // 2][:, (k % 2) * SEQ + m * P:(k % 2) * SEQ + m * P + P],
                                      attn[:, m, k * P:(k + 1) * P], ident[:, :])
                if k % 2:
                    tr.then_inc(attn_turned, 1)

        def mix1_act(act, order):
            for j in range(10):
                split_hi(act, M1 + 3 + j)
                act.wait_ge(panel_used, M1 + j + 1)
                src = up_bank(j)[:, 0:SEQ]
                if j < 4:
                    ins = act.activation(u_t[:, j, :], src, ACT.Copy)
                elif j < 8:
                    ins = act.activation(q_t[:, j - 4, :], src, ACT.Copy, scale=HD ** -0.5)
                else:
                    ins = act.activation(k_t if j == 8 else v_t, src, ACT.Copy)
                ins.then_inc(m1_evac, 1)
            act_panels(act, M1 + 13, 3)
            act.wait_ge(v_turned, 1)
            act.activation(v_tok[:, :, :].rearrange("p m c -> p (m c)"), bank[4][:, 0:SEQ],
                           ACT.Copy).then_inc(v_ready, 1)
            for head in range(8):
                if head % 4 == 0:
                    act.wait_ge(sc_max, 3 * head // 4 + 3)
                    sink = m1_small[:, SINK, 2 * head:2 * head + 8]
                    order(act.activation(sink, sink, ACT.Exp))
                for b, c in ((0, slice(0, P)), (1, slice(P, 3 * P))):
                    i = 2 * head + b
                    act.activation(scores[:, head, c], scores[:, head, c], ACT.Exp,
                                   bias=m1_small[:, NEGMAX, i:i + 1],
                                   accum_out=m1_small[:, SUMS, i:i + 1]).then_inc(sc_exp, 1)
            for head in range(8):
                act.wait_ge(p_in_psum, head + 1)
                if head >= 2:
                    act.wait_ge(pv_done, head - 1)
                act.activation(p_turned[:, head % 2, :], bank[4 + head % 2][:, 0:384],
                               ACT.Copy).then_inc(p_evac, 1)
            for m in range(MT):
                act.wait_ge(attn_done, m + 1)
                act.activation(region(1024 * m, 512), attn[:, m, :], ACT.Square,
                               accum_out=stat[:, 32 + m:33 + m]).then_inc(attn_squares, 1)
            for k in range(4):
                act.wait_ge(attn_turned, k // 2 + 1)
                act.activation(h32[:, k, :], bank[4 + k // 2][:, (k % 2) * SEQ:(k % 2 + 1) * SEQ],
                               ACT.Copy, scale=col("g_attn", k)).then_inc(m_evac, 1)
            for b in range(2):
                act.wait_ge(m_evac, 2 * b + 2)
                act.activation(h_hi[:, 2 * b:2 * b + 2, :], h32[:, 2 * b:2 * b + 2, :],
                               ACT.Copy).then_inc(m_hi, 1)
            for b in range(2):
                act.wait_ge(y_skip, 2 * b + 2)
                r = slice(2 * b, 2 * b + 2)
                then(act, act.activation(y32[:, r, :], y32[:, r, :], ACT.Gelu_apprx_tanh), gelu_done, b + 1)
                act.activation(h_hi[:, 4 + 2 * b:6 + 2 * b, :], y32[:, r, :], ACT.Copy).then_inc(y_hi, 1)
            for n in range(4):
                act.wait_ge(panel_used, M1 + 11 + n // 2)
                act.activation(gate_in[:, n, :], bank[6 + n // 2][:, (n % 2) * SEQ:(n % 2 + 1) * SEQ],
                               ACT.Sigmoid, bias=col("b_glu", n)).then_inc(sig_done, 1)
            act_panels(act, M1 + 16, 2)
            for n in range(4):
                act.wait_ge(gated, n + 1)
                act.activation(y_squares[:, n, :], gate_in[:, n, :], ACT.Square).then_inc(gsq_done, 1)
            act_panels(act, M1 + 18, 2)
            for b in range(2, 4):
                act.wait_ge(m_evac, 2 * b + 2)
                act.activation(h_hi[:, 2 * b:2 * b + 2, :], h32[:, 2 * b:2 * b + 2, :],
                               ACT.Copy).then_inc(m_hi, 1)
            act_panels(act, M1 + 20, 3)

        def mix1_pool(pool, order):
            pool.wait_ge(x_done, 4)
            load_gate_1(pool, ADA_RING, KT)
            pool.dma_start(sink_row, sinks.partition_broadcast(P)).then_inc(near_loaded, 16)
            pool.wait_ge(h_lo_done, 2 * KT)
            pool.dma_start(near_sb, near).then_inc(near_loaded, 16)
            for s in range(STATE_TILES):
                pool.wait_ge(states_done, 2 * s + 2)
                if s >= 2:
                    pool.wait_ge(y_done, s - 1)
                z = states[s % 2]
                for part in range(2):
                    r = rot[:, part, s, :].unsqueeze(1).to_broadcast([P, 2, SEQ])
                    pool.tensor_tensor(rot_out[:, s % 2, 2 * part:2 * part + 2, :], z, r,
                                       ALU.mult).then_inc(rot_done, 1)
                if s == 13:
                    for m in range(MT):
                        pool.wait_ge(attn_squares, m + 1)
                        ss = stat[:, 32 + m:33 + m]
                        order(pool.tensor_scalar(ss, ss, 1.0 / 512, EPS, ALU.mult, ALU.add))
                        pool.tensor_tensor(ss, ss, stat[:, MINUS_HALF:MINUS_HALF + 1],
                                           ALU.pow).then_inc(attn_rstd, 1)
            pool.wait_ge(rms_mean, 1)
            pow_pool(pool, MT)

        def states_dve(dve, order, s):
            w = bank[2 + s % 2][:, :].rearrange("p (i t) -> p i t", i=2)
            a, x = turned_back, states[s % 2]
            dve.wait_ge(bu_done, s + 1)
            if s:
                dve.wait_ge(states_done, 2 * s)
            if s >= 2:
                dve.wait_ge(rot_done, 2 * s - 2)
            for part, dst in ((0, a), (1, x)):
                r = rot[:, part, s, :].unsqueeze(1).to_broadcast([P, 2, SEQ])
                ins = dve.tensor_tensor(dst, w, r, ALU.mult)
                if part:
                    then(dve, ins, bu_read, s + 1)
                else:
                    order(ins)
            order(dve.tensor_tensor(a[:, 0, :], a[:, 0, :], x[:, 1, :], ALU.add))
            order(dve.tensor_tensor(a[:, 1, :], a[:, 1, :], x[:, 0, :], ALU.subtract))
            r = par[:, RAD, s:s + 1].to_broadcast([P, SEQ])
            for part in range(2):
                dve.tensor_tensor_scan(x[:, part, :], r, a[:, part, :], 0.0, ALU.mult,
                                       ALU.add).then_inc(states_done, 1)

        def mix1_dve(dve, order):
            dve.wait_ge(acc_ready, 32)
            for j in range(KT):
                if j < 6:
                    split_lo(dve, M1 + 3 + j)
                ada_add_gate_1(dve, j)
            dve.wait_ge(ada_used, ADA_GATE_2)
            dve.wait_ge(rot_ready, 1)

            def bias(head):
                dve.wait_ge(sc_product, head + 1)
                then(dve, dve.scalar_tensor_tensor(out=scores[:, head, :], in0=near_sb,
                                                   scalar=2.0 ** -(head + 1),
                                                   in1=bank[4 + head % 2][:, 0:384], op0=ALU.mult,
                                                   op1=ALU.add), sc_biased, head + 1)
                order(dve.tensor_reduce(max3[:, head, :],
                                        scores[:, head, :].rearrange("p (b k) -> p b k", b=3),
                                        AX.X, ALU.max))

            def maxima(half):
                heads, cols = slice(4 * half, 4 * half + 4), slice(8 * half, 8 * half + 8)
                mx = m1_small[:, NEGMAX, cols].rearrange("p (h b) -> p h b", b=2)
                sx = m1_small[:, SINK, cols].rearrange("p (h b) -> p h b", b=2)
                order(dve.tensor_tensor(max3[:, heads, 1], max3[:, heads, 1], max3[:, heads, 2], ALU.max))
                for b in range(2):
                    order(dve.tensor_tensor(mx[:, :, b], max3[:, heads, b], sink_row[:, heads], ALU.max))
                for b in range(2):
                    dve.tensor_tensor(sx[:, :, b], sink_row[:, heads], mx[:, :, b],
                                      ALU.subtract).then_inc(sc_max, 1)
                dve.wait_ge(sc_max, 3 * half + 2)
                dve.tensor_scalar(m1_small[:, NEGMAX, cols], m1_small[:, NEGMAX, cols], -1.0, None,
                                  ALU.mult).then_inc(sc_max, 1)

            def attention_out():
                dve.wait_ge(sc_exp, 16)
                order(dve.tensor_tensor(m1_small[:, RDEN, :], m1_small[:, SUMS, :], m1_small[:, SINK, :],
                                        ALU.add))
                order(dve.reciprocal(m1_small[:, RDEN, :], m1_small[:, RDEN, :]))
                dve.wait_ge(pv_done, 8)
                rd = m1_small[:, RDEN, :].rearrange("p (h b) -> p h b", b=2)
                for b in range(2):
                    r = rd[:, :, b].unsqueeze(2).to_broadcast([P, 8, HD])
                    dve.tensor_tensor(attn[:, b, :].rearrange("p (h d) -> p h d", d=HD),
                                      bank[b][:, :].rearrange("p (h d) -> p h d", d=HD), r,
                                      ALU.mult).then_inc(attn_done, 1)

            def skip(b):
                dve.wait_ge(y_done, 8 * b + 8)
                if b == 0:
                    dve.wait_ge(sc_product, 8)
                for j in range(2):
                    q = 2 * b + j
                    dve.scalar_tensor_tensor(out=y32[:, q, :], in0=u_t[:, q, :], scalar=col("ssm_d", q),
                                             in1=bank[6 + b][:, j * SEQ:(j + 1) * SEQ], op0=ALU.mult,
                                             op1=ALU.add).then_inc(y_skip, 1)

            for s in range(STATE_TILES):
                states_dve(dve, order, s)
                if s < 7:
                    split_lo(dve, M1 + 9 + s)
                if s == 4:
                    gate_dve(dve, 1, (0, 1), order)
                    dve.wait_ge(near_loaded, 32)
                if 4 <= s < 8:
                    bias(2 * s - 8)
                    bias(2 * s - 7)
                    if s % 2:
                        maxima((s - 5) // 2)
                if s == 12:
                    attention_out()
                if s == 13:
                    skip(0)
                if s == 14:
                    for m in range(MT):
                        dve.wait_ge(attn_rstd, m + 1)
                        dve.tensor_scalar(attn[:, m, :], attn[:, m, :], stat[:, 32 + m:33 + m], None,
                                          ALU.mult).then_inc(attn_scaled, 1)
            skip(1)
            for b in range(2):
                dve.wait_ge(m_hi, b + 1)
                r = slice(2 * b, 2 * b + 2)
                dve.tensor_tensor(h_lo[:, r, :], h32[:, r, :], h_hi[:, r, :].bitcast(F32),
                                  ALU.subtract).then_inc(m_lo, 1)
            for b in range(2):
                for j in range(2):
                    dve.wait_ge(y_hi, b + 1)
                    k = 4 + 2 * b + j
                    dve.tensor_tensor(h_lo[:, k, :], y32[:, 2 * b + j, :], h_hi[:, k, :].bitcast(F32),
                                      ALU.subtract).then_inc(y_lo, 1)
            for n in range(4):
                dve.wait_ge(sig_done, n + 1)
                dve.tensor_tensor(gate_in[:, n, :], gate_in[:, n, :], y32[:, n, :],
                                  ALU.mult).then_inc(gated, 1)
            dve_panels(dve, M1 + 16, 2)
            dve.wait_ge(gsum_done, 1)
            dve.tensor_scalar(rms_col[:, 0:MT], bank[4][:, 0:MT], 1.0 / 512, EPS, ALU.mult,
                              ALU.add).then_inc(rms_mean, 1)
            diagonals_dve(dve, MT, (rms_pow, 1), rms_diag_done)
            dve.wait_ge(rms_rows, 1)
            for n in range(4):
                dve.scalar_tensor_tensor(out=h32[:, 4 + n, :], in0=gate_in[:, n, :],
                                         scalar=col("g_ssm", n), in1=bank[4][:, 0:SEQ], op0=ALU.mult,
                                         op1=ALU.mult).then_inc(m_evac, 1)
            dve_panels(dve, M1 + 18, 2)
            for b in range(2, 4):
                dve.wait_ge(m_hi, b + 1)
                r = slice(2 * b, 2 * b + 2)
                dve.tensor_tensor(h_lo[:, r, :], h32[:, r, :], h_hi[:, r, :].bitcast(F32),
                                  ALU.subtract).then_inc(m_lo, 1)
            dve_panels(dve, M1 + 20, 3)

        forward = region(4096, 2, MT, SEQ)
        inverse = region(5120, 2, MT, SEQ)
        averages = region(6144, 4 * MT, SEQ)
        pool_ws = region(8192, 4, P)
        filters = region(8704, 8, 512)
        a_tok = region(12800, MT, 512)
        averaged = region(13824, 4, SEQ)
        conv = region(14848, 12, SEQ)
        z_tok = region(17920, MT, 512)
        product = region(18944, 4, 512)
        terms = region(20992, 4, 512)
        z_bias = region(23040, 4, SEQ)
        z_sum = region(24064, 2, SEQ)

        m2_loaded = sem("m2_loaded")
        a_evac = sem("a_evac")
        conv_centre = sem("conv_centre")
        conv_done = sem("conv_done")
        averages_done = sem("averages_done")
        averages_evac = sem("averages_evac")
        grouped_done = sem("grouped_done")
        z_turned = sem("z_turned")
        z_evac = sem("z_evac")
        z_spectrum = sem("z_spectrum")
        spectra_product = sem("spectra_product")
        z_back = sem("z_back")
        z_biased = sem("z_biased")
        z_done = sem("z_done")
        m2_evac = sem("m2_evac")
        m2_hi = sem("m2_hi")
        m2_lo = sem("m2_lo")
        BACK_BANKS = (6, 7, 4, 5)
        M2 = FIRST[("mix2", 0)]

        def mix2_loads(pool):
            pool.wait_ge(x_done, 12)
            pool.dma_start(forward, pool_mats[4:6].rearrange("i p m t -> p i m t")).then_inc(m2_loaded, 16)
            pool.dma_start(inverse, pool_mats[6:8].rearrange("i p m t -> p i m t")).then_inc(m2_loaded, 16)
            pool.dma_start(averages.rearrange("p (i m) t -> p i m t", m=MT),
                           pool_mats[0:4].rearrange("i p m t -> p i m t")).then_inc(m2_loaded, 16)
            pool.dma_start(pool_ws, pool_w).then_inc(m2_loaded, 16)
            pool.dma_start(filters.rearrange("p (o q) c -> p o q c", o=2),
                           spectrum.rearrange("o p q c -> p o q c")).then_inc(m2_loaded, 16)

        def forward_pe(pe, first_bank, o):
            pe.wait_ge(z_evac, MT * (o + 1))
            for f in range(2):
                for s in range(2):
                    for m in range(MT):
                        mm = pe.matmul(bank[first_bank + 2 * f + s][:, :],
                                       forward[:, s, m, f * P:(f + 1) * P], z_tok[:, m, :],
                                       start=m == 0, stop=m == MT - 1)
                    mm.then_inc(z_spectrum, 1)

        def inverse_pe(pe, o):
            pe.wait_ge(spectra_product, 4 * o + 4)
            for c in range(4):
                if o == 0 and c == 2:
                    pe.wait_ge(conv_done, 12)
                for f in range(2):
                    for s in range(2):
                        mm = pe.matmul(bank[BACK_BANKS[c]][:, 0:SEQ],
                                       product[:, 2 * f + s, c * P:(c + 1) * P], inverse[:, s, f, :],
                                       start=f + s == 0, stop=f + s == 2)
                mm.then_inc(z_back, 1)

        def turn_z_pe(pe, o):
            for c in range(4):
                pe.wait_ge(*((z_done, c + 1) if o else (conv_done, c + 1)))
                for m in range(MT):
                    tr = pe.transpose(bank[2 + m][:, c * P:(c + 1) * P],
                                      conv[:, c, m * P:(m + 1) * P], ident[:, :])
                    if c == 3:
                        tr.then_inc(z_turned, 1)

        def mix2_pe(pe):
            for j in range(4):
                g = M2 + j
                pe.wait_ge(lo_ready, g + 1)
                for half in range(2):
                    k, w = 2 * j + half, slice(512 * half, 512 * half + 512)
                    pe.wait_ge(h_lo_done, KT * 4 + k + 1)
                    for m in range(MT):
                        t = slice(m * P, (m + 1) * P)
                        mm = product3(pe, bank[m][:, :], w_hi[:, g % RING, w], w_lo[:, g % RING, w],
                                      h_hi[:, k, t], h_lo[:, k, t], k == 0, k == KT - 1,
                                      weights_move=True)
                mm.then_inc(panel_used, 1)

            def parts(lo, hi):
                for j in range(lo, hi):
                    if j >= 2:
                        pe.wait_ge(conv_done, j - 1)
                    channel_product(pe, bank[4 + j % 2][:, 0:SEQ], M2 + 4 + j)

            parts(0, 4)
            pe.wait_ge(m2_loaded, 16 * 5)
            pe.wait_ge(a_evac, 2)
            for g in range(4):
                for m in range(MT):
                    mm = pe.matmul(bank[6 + g // 2][:, (g % 2) * SEQ:(g % 2 + 1) * SEQ],
                                   a_tok[:, m, g * P:(g + 1) * P], averages[:, MT * g + m, :],
                                   start=m == 0, stop=m == MT - 1)
                if g % 2:
                    mm.then_inc(averages_done, 1)
            parts(4, 6)
            turn_z_pe(pe, 0)
            parts(6, 8)
            for g in range(4):
                if g % 2 == 0:
                    pe.wait_ge(averages_evac, g // 2 + 1)
                mm = pe.matmul(bank[6 + g // 2][:, (g % 2) * SEQ:(g % 2 + 1) * SEQ], pool_ws[:, g, :],
                               averaged[:, g, :], start=True, stop=True)
                if g % 2:
                    mm.then_inc(grouped_done, 1)
            forward_pe(pe, 0, 0)
            parts(8, 12)
            pe.wait_ge(m2_evac, 4)
            inverse_pe(pe, 0)
            turn_z_pe(pe, 1)
            forward_pe(pe, 4, 1)
            for k in range(KT):
                if k == 4:
                    inverse_pe(pe, 1)
                pe.wait_ge(m2_lo, k // 2 + 1 if k < 4 else k - 1)
                token_product(pe, M2 + 16 + k, h_hi[:, k, :], h_lo[:, k, :], k == 0, k == KT - 1)

        def mix2_act(act, order):
            def centre(j):
                act.wait_ge(panel_used, M2 + 5 + j)
                tile = (j + 8) % 12
                act.activation(conv[:, j, :], bank[4 + j % 2][:, 0:SEQ], ACT.Identity,
                               scale=col("conv_w", 12 + tile),
                               bias=col("conv_b", tile)).then_inc(conv_centre, 1)

            def evac_z(n):
                for m in range(MT):
                    act.wait_ge(z_turned, n + m + 1)
                    act.activation(z_tok[:, m, :], bank[2 + m][:, :], ACT.Copy).then_inc(z_evac, 1)

            def high(lo, hi):
                r = slice(lo, hi)
                act.activation(h_hi[:, r, :], h32[:, r, :], ACT.Copy).then_inc(m2_hi, 1)

            def bias(o):
                for c in range(4):
                    act.wait_ge(*((z_done, c + 1) if o else (conv_done, c + 1)))
                    act.activation(z_bias[:, c, :], conv[:, c, :], ACT.Copy,
                                   scale=col("bias", 4 * o + c)).then_inc(z_biased, 1)

            act_panels(act, M2 + 3, 4)
            act.wait_ge(panel_used, M2 + 4)
            for m in range(MT):
                act.activation(a_tok[:, m, :], bank[m][:, :], ACT.Copy).then_inc(a_evac, 1)
            for j in range(12):
                split_hi(act, M2 + 7 + j)
                centre(j)
                if j == 4:
                    for b in range(2):
                        act.wait_ge(averages_done, b + 1)
                        act.activation(averaged[:, 2 * b:2 * b + 2, :].rearrange("p g t -> p (g t)"),
                                       bank[6 + b][:, :], ACT.Copy).then_inc(averages_evac, 1)
                if j == 6:
                    evac_z(0)
                if j == 8:
                    bias(0)
                if j == 9:
                    for g in range(4):
                        act.wait_ge(grouped_done, g // 2 + 1)
                        act.activation(h32[:, g, :], bank[6 + g // 2][:, (g % 2) * SEQ:(g % 2 + 1) * SEQ],
                                       ACT.Copy, scale=col("pool_scale", g)).then_inc(m2_evac, 1)
            act_panels(act, M2 + 19, 3)
            for b in range(2):
                act.wait_ge(m2_evac, 2 * b + 2)
                high(2 * b, 2 * b + 2)
            evac_z(2)
            bias(1)
            act_panels(act, M2 + 22, 4)
            for k in range(4, KT):
                act.wait_ge(z_done, k + 1)
                high(k, k + 1)
            act_panels(act, M2 + 26, 1)

        def mix2_dve(dve, order):
            def taps_of(j):
                dve.wait_ge(conv_centre, j + 1)
                tile = (j + 8) % 12
                src, dst = bank[4 + j % 2], conv[:, j, :]
                order(dve.scalar_tensor_tensor(out=dst[:, 1:SEQ], in0=src[:, 0:SEQ - 1],
                                               scalar=col("conv_w", tile), in1=dst[:, 1:SEQ],
                                               op0=ALU.mult, op1=ALU.add))
                then(dve, dve.scalar_tensor_tensor(out=dst[:, 0:SEQ - 1], in0=src[:, 1:SEQ],
                                                   scalar=col("conv_w", 24 + tile),
                                                   in1=dst[:, 0:SEQ - 1], op0=ALU.mult, op1=ALU.add),
                     conv_done, j + 1)

            def multiply(o, first_bank, f):
                k = filters[:, 4 * o + 2 * f:4 * o + 2 * f + 2, :]
                for s in range(2):
                    dve.wait_ge(z_spectrum, 4 * o + 2 * f + s + 1)
                    z = bank[first_bank + 2 * f + s][:, :].unsqueeze(1).to_broadcast([P, 2, 512])
                    order(dve.tensor_tensor(terms[:, 2 * s:2 * s + 2, :], k, z, ALU.mult))
                dve.tensor_tensor(product[:, 2 * f, :], terms[:, 0, :], terms[:, 3, :],
                                  ALU.subtract).then_inc(spectra_product, 1)
                then(dve, dve.tensor_tensor(product[:, 2 * f + 1, :], terms[:, 1, :], terms[:, 2, :],
                                            ALU.add), spectra_product, 4 * o + 2 * f + 2)

            def gate(o, c):
                dve.wait_ge(z_back, 4 * o + c + 1)
                dve.wait_ge(z_biased, 4 * o + c + 1)
                order(dve.scalar_tensor_tensor(out=z_sum[:, c % 2, :], in0=bank[BACK_BANKS[c]][:, 0:SEQ],
                                               scalar=filter_scale[:, 4 * o + c:4 * o + c + 1],
                                               in1=z_bias[:, c, :], op0=ALU.mult, op1=ALU.add))
                then(dve, dve.tensor_tensor(h32[:, 4 + c, :] if o else conv[:, c, :],
                                            z_sum[:, c % 2, :], conv[:, 4 + 4 * o + c, :],
                                            ALU.mult), z_done, 4 * o + c + 1)

            def low(n, lo, hi):
                dve.wait_ge(m2_hi, n)
                r = slice(lo, hi)
                dve.tensor_tensor(h_lo[:, r, :], h32[:, r, :], h_hi[:, r, :].bitcast(F32),
                                  ALU.subtract).then_inc(m2_lo, 1)

            dve_panels(dve, M2 + 3, 4)
            for j in range(8):
                split_lo(dve, M2 + 7 + j)
                taps_of(j)
            dve.wait_ge(m2_loaded, 16 * 5)
            for f in range(2):
                multiply(0, 0, f)
                for j in (8 + 2 * f, 9 + 2 * f):
                    split_lo(dve, M2 + 7 + j)
                    taps_of(j)
            dve.wait_ge(filter_scaled, 2)
            for c in range(4):
                gate(0, c)
            dve_panels(dve, M2 + 19, 3)
            low(1, 0, 2)
            low(2, 2, 4)
            for f in range(2):
                multiply(1, 4, f)
            dve_panels(dve, M2 + 22, 4)
            gate(1, 0)
            for c in range(1, 4):
                gate(1, c)
                low(2 + c, 3 + c, 4 + c)
            low(6, 7, 8)
            dve_panels(dve, M2 + 26, 1)

        QK = 96
        SCALE = QK ** -0.5
        q_rows = region(4096, MLA_HEADS, SEQ)
        k_rows = region(8192, MLA_HEADS, SEQ)
        values = region(12288, MT, D)
        probs = region(14336, 2, 512)
        probs_by_key = region(15360, 2, 512)
        attended = region(16384, MT, D)
        rope_t = region(18432, 2, SEQ)
        latent = region(18944, 3, SEQ)
        latent_sq = region(19712, 3, SEQ)
        latent_g = region(14336, 3, SEQ)
        k_turn = region(20992, 2, SEQ)
        q_turn = region(21504, 2, 4, SEQ)
        soft = region(23552, 4, 2 * MLA_HEADS)
        MAX3, NEG3, SUM3, REC3 = range(4)

        rope_loaded = sem("rope_loaded")
        latent_squares = sem("latent_squares")
        latent_sums = sem("latent_sums")
        latent_diag = sem("latent_diag")
        latent_rows = sem("latent_rows")
        latent_done = sem("latent_done")
        latent_hi = sem("latent_hi")
        latent_lo = sem("latent_lo")
        k_rope_done = sem("k_rope_done")
        q_evac = sem("q_evac")
        q_rope_read = sem("q_rope_read")
        q_rope_done = sem("q_rope_done")
        kv_act = sem("kv_act")
        kv_dve = sem("kv_dve")
        scored = sem("scored")
        soft_max = sem("soft_max")
        soft_exp = sem("soft_exp")
        probs_turned = sem("probs_turned")
        probs_evac = sem("probs_evac")
        head_done = sem("head_done")
        divided = sem("divided")
        attended_turned = sem("attended_turned")
        m3_hi = sem("m3_hi")
        m3_lo = sem("m3_lo")
        M3 = FIRST[("mix3", 0)]

        def mix3_loads(pool):
            pool.wait_ge(x_done, 20)
            pool.dma_start(rope_t, rope).then_inc(rope_loaded, 16)

        def add_turned(eng, j):
            rows = slice(32 * j, 32 * j + 32)
            eng.tensor_tensor(q_rows[64:96, j::4, :], q_turn[rows, 0, :, :], q_turn[rows, 1, :, :],
                              ALU.add).then_inc(q_rope_done, 1)

        def mix3_pool(pool):
            pool.wait_ge(rms_mean, 3)
            pow_pool(pool, 4)
            pool.wait_ge(q_rope_read, 4)
            add_turned(pool, 3)

        def mix3_pe(pe):
            for j in range(4):
                channel_product(pe, bank[(0, 0, 1, 2)[j]][:, SEQ * (j == 1):SEQ * (j == 1) + SEQ],
                                M3 + j, norm=7 if j == 0 else None)
            pe.wait_ge(latent_squares, 2)
            for j in range(4):
                t = slice((j % 2) * P, (j % 2 + 1) * P)
                for n in ((0, 1), (2,))[j // 2]:
                    mm = pe.matmul(bank[3][:, j:j + 1], latent_sq[:, n, t], ones[:, 0:1], start=n != 1,
                                   stop=n != 0)
            mm.then_inc(latent_sums, 1)
            rows_pe(pe, bank[3], 4, (latent_diag, 1), latent_rows)
            pe.wait_ge(latent_lo, 1)
            for n in range(8):
                channel_product(pe, bank[4 + n // 2][:, SEQ * (n % 2):SEQ * (n % 2) + SEQ],
                                M3 + 4 + n // 4, k_tiles=2, at=256 * (n % 4), used=n % 4 == 3)
            pe.wait_ge(k_rope_done, 1)
            for n in range(8):
                channel_product(pe, bank[n // 2][:, SEQ * (n % 2):SEQ * (n % 2) + SEQ],
                                M3 + 6 + n // 4, k_tiles=2, at=256 * (n % 4), used=n % 4 == 3)
            for n in range(8):
                if n % 2 == 0:
                    pe.wait_ge(q_evac, n // 2 + 1)
                channel_product(pe, bank[4 + n // 2][:, SEQ * (n % 2):SEQ * (n % 2) + SEQ],
                                M3 + 8, k_tiles=1, at=P * n, k0=2, used=n == 7)
            pe.wait_ge(q_rope_read, 4)
            token_product(pe, M3 + 9, h_hi[:, 2, :], h_lo[:, 2, :], True, True, result=False)

            def score(h):
                if h >= 2:
                    pe.wait_ge(soft_exp, 2 * h - 2)
                for m in range(MT):
                    mm = pe.matmul(bank[4 + h % 2][:, SEQ * m:SEQ * m + SEQ],
                                   q_rows[0:QK, h, P * m:P * m + P], k_rows[0:QK, h, :],
                                   start=True, stop=True)
                mm.then_inc(scored, 1)

            def turn(h):
                pe.wait_ge(soft_exp, 2 * h + 2)
                if h >= 2:
                    pe.wait_ge(probs_evac, h - 1)
                for m in range(MT):
                    for c in range(MT):
                        tr = pe.transpose(bank[6 + h % 2][:, SEQ * c + P * m:SEQ * c + P * m + P],
                                          probs[:, h % 2, SEQ * m + P * c:SEQ * m + P * c + P], ident[:, :])
                tr.then_inc(probs_turned, 1)

            def weigh(h):
                if h == 0:
                    pe.wait_ge(kv_act, 6)
                    pe.wait_ge(kv_dve, 2)
                pe.wait_ge(probs_evac, h + 1)
                for m in range(MT):
                    for c in range(MT):
                        mm = pe.matmul(bank[2 * m + h // 8][:, 64 * (h % 8):64 * (h % 8) + 64],
                                       probs_by_key[:, h % 2, SEQ * c + P * m:SEQ * c + P * m + P],
                                       values[:, c, 64 * h:64 * h + 64], start=c == 0, stop=c == 1)
                mm.then_inc(head_done, 1)

            pe.wait_ge(q_rope_done, 5)
            pe.wait_ge(kv_act, 4)
            score(0)
            score(1)
            for h in range(MLA_HEADS):
                turn(h)
                if h + 2 < MLA_HEADS:
                    score(h + 2)
                if h:
                    weigh(h - 1)
            weigh(MLA_HEADS - 1)
            for b in range(4):
                pe.wait_ge(divided, 2 + b // 2 * 2)
                for j in range(2):
                    for m in range(MT):
                        tr = pe.transpose(bank[4 + b][:, j * SEQ + m * P:j * SEQ + (m + 1) * P],
                                          attended[:, m, (2 * b + j) * P:(2 * b + j + 1) * P], ident[:, :])
                tr.then_inc(attended_turned, 1)
            pe.wait_ge(divided, 4)
            for k in range(KT):
                pe.wait_ge(m3_lo, k // 2 + 1)
                token_product(pe, M3 + 10 + k, h_hi[:, k, :], h_lo[:, k, :], k == 0, k == KT - 1)

        def by_head(rows, b, odd):
            return rows[0:64, 4 * b + odd:4 * b + odd + 3:2, :]

        def of_bank(b, odd):
            return bank[4 + b][64 * odd:64 * odd + 64, :].rearrange("p (t q) -> p t q", t=2)

        def mix3_act(act, order):
            act_panels(act, M3 + 3, 3)
            act.wait_ge(panel_used, M3 + 2)
            act.activation(latent_sq[:, 0:2, :].rearrange("p t q -> p (t q)"), bank[0][:, :],
                           ACT.Square).then_inc(latent_squares, 1)
            act.wait_ge(panel_used, M3 + 3)
            act.activation(latent_sq[:, 2, :], bank[1][:, 0:SEQ], ACT.Square).then_inc(latent_squares, 1)
            for n in range(3):
                act.activation(latent_g[:, n, :], bank[n // 2][:, SEQ * (n % 2):SEQ * (n % 2) + SEQ],
                               ACT.Copy, scale=col("q_g", n) if n < 2 else col("kv_g")).then_inc(
                                   latent_squares, 1)
            act.wait_ge(latent_done, 2)
            act.activation(h_hi[:, 0:3, :], latent[:, :, :], ACT.Copy).then_inc(latent_hi, 1)
            act_panels(act, M3 + 6, 4)
            for b in range(4):
                act.wait_ge(panel_used, M3 + 5 + b // 2)
                order(act.activation(by_head(q_rows, b, 0), of_bank(b, 0), ACT.Copy))
                act.activation(by_head(q_rows, b, 1), of_bank(b, 1), ACT.Copy).then_inc(q_evac, 1)
            act_panels(act, M3 + 10, 3)
            act.wait_ge(panel_used, M3 + 9)
            for b in range(4):
                for odd in range(2):
                    ins = act.activation(by_head(k_rows, b, odd), of_bank(b, odd), ACT.Copy)
                    if odd:
                        ins.then_inc(kv_act, 1)
                    else:
                        order(ins)
            act.wait_ge(panel_used, M3 + 10)
            for half in range(2):
                act.activation(values[:, 0, 512 * half:512 * half + 512], bank[half][:, :],
                               ACT.Copy).then_inc(kv_act, 1)
            for h in range(MLA_HEADS):
                act.wait_ge(soft_max, h + 1)
                if h >= 2:
                    act.wait_ge(probs_turned, h - 1)
                for m in range(MT):
                    i = 2 * h + m
                    act.activation(probs[:, h % 2, SEQ * m:SEQ * m + SEQ],
                                   bank[4 + h % 2][:, SEQ * m:SEQ * m + SEQ], ACT.Exp, scale=SCALE,
                                   bias=soft[:, NEG3, i:i + 1],
                                   accum_out=soft[:, SUM3, i:i + 1]).then_inc(soft_exp, 1)
                if h in (5, 8, 11):
                    split_hi(act, M3 + 12 + h // 3)
            for b in range(4):
                act.wait_ge(attended_turned, b + 1)
                act.activation(h_hi[:, 2 * b:2 * b + 2, :].rearrange("p k t -> p (k t)"),
                               bank[4 + b][:, :], ACT.Copy).then_inc(m3_hi, 1)
            act_panels(act, M3 + 16, 5)

        def mix3_dve(dve, order):
            cos, sin = rope_t[:, 0, :], rope_t[:, 1, :]
            dve_panels(dve, M3 + 3, 3)
            dve.wait_ge(latent_sums, 1)
            for j, width in ((0, 256), (2, 128)):
                dve.tensor_scalar(rms_col[:, j:j + 2], bank[3][:, j:j + 2], 1.0 / width, EPS, ALU.mult,
                                  ALU.add).then_inc(rms_mean, 1)
            diagonals_dve(dve, 4, (rms_pow, 2), latent_diag)
            dve.wait_ge(latent_squares, 5)
            dve.wait_ge(latent_rows, 1)
            for tiles, rows in ((slice(0, 2), bank[3][:, 0:SEQ]), (slice(2, 3), bank[3][:, SEQ:2 * SEQ])):
                n = tiles.stop - tiles.start
                dve.tensor_tensor(latent[:, tiles, :], latent_g[:, tiles, :],
                                  rows.unsqueeze(1).to_broadcast([P, n, SEQ]), ALU.mult).then_inc(latent_done, 1)
            dve.wait_ge(latent_hi, 1)
            dve.tensor_tensor(h_lo[:, 0:3, :], latent[:, :, :], h_hi[:, 0:3, :].bitcast(F32),
                              ALU.subtract).then_inc(latent_lo, 1)
            dve_panels(dve, M3 + 6, 1)
            dve.wait_ge(rope_loaded, 16)
            r, s = slice(64, 96), slice(96, 128)
            order(dve.tensor_tensor(k_turn[r, 0, :], bank[2][r, 0:SEQ], cos[r, :], ALU.mult))
            order(dve.tensor_tensor(k_turn[r, 1, :], bank[2][s, 0:SEQ], sin[s, :], ALU.mult))
            dve.tensor_tensor(k_turn[r, 0, :], k_turn[r, 0, :], k_turn[r, 1, :],
                              ALU.add).then_inc(k_rope_done, 1)
            dve_panels(dve, M3 + 7, 3)
            dve.wait_ge(k_rope_done, 1)
            dve.tensor_copy(k_rows[64:96, :, :], k_turn[64:96, 0, :].unsqueeze(1).to_broadcast(
                [32, MLA_HEADS, SEQ])).then_inc(q_rope_done, 1)
            dve_panels(dve, M3 + 10, 2)
            dve.wait_ge(panel_used, M3 + 8)
            for part, table in enumerate((cos, sin)):
                for b in range(2):
                    dve.tensor_tensor(q_turn[:, part, 2 * b:2 * b + 2, :],
                                      bank[2 * part + b][:, :].rearrange("p (t q) -> p t q", t=2),
                                      table.unsqueeze(1).to_broadcast([P, 2, SEQ]),
                                      ALU.mult).then_inc(q_rope_read, 1)
            dve.wait_ge(q_rope_read, 4)
            for j in range(3):
                add_turned(dve, j)
            dve.wait_ge(panel_used, M3 + 10)

            def turned_probs(h):
                dve.wait_ge(probs_turned, h + 1)
                if h >= 2:
                    dve.wait_ge(head_done, h - 1)
                dve.tensor_copy(probs_by_key[:, h % 2, :], bank[6 + h % 2][:, :]).then_inc(probs_evac, 1)

            for h in range(MLA_HEADS):
                dve.wait_ge(scored, h + 1)
                order(dve.tensor_reduce(soft[:, MAX3, 2 * h:2 * h + 2],
                                        bank[4 + h % 2][:, :].rearrange("p (m k) -> p m k", m=2),
                                        AX.X, ALU.max))
                dve.tensor_scalar(soft[:, NEG3, 2 * h:2 * h + 2], soft[:, MAX3, 2 * h:2 * h + 2],
                                  -SCALE, None, ALU.mult).then_inc(soft_max, 1)
                if h < 2:
                    dve.tensor_copy(values[:, 1, 512 * h:512 * h + 512], bank[2 + h][:, :]).then_inc(kv_dve, 1)
                if h:
                    turned_probs(h - 1)
                if h in (2, 5, 8, 11):
                    split_lo(dve, M3 + 12 + h // 3)
            turned_probs(MLA_HEADS - 1)
            dve.wait_ge(soft_exp, 2 * MLA_HEADS)
            order(dve.reciprocal(soft[:, REC3, :], soft[:, SUM3, :]))
            dve.wait_ge(head_done, MLA_HEADS)
            rec = soft[:, REC3, :].rearrange("p (h m) -> p h m", m=MT)
            for half in range(2):
                for m in range(MT):
                    dve.tensor_tensor(
                        attended[:, m, 512 * half:512 * half + 512].rearrange("p (h d) -> p h d", d=64),
                        bank[2 * m + half][:, :].rearrange("p (h d) -> p h d", d=64),
                        rec[:, 8 * half:8 * half + 8, m].unsqueeze(2).to_broadcast([P, 8, 64]),
                        ALU.mult).then_inc(divided, 1)
            for b in range(4):
                dve.wait_ge(m3_hi, b + 1)
                r = slice(2 * b, 2 * b + 2)
                dve.tensor_tensor(h_lo[:, r, :].rearrange("p k t -> p (k t)"), bank[4 + b][:, :],
                                  h_hi[:, r, :].bitcast(F32).rearrange("p k t -> p (k t)"),
                                  ALU.subtract).then_inc(m3_lo, 1)
            dve_panels(dve, M3 + 16, 5)

        stages = STAGES[:last_stage]

        block = ctx.enter_context(nc.Block())
        out_stored = sem("out_stored")
        final_done = sem("final_done")
        final_loaded = sem("final_loaded")
        final_row = region(13824, D)
        final = region(0, MT, D)

        @block.sync
        def _(sp):
            def load_panel(g0, i=0):
                slot = g0 % RING
                if g0 >= RING:
                    sp.wait_ge(lo_ready, g0 - (RING - 1) + RING * i)
                sp.dma_start(raw[:, slot, :], panels[g0 + RING * i]).then_inc(raw_loaded[slot], 16)

            def load_ada(a, i=0):
                slot = a % ADA_RING
                if a >= ADA_RING:
                    sp.wait_ge(ada_used, a - (ADA_RING - 1) + ADA_RING * i)
                sp.dma_start(ada_ring[:, slot, :], ada[a + ADA_RING * i]).then_inc(ada_loaded[slot], 16)

            sp.dma_start(C[:, :], cols).then_inc(small_loaded, 16)
            sp.dma_start(X[:, :, :], x_in.rearrange("(m p) d -> p m d", p=P)).then_inc(x_loaded, 16)
            for a in range(ADA_FIRST):
                load_ada(a)
            for g in range(8):
                load_panel(g)
            with sp.Fori(0, KT) as i:
                for half, chunks in enumerate(((0, 1), (2, 3, 4))):
                    for j in range(3):
                        load_panel(8 + 3 * half + j, i)
                    for c in chunks:
                        load_ada(ADA_FIRST + c, i)
            done, total = 8 + KT * RING, min(last_panel(*stages[-1]) + 3, TOTAL)
            turns = (total - done) // RING
            if turns:
                with sp.Fori(0, turns) as i:
                    for j in range(RING):
                        load_panel(done + j, i)
            for g in range(done + RING * turns, total):
                load_panel(g)

        @block.gpsimd
        def _(pool):
            order = Order(pool, pool_order)
            pool.memset(ones[:, :], 1.0).then_inc(const_ready, 1)
            pool.memset(stat[:, MINUS_HALF:MINUS_HALF + 4], -0.5).then_inc(const_ready, 1)
            pool.wait_ge(const_ready, 2)
            norm_pool(pool, 0, order)
            spectrum_pool(pool, order)
            ada_middle_pool(pool, order)
            params_pool(pool, order)
            gate_rows_pool(pool, order)
            for at, (kind, n) in enumerate(stages):
                if kind == "mix1":
                    mix1_pool(pool, order)
                if kind == "mix3":
                    mix3_pool(pool)
                if at < 3:
                    add_pool(pool, at, order)
                norm_pool(pool, at + 1, order)
                if at == 1:
                    gate_2_pool(pool, order)
                if at == 2:
                    mix2_loads(pool)
                if at == 4:
                    mix3_loads(pool)
                if at + 1 == len(stages):
                    pool.dma_start(final_row, rows[6:7, :].partition_broadcast(P)).then_inc(final_loaded, 16)
            for m in range(MT):
                pool.wait_ge(final_done, m + 1)
                pool.dma_start(out[m * P:(m + 1) * P, :], final[:, m, :]).then_inc(out_stored, 16)
            pool.wait_ge(out_stored, 32)

        @block.scalar
        def _(act):
            order = Order(act, act_order)
            act.dma_start(ident[:, :], tables[0]).then_inc(small_loaded, 16)
            act.dma_start(feat_t, feats).then_inc(spec_loaded, 16)
            act.dma_start(mlp_ws, mlp_w[:, 0:192]).then_inc(spec_loaded, 16)
            act.wait_ge(small_loaded, 32)
            act.activation(c_act, col("c", 0, 8), ACT.Silu).then_inc(c_ready, 1)
            act.wait_ge(spec_loaded, 32)
            act.dma_start(filter_out[0:64, :], mlp_w[:, 192:2240]).then_inc(spec_loaded, 16)
            act.dma_start(dft[:, 0, :, :], pool_mats[4]).then_inc(spec_loaded, 16)
            act.dma_start(dft[:, 1, :, :], pool_mats[5]).then_inc(spec_loaded, 16)
            act.dma_start(decay_rows, decay[0:1, :].partition_broadcast(P)).then_inc(decay_loaded, 16)
            norm_act_squares(act, 0)
            spectrum_act(act, order)
            norm_act_rest(act, 0)
            for at, (kind, n) in enumerate(stages):
                if kind == "ffn":
                    ffn_act(act, n)
                elif kind == "mix1":
                    mix1_act(act, order)
                elif kind == "mix2":
                    mix2_act(act, order)
                else:
                    mix3_act(act, order)
                if at < 3:
                    add_act(act, kind, n, at)
                norm_act_squares(act, at + 1)
                if at + 1 < len(stages):
                    norm_act_rest(act, at + 1)

        @block.vector
        def _(dve):
            order = Order(dve, dve_order)
            ada_next = iter(range(ADA_FIRST))

            def spare():
                a = next(ada_next, None)
                if a is not None:
                    ada_add(dve, a, acc0[:, a // KT, :])

            dve.wait_ge(small_loaded, 32)
            spectrum_dve(dve, order, spare)
            for _ in range(ADA_FIRST):
                spare()
            dve_panels(dve, 0, 3)
            filter_sums_dve(dve)
            ada_first_dve(dve, order)
            norm_dve(dve, 0, order)
            for at, (kind, n) in enumerate(stages):
                if kind == "ffn":
                    ffn_dve(dve, n, order)
                elif kind == "mix1":
                    mix1_dve(dve, order)
                elif kind == "mix2":
                    mix2_dve(dve, order)
                else:
                    mix3_dve(dve, order)
                add_dve(dve, kind, n, at)
                if at + 1 < len(stages):
                    norm_dve(dve, at + 1, order)
            dve.wait_ge(final_loaded, 16)
            last = len(stages)
            for m in range(MT):
                dve.wait_ge(rstd_done, 2 * last + m + 1)
                dve.scalar_tensor_tensor(out=final[:, m, :], in0=X[:, m, :],
                                         scalar=stat[:, RS + m:RS + m + 1], in1=final_row[:, :],
                                         op0=ALU.mult, op1=ALU.mult).then_inc(final_done, 1)

        @block.tensor
        def _(pe):
            pe.wait_ge(const_ready, 2)
            pe.wait_ge(small_loaded, 32)
            spectrum_pe(pe)
            ada_first_pe(pe)
            norm_pe(pe, 0)
            for at, (kind, n) in enumerate(stages):
                if kind == "ffn":
                    ffn_pe(pe, n)
                elif kind == "mix1":
                    mix1_pe(pe)
                elif kind == "mix2":
                    mix2_pe(pe)
                else:
                    mix3_pe(pe)
                if at + 1 < len(stages):
                    norm_pe(pe, at + 1)



def stream_of_panels(a):
    def columns(w):
        k, n = w.shape[0] // P, w.shape[1] // P
        return w.reshape(k, P, n, P).transpose(2, 1, 0, 3).reshape(n, P, k * P)

    def together(p, n):
        return p.reshape(-1, n, P, p.shape[2]).transpose(0, 2, 1, 3).reshape(-1, P, n * p.shape[2])

    def ffn(gate, up, down):
        g, u, d = columns(gate), columns(up), down.reshape(FT, P, D)
        order = [g[0], u[0]]
        for f in range(1, FT):
            order += [g[f], u[f], d[f - 1]]
        return np.stack(order + [d[FT - 1]])

    def mix1():
        w = a["w_in"][0]
        q = w[:, :512].reshape(D, 2, 4, HD).transpose(0, 2, 1, 3).reshape(D, 512)
        return [columns(w[:, 768:]), columns(q), columns(w[:, 512:768]),
                together(columns(a["ssm_w_glu"][0]), 2), a["w_out"][0].reshape(8, P, D)]

    def mix2():
        w = a["mix_w_in_2"][0]
        return [together(w[:, :512].reshape(8, P, 512), 2),
                columns(w[:, 1536:]), columns(w[:, 512:1536]), a["mix_w_out_2"][0].reshape(8, P, D)]

    def mix3():
        uq = a["mla_w_uq_2"][0].reshape(256, MLA_HEADS, 96)
        dkv, ukv = a["mla_w_dkv_2"][0], a["mla_w_ukv_2"][0].reshape(P, MLA_HEADS, P)
        swap = np.r_[16:32, 0:16]
        rope = uq[:, :, 64:]
        return [columns(a["mla_w_dq_2"][0]), columns(dkv[:, :P]),
                columns(np.concatenate([dkv[:, P:], dkv[:, P:][:, swap]] * 2, 1)),
                together(columns(uq[:, :, :64].reshape(256, 1024)), 4),
                together(columns(rope.reshape(256, 512)), 4),
                together(columns(rope[:, :, swap].reshape(256, 512)), 4),
                ukv[:, :, :64].reshape(1, P, D), ukv[:, :, 64:].reshape(1, P, D),
                a["mla_w_o_2"][0].reshape(8, P, D)]

    g, u, d = a["ffn_w_gate_2"], a["ffn_w_up_2"], a["ffn_w_down_2"]
    feed = [ffn(a["w1_gate"][0], a["w1_up"][0], a["w1_down"][0]),
            ffn(a["w2_gate"][0], a["w2_up"][0], a["w2_down"][0])]
    feed += [ffn(g[i, j], u[i, j], d[i, j]) for i in range(2) for j in range(2)]
    parts = []
    for kind, n in STAGES:
        parts += [feed[n]] if kind == "ffn" else {"mix1": mix1, "mix2": mix2, "mix3": mix3}[kind]()
    return np.concatenate(parts)


def small_columns(a):
    def cut(v):
        return v.reshape(-1, P).T

    def states(v):
        return v.reshape(STATE_TILES, P).T

    def short(v):
        return np.concatenate([v, np.zeros((P - 64,) + v.shape[1:], np.float32)])

    t = np.linspace(0.0, 1.0, SEQ, dtype=np.float32)
    parts = [("c", cut(a["c"])), ("b_ada", cut(a["b_ada"])),
             ("g_pre", np.concatenate([cut(a[n]) for n in ("g_pre_ff1", "g_pre_mix", "g_pre_ff2")], 1)),
             ("norm_g", cut(a["norm_g_2"])), ("pool_scale", cut(a["pool_scale_2"])),
             ("conv_b", cut(a["hyena_conv_b_2"])), ("conv_w", cut(a["hyena_conv_w_2"])),
             ("bias", cut(a["hyena_bias_2"])), ("g_attn", cut(a["g_attn_out"])),
             ("g_ssm", cut(a["g_ssm_out"])), ("ssm_d", cut(a["ssm_d"])), ("b_glu", cut(a["ssm_b_glu"])),
             ("q_g", cut(a["mla_q_norm_g_2"])), ("kv_g", cut(a["mla_kv_norm_g_2"])),
             ("a_re", states(a["ssm_a_re"])), ("a_im", states(a["ssm_a_im"])),
             ("log_step", states(np.repeat(a["ssm_log_step"][0], 64))),
             ("sin_freq", short(a["hyena_sin_freq_2"][0].T)),
             ("mlp_b", short(np.stack([a[f"hyena_ffn_b{i}_2"][0] for i in (1, 2, 3)], 1))),
             ("neg_t", cut(-t))]
    for (name, v), (key, (_, n)) in zip(parts, COLS.items()):
        assert name == key and v.shape == (P, n), (name, v.shape, n)
    return np.concatenate([v for _, v in parts], 1)


def shape_constants():
    t = np.arange(SEQ)
    angle = np.outer(t, 2 * t + 1) * (math.pi / 512)
    cos, sin = np.cos(angle), np.sin(angle)
    tiles = lambda m: m.reshape(MT, P, SEQ).transpose(1, 0, 2)
    mats = []
    for w in (2, 4, 8, 16):
        lo = np.clip(t - w // 2, 0, SEQ)
        hi = np.clip(t - w // 2 + w, 0, SEQ)
        s = t[:, None]
        mats.append(((s >= lo) & (s < hi)) / (hi - lo) - (s == t))
    mats += [cos, sin, cos.T / 256, sin.T / 256]
    pool_mats = np.stack([tiles(m) for m in mats]).astype(np.float32)
    inv = (10000.0 ** (-np.arange(0, 32, 2, dtype=np.float32) / 32)).astype(np.float32)
    ang = np.arange(SEQ, dtype=np.float32)[:, None] * inv[None, :]
    c, s = np.cos(ang.astype(np.float64)).T, np.sin(ang.astype(np.float64)).T
    rope = np.stack([np.tile(np.concatenate([c, c]), (4, 1)),
                     np.tile(np.concatenate([-s, s]), (4, 1))], 1).astype(np.float32)
    i, j = np.arange(P)[:, None], np.arange(2 * P)[None, :]
    dist = i + P - j
    near = np.where((dist >= 0) & (dist < P), -dist, -1e38).astype(np.float32)
    near = np.concatenate([near[:, P:], near], 1)
    bands = 16
    w = (2.0 * math.pi * np.arange(SEQ, dtype=np.float32) / SEQ).astype(np.float32)
    f = np.linspace(1e-4, bands - 1, bands, dtype=np.float32)
    phase = (w[:, None] * f[None, :]).astype(np.float64)
    z = np.concatenate([np.linspace(0.0, 1.0, SEQ)[:, None], np.cos(phase), -np.sin(phase)], 1)
    return {"tables": np.eye(P, dtype=np.float32)[None], "pool_mats": pool_mats, "rope": rope,
            "near": near, "feats": np.ascontiguousarray(z.T.astype(np.float32))}


def lay_out(a):
    a = {k: np.asarray(v) for k, v in a.items()}
    ada = a["w_ada"][0].reshape(KT, P, 9, D).transpose(2, 0, 1, 3)
    ada = np.concatenate([ada[0], ada[1], ada[list(ADA_MIDDLE)].transpose(1, 0, 2, 3).reshape(-1, P, D),
                          ada[5], ada[8]])
    b_ada = a["b_ada"].reshape(9, D)
    rows = np.stack([b_ada[2], b_ada[5], b_ada[8], a["g_post_ff1"][0], a["g_post_mix"][0],
                     a["g_post_ff2"][0], a["final_norm_g_2"]])
    b = [a[n][0].reshape(STATE_TILES, P, 16).transpose(1, 0, 2).reshape(P, 256)
         for n in ("ssm_b_re", "ssm_b_im")]
    c = [a[n][0].reshape(STATE_TILES, 2, 16, 64).transpose(1, 3, 0, 2).reshape(P, 256)
         for n in ("ssm_c_re", "ssm_c_im")]
    mlp_w = np.zeros((64, 2240), np.float32)
    mlp_w[:33, 0:64] = a["hyena_ffn_w1_2"][0]
    mlp_w[:, 64:128] = a["hyena_ffn_w2_2"][0]
    mlp_w[:, 128:192] = a["hyena_ffn_w3_2"][0]
    mlp_w[:, 192:] = a["hyena_ffn_w_out_2"][0]
    got = {"panels": stream_of_panels(a), "ada": ada, "cols": small_columns(a), "rows": rows,
           "sinks": a["attn_sinks"], "ssm_mats": np.stack(b + c, 1),
           "pool_w": a["pool_w_2"][0].transpose(1, 0, 2), "decay": a["hyena_decay_2"][0].reshape(2, 1024),
           "mlp_w": mlp_w, "x_in": a["x"][0]}
    got.update(shape_constants())
    return {k: np.ascontiguousarray(v) for k, v in got.items()}


def kernel(last_stage=len(STAGES), **inputs):
    from concourse import bacc
    from concourse.bass_utils import run_bass_kernel_spmd

    nc = bacc.Bacc("TRN2", target_bir_lowering=False, num_devices=1)
    arrays = lay_out(inputs)
    args = {name: nc.dram_tensor(name, v.shape, F32, kind="ExternalInput").ap()
            for name, v in arrays.items()}
    out = nc.dram_tensor("out", (SEQ, D), F32, kind="ExternalOutput").ap()
    spectrum = nc.dram_tensor("spectrum", (2, P, 4, 512), F32, kind="Internal").ap()
    build_program(nc, out=out, spectrum=spectrum, last_stage=last_stage, **args)
    result = run_bass_kernel_spmd(nc, [arrays], core_ids=[0])
    return result.results[0]["out"].reshape(1, SEQ, D)
```
